# Optimizing a Trainium2 kernel written in Bass

```python
import jax, jax.numpy as jnp
from jax import lax
import numpy as np
import math

D_MODEL = 1024
BATCH = 1
SEQ = 256
DEPTH = 2

GRID_W = 64
CTX_LEN = 256
N_MIXERS = 2
N_A_LAYERS = (DEPTH + N_MIXERS - 1) // N_MIXERS
N_B_LAYERS = DEPTH // N_MIXERS
DN_ALPHA = (2.0 * DEPTH) ** 0.25
DN_BETA = (8.0 * DEPTH) ** -0.25
LN_EPS = 1e-5
CHUNK = 128
ROWS_PER_CHUNK = CHUNK // GRID_W
A_WIDTH = D_MODEL
A_HEADS = 8
A_GROUP = A_WIDTH // A_HEADS
GLA_HEADS = 4
GLA_DK = D_MODEL // 2 // GLA_HEADS
GLA_DV = D_MODEL // GLA_HEADS
GLA_QK = GLA_HEADS * GLA_DK
GLA_V = GLA_HEADS * GLA_DV
GLA_GATE_RANK = 16
GLA_TAU = 16.0
GLA_CHUNK = 64
GLA_IN = 2 * GLA_QK + 2 * GLA_V + 2 * GLA_GATE_RANK
PEER_HEADS = 8
PEER_NKEYS = 128
PEER_EXPERTS = PEER_NKEYS * PEER_NKEYS
PEER_QDIM = 128
PEER_HALF = PEER_QDIM // 2
PEER_TOPK = 16
PEER_BLOCK = 128


def layer_norm(x, g, b):
    xf = x.astype(jnp.float32)
    mu = jnp.mean(xf, axis=-1, keepdims=True)
    var = jnp.mean(jnp.square(xf - mu), axis=-1, keepdims=True)
    y = (xf - mu) * lax.rsqrt(var + LN_EPS)
    return (y * g + b).astype(x.dtype)

def chunk_mlp(h, n_chunks, w_in, norm_g, norm_b, w_s, b_s, w_out):
    bsz, t, _ = h.shape
    z = jax.nn.gelu(h @ w_in)
    u, v = jnp.split(z, 2, axis=-1)
    v = layer_norm(v, norm_g, norm_b)
    vb = v.reshape(bsz, n_chunks, CHUNK, A_HEADS, A_GROUP)
    s = jnp.einsum('hpq,bnqhc->bnphc', w_s, vb) + b_s.T[None, None, :, :, None]
    return (u * s.reshape(bsz, t, A_WIDTH)) @ w_out

def gla_chunked(q, k, v, g, s0):
    bsz, t, h, dk = q.shape
    dv = v.shape[-1]
    n = t // GLA_CHUNK
    f32 = jnp.float32
    q = q.astype(f32).reshape(bsz, n, GLA_CHUNK, h, dk)
    k = k.astype(f32).reshape(bsz, n, GLA_CHUNK, h, dk)
    v = v.astype(f32).reshape(bsz, n, GLA_CHUNK, h, dv)
    b = jnp.cumsum(g.astype(f32).reshape(bsz, n, GLA_CHUNK, h, dk), axis=2)
    b_end = b[:, :, -1:]
    q_in = q * jnp.exp(b)
    k_in = k * jnp.exp(-b)
    k_end = k * jnp.exp(b_end - b)
    att = jnp.einsum('bnihd,bnjhd->bnhij', q_in, k_in)
    mask = jnp.tril(jnp.ones((GLA_CHUNK, GLA_CHUNK), dtype=bool))
    att = jnp.where(mask, att, 0.0)
    o_intra = jnp.einsum('bnhij,bnjhe->bnihe', att, v)

    def step(state, inp):
        qc, kc, vc, dc = inp
        o = jnp.einsum('bihd,bhde->bihe', qc, state)
        state = dc[..., None] * state + jnp.einsum('bjhd,bjhe->bhde', kc, vc)
        return state, o

    xs = (jnp.moveaxis(q_in, 1, 0), jnp.moveaxis(k_end, 1, 0), jnp.moveaxis(v, 1, 0),
          jnp.moveaxis(jnp.exp(b_end[:, :, 0]), 1, 0))
    s_fin, o_inter = lax.scan(step, s0.astype(f32), xs)
    o = o_intra + jnp.moveaxis(o_inter, 0, 1)
    return o.reshape(bsz, t, h, dv), s_fin

def gla_reverse(q, k, v, g, s0):
    o, s_fin = gla_chunked(jnp.flip(q, 1), jnp.flip(k, 1), jnp.flip(v, 1), jnp.flip(g, 1), s0)
    return jnp.flip(o, 1), s_fin

def gla_project(h, w_in, w_gate, gate_bias):
    bsz, t, _ = h.shape
    z = h @ w_in
    q, k, v, r, gl = jnp.split(z, [GLA_QK, 2 * GLA_QK, 2 * GLA_QK + GLA_V, 2 * GLA_QK + 2 * GLA_V], axis=-1)
    q = q.reshape(bsz, t, GLA_HEADS, GLA_DK) * (GLA_DK ** -0.5)
    k = k.reshape(bsz, t, GLA_HEADS, GLA_DK)
    v = v.reshape(bsz, t, GLA_HEADS, GLA_DV)
    gl = gl.reshape(bsz, t, 2, GLA_GATE_RANK)
    zg = (jnp.einsum('btjr,jrd->btjd', gl, w_gate) + gate_bias).astype(jnp.float32)
    glog = (jax.nn.log_sigmoid(zg) / GLA_TAU).reshape(bsz, t, 2, GLA_HEADS, GLA_DK)
    return q, k, v, r, glog

def gla_readout(o, r, gn_g, w_out):
    bsz, t = o.shape[:2]
    mu = jnp.mean(o, axis=-1, keepdims=True)
    var = jnp.mean(jnp.square(o - mu), axis=-1, keepdims=True)
    y = ((o - mu) * lax.rsqrt(var + LN_EPS)).reshape(bsz, t, GLA_V) * gn_g
    return (y.astype(r.dtype) * jax.nn.silu(r)) @ w_out

def gla_mixer(h_lat, h_ctx, w_in, w_gate, gate_bias, gn_g, w_out, need_ctx_out):
    qc, kc, vc, rc, gc = gla_project(h_ctx, w_in, w_gate, gate_bias)
    ql, kl, vl, rl, gll = gla_project(h_lat, w_in, w_gate, gate_bias)
    s0 = jnp.zeros((h_ctx.shape[0], GLA_HEADS, GLA_DK, GLA_DV), jnp.float32)
    o_cf, s_f = gla_chunked(qc, kc, vc, gc[:, :, 0], s0)
    o_cb, s_b = gla_reverse(qc, kc, vc, gc[:, :, 1], s0)
    o_lf, _ = gla_chunked(ql, kl, vl, gll[:, :, 0], s_f)
    o_lb, _ = gla_reverse(ql, kl, vl, gll[:, :, 1], s_b)
    out_lat = gla_readout(o_lf + o_lb, rl, gn_g, w_out)
    out_ctx = gla_readout(o_cf + o_cb, rc, gn_g, w_out) if need_ctx_out else None
    return out_lat, out_ctx

def peer_ffn(h, w_q, sub_keys, u_tab, v_tab):
    bsz, t, d = h.shape
    blocks = h.reshape(-1, PEER_BLOCK, d)

    def one_block(xb):
        q = (xb @ w_q).reshape(PEER_BLOCK, PEER_HEADS, 2, PEER_HALF)
        s = jnp.einsum('thpd,pkd->thpk', q, sub_keys).astype(jnp.float32)
        s1, i1 = lax.top_k(s[:, :, 0], PEER_TOPK)
        s2, i2 = lax.top_k(s[:, :, 1], PEER_TOPK)
        cand_s = (s1[..., :, None] + s2[..., None, :]).reshape(PEER_BLOCK, PEER_HEADS, PEER_TOPK * PEER_TOPK)
        cand_i = (i1[..., :, None] * PEER_NKEYS + i2[..., None, :]).reshape(PEER_BLOCK, PEER_HEADS, PEER_TOPK * PEER_TOPK)
        top_s, pos = lax.top_k(cand_s, PEER_TOPK)
        idx = jnp.take_along_axis(cand_i, pos, axis=-1)
        wts = jax.nn.softmax(top_s, axis=-1).astype(xb.dtype)
        act = jax.nn.gelu(jnp.einsum('thkd,td->thk', u_tab[idx], xb)) * wts
        return jnp.einsum('thk,thkd->td', act, v_tab[idx])

    return lax.map(one_block, blocks).reshape(bsz, t, d)

def first_inputs(seed: int = 0) -> dict:
    key = jax.random.key(seed)
    ks = jax.random.split(key, 24)
    f32 = jnp.float32

    def nrm(k, shape, s):
        return jax.random.normal(k, shape, f32) * s

    d = D_MODEL
    return {
        "x": nrm(ks[0], (BATCH, SEQ, d), 1.0),
        "c": nrm(ks[1], (BATCH, d), 1.0),
        "ctx": nrm(ks[2], (BATCH, CTX_LEN, d), 1.0),
        "c_ctx": nrm(ks[3], (d,), 1.0),
        "w_mod": nrm(ks[4], (DEPTH, d, 6 * d), 0.5 * d ** -0.5),
        "b_mod": nrm(ks[5], (DEPTH, 6 * d), 0.01),
        "ln_g": 1.0 + nrm(ks[6], (DEPTH, 2, d), 0.01),
        "ln_b": nrm(ks[7], (DEPTH, 2, d), 0.01),
        "a_w_in": nrm(ks[8], (N_A_LAYERS, d, 2 * A_WIDTH), d ** -0.5),
        "a_norm_g": 1.0 + nrm(ks[9], (N_A_LAYERS, A_WIDTH), 0.01),
        "a_norm_b": nrm(ks[10], (N_A_LAYERS, A_WIDTH), 0.01),
        "a_w_s": nrm(ks[11], (N_A_LAYERS, A_HEADS, CHUNK, CHUNK), CHUNK ** -0.5),
        "a_b_s": 1.0 + nrm(ks[12], (N_A_LAYERS, A_HEADS, CHUNK), 0.01),
        "a_w_out": nrm(ks[13], (N_A_LAYERS, A_WIDTH, d), DN_BETA * A_WIDTH ** -0.5),
        "b_w_in": nrm(ks[14], (N_B_LAYERS, d, GLA_IN), d ** -0.5),
        "b_w_gate": nrm(ks[15], (N_B_LAYERS, 2, GLA_GATE_RANK, GLA_QK), GLA_GATE_RANK ** -0.5),
        "b_gate_bias": nrm(ks[16], (N_B_LAYERS, 2, GLA_QK), 0.01),
        "b_gn_g": 1.0 + nrm(ks[17], (N_B_LAYERS, GLA_V), 0.01),
        "b_w_out": nrm(ks[18], (N_B_LAYERS, GLA_V, d), DN_BETA * GLA_V ** -0.5),
        "p_w_q": nrm(ks[19], (DEPTH, d, PEER_HEADS * PEER_QDIM), d ** -0.5),
        "p_keys": nrm(ks[20], (DEPTH, 2, PEER_NKEYS, PEER_HALF), PEER_HALF ** -0.5),
        "p_u": nrm(ks[21], (DEPTH, PEER_EXPERTS, d), d ** -0.5),
        "p_v": nrm(ks[22], (DEPTH, PEER_EXPERTS, d), DN_BETA),
    }

def first_block(x, c, ctx, c_ctx, w_mod, b_mod, ln_g, ln_b,
              a_w_in, a_norm_g, a_norm_b, a_w_s, a_b_s, a_w_out,
              b_w_in, b_w_gate, b_gate_bias, b_gn_g, b_w_out,
              p_w_q, p_keys, p_u, p_v):
    bsz, seq, d = x.shape
    rows = seq // GRID_W
    lat_chunks = rows // ROWS_PER_CHUNK
    ctx_chunks = ctx.shape[1] // CHUNK
    sc = jax.nn.silu(c)
    sc_ctx = jax.nn.silu(c_ctx)
    for i in range(DEPTH):
        last = i == DEPTH - 1
        m = (sc @ w_mod[i] + b_mod[i]).reshape(bsz, 6, d)
        mc = (sc_ctx @ w_mod[i] + b_mod[i]).reshape(6, d)
        sh1, s1, g1, sh2, s2, g2 = [m[:, j, None, :] for j in range(6)]
        sh1c, s1c, g1c, sh2c, s2c, g2c = [mc[j] for j in range(6)]
        h_lat = x * (1.0 + s1) + sh1
        if i % N_MIXERS == 0:
            j = i // N_MIXERS
            prm = (a_w_in[j], a_norm_g[j], a_norm_b[j], a_w_s[j], a_b_s[j], a_w_out[j])
            mix_lat = chunk_mlp(h_lat, lat_chunks, *prm)
            mix_ctx = None if last else chunk_mlp(ctx * (1.0 + s1c) + sh1c, ctx_chunks, *prm)
        else:
            j = i // N_MIXERS
            h_ctx = ctx * (1.0 + s1c) + sh1c
            mix_lat, mix_ctx = gla_mixer(h_lat, h_ctx, b_w_in[j], b_w_gate[j], b_gate_bias[j],
                                         b_gn_g[j], b_w_out[j], not last)
        x = layer_norm(DN_ALPHA * x + g1 * mix_lat, ln_g[i, 0], ln_b[i, 0])
        ffn_lat = peer_ffn(x * (1.0 + s2) + sh2, p_w_q[i], p_keys[i], p_u[i], p_v[i])
        x = layer_norm(DN_ALPHA * x + g2 * ffn_lat, ln_g[i, 1], ln_b[i, 1])
        if not last:
            ctx = layer_norm(DN_ALPHA * ctx + g1c * mix_ctx, ln_g[i, 0], ln_b[i, 0])
            ffn_ctx = peer_ffn(ctx * (1.0 + s2c) + sh2c, p_w_q[i], p_keys[i], p_u[i], p_v[i])
            ctx = layer_norm(DN_ALPHA * ctx + g2c * ffn_ctx, ln_g[i, 1], ln_b[i, 1])
    return x


HEAD_DIM = 64
MIX_WIDTH = D_MODEL
SB_WIDTH = MIX_WIDTH // 2
SB_HEADS = SB_WIDTH // HEAD_DIM
SSM_WIDTH = MIX_WIDTH - SB_WIDTH
SSM_GROUP = 16
SSM_GROUPS = SSM_WIDTH // SSM_GROUP
SSM_STATE = 64
DSA_HEADS = MIX_WIDTH // HEAD_DIM
DSA_KV_HEADS = 4
DSA_REP = DSA_HEADS // DSA_KV_HEADS
DSA_WIDTH = DSA_HEADS * HEAD_DIM
IDX_HEADS = 8
IDX_DIM = 32
TOPK_MAX = 256
D_FF = 4 * D_MODEL
Q_BLOCK = 128
N_EVEN = (DEPTH + 1) // 2
N_ODD = DEPTH // 2
ALPHA = (2 * DEPTH) ** 0.25
BETA = (8 * DEPTH) ** -0.25
SB_IN = 3 * SB_WIDTH + SSM_WIDTH
DSA_SIZES = (DSA_WIDTH, DSA_KV_HEADS * HEAD_DIM, DSA_KV_HEADS * HEAD_DIM, IDX_HEADS * IDX_DIM, IDX_DIM, IDX_HEADS)
DSA_IN = sum(DSA_SIZES)
DSA_SPLITS = tuple(int(v) for v in np.cumsum(DSA_SIZES)[:-1])


def layer_norm_2(x, g, b):
    xf = x.astype(jnp.float32)
    mu = jnp.mean(xf, axis=-1, keepdims=True)
    var = jnp.mean(jnp.square(xf - mu), axis=-1, keepdims=True)
    y = (xf - mu) * lax.rsqrt(var + LN_EPS) * g.astype(jnp.float32) + b.astype(jnp.float32)
    return y.astype(x.dtype)

def to_blocks(a, nb):
    return jnp.moveaxis(a.reshape((a.shape[0], nb, Q_BLOCK) + a.shape[2:]), 1, 0)

def stick_breaking_attention(q, k, v):
    Bn, S, H, dh = q.shape
    nb = S // Q_BLOCK
    spos = jnp.arange(S)
    scale = dh ** -0.5

    def block(args):
        q_b, bid = args
        tpos = bid * Q_BLOCK + jnp.arange(Q_BLOCK)
        z = jnp.einsum('bqhd,bshd->bhqs', q_b, k).astype(jnp.float32) * scale
        causal = (spos[None, :] < tpos[:, None])[None, None]
        log_beta = jax.nn.log_sigmoid(z)
        log_1mb = jnp.where(causal, jax.nn.log_sigmoid(-z), 0.0)
        csum = jnp.cumsum(log_1mb, axis=-1)
        log_w = log_beta + csum[..., -1:] - csum
        w = jnp.where(causal, jnp.exp(log_w), 0.0).astype(v.dtype)
        return jnp.einsum('bhqs,bshd->bqhd', w, v)

    out = lax.map(block, (to_blocks(q, nb), jnp.arange(nb)))
    return jnp.moveaxis(out, 0, 1).reshape(Bn, S, H * dh)

def _complex_scan_op(e_i, e_j):
    air, aii, bir, bii = e_i
    ajr, aji, bjr, bji = e_j
    ar = ajr * air - aji * aii
    ai = ajr * aii + aji * air
    br = ajr * bir - aji * bii + bjr
    bi = ajr * bii + aji * bir + bji
    return (ar, ai, br, bi)

def s5_ssm(u, log_dt, lam_re, lam_im, b_re, b_im, c_re, c_im, d):
    f32 = jnp.float32
    S = u.shape[1]
    dt = jnp.exp(log_dt.astype(f32))[:, None]
    lr = lam_re.astype(f32)
    li = lam_im.astype(f32)
    mag = jnp.exp(lr * dt)
    abar_r = mag * jnp.cos(li * dt)
    abar_i = mag * jnp.sin(li * dt)
    den = lr * lr + li * li
    nr = abar_r - 1.0
    coef_r = ((nr * lr + abar_i * li) / den)[..., None]
    coef_i = ((abar_i * lr - nr * li) / den)[..., None]
    br = b_re.astype(f32)
    bi = b_im.astype(f32)
    bbar_r = coef_r * br - coef_i * bi
    bbar_i = coef_r * bi + coef_i * br
    uf = u.astype(f32)
    bu_r = jnp.einsum('bsgc,gnc->bsgn', uf, bbar_r)
    bu_i = jnp.einsum('bsgc,gnc->bsgn', uf, bbar_i)
    a_r = jnp.broadcast_to(abar_r, (1, S) + abar_r.shape)
    a_i = jnp.broadcast_to(abar_i, (1, S) + abar_i.shape)
    _, _, x_r, x_i = lax.associative_scan(_complex_scan_op, (a_r, a_i, bu_r, bu_i), axis=1)
    y = (jnp.einsum('gcn,bsgn->bsgc', c_re.astype(f32), x_r)
         - jnp.einsum('gcn,bsgn->bsgc', c_im.astype(f32), x_i)
         + d.astype(f32) * uf)
    return y.astype(u.dtype)

def mixer_sb_ssm(x, w_in, log_dt, lam_re, lam_im, b_re, b_im, c_re, c_im, d, w_glu, b_glu, w_out):
    Bn, S, _ = x.shape
    proj = x @ w_in
    q, k, v, u = jnp.split(proj, [SB_WIDTH, 2 * SB_WIDTH, 3 * SB_WIDTH], axis=-1)
    hs = (Bn, S, SB_HEADS, HEAD_DIM)
    a_out = stick_breaking_attention(q.reshape(hs), k.reshape(hs), v.reshape(hs))
    y = s5_ssm(u.reshape(Bn, S, SSM_GROUPS, SSM_GROUP), log_dt, lam_re, lam_im,
               b_re, b_im, c_re, c_im, d).reshape(Bn, S, SSM_WIDTH)
    y = jax.nn.gelu(y)
    y = y * jax.nn.sigmoid(y @ w_glu + b_glu)
    return jnp.concatenate([a_out, y], axis=-1) @ w_out

def alibi_slopes(n_heads):
    return jnp.asarray(2.0 ** (-8.0 * np.arange(1, n_heads + 1) / n_heads), dtype=jnp.float32)

def mixer_dsa(x, w_in, w_out):
    Bn, S, _ = x.shape
    proj = x @ w_in
    q, k, v, qi, ki, wi = jnp.split(proj, DSA_SPLITS, axis=-1)
    q = q.reshape(Bn, S, DSA_KV_HEADS, DSA_REP, HEAD_DIM)
    k = k.reshape(Bn, S, DSA_KV_HEADS, HEAD_DIM)
    v = v.reshape(Bn, S, DSA_KV_HEADS, HEAD_DIM)
    qi = qi.reshape(Bn, S, IDX_HEADS, IDX_DIM)
    topk = min(TOPK_MAX, S // 4)
    nb = S // Q_BLOCK
    spos = jnp.arange(S)
    slopes = alibi_slopes(DSA_HEADS).reshape(DSA_KV_HEADS, DSA_REP)
    idx_scale = (IDX_DIM ** -0.5) * (IDX_HEADS ** -0.5)

    def block(args):
        q_b, qi_b, wi_b, bid = args
        tpos = bid * Q_BLOCK + jnp.arange(Q_BLOCK)
        rel = jax.nn.relu(jnp.einsum('bqhd,bsd->bqsh', qi_b, ki).astype(jnp.float32))
        score = jnp.einsum('bqsh,bqh->bqs', rel, wi_b.astype(jnp.float32)) * idx_scale
        causal = (spos[None, :] <= tpos[:, None])[None]
        score = jnp.where(causal, score, -jnp.inf)
        _, idx = lax.top_k(score, topk)
        k_sel = jax.vmap(lambda kb, ib: kb[ib])(k, idx)
        v_sel = jax.vmap(lambda vb, ib: vb[ib])(v, idx)
        logits = jnp.einsum('bqgrd,bqkgd->bqgrk', q_b, k_sel).astype(jnp.float32) * (HEAD_DIM ** -0.5)
        dist = (tpos[None, :, None] - idx).astype(jnp.float32)
        logits = logits - slopes[None, None, :, :, None] * dist[:, :, None, None, :]
        valid = (idx <= tpos[None, :, None])[:, :, None, None, :]
        logits = jnp.where(valid, logits, -jnp.inf)
        p = jax.nn.softmax(logits, axis=-1).astype(v.dtype)
        o = jnp.einsum('bqgrk,bqkgd->bqgrd', p, v_sel)
        return o.reshape(Bn, Q_BLOCK, DSA_WIDTH)

    out = lax.map(block, (to_blocks(q, nb), to_blocks(qi, nb), to_blocks(wi, nb), jnp.arange(nb)))
    out = jnp.moveaxis(out, 0, 1).reshape(Bn, S, DSA_WIDTH)
    return out @ w_out

def sq_relu_mlp(x, w1, w2):
    return jnp.square(jax.nn.relu(x @ w1)) @ w2

def second_inputs(seed: int = 0) -> dict:
    key = jax.random.key(seed)
    ks = jax.random.split(key, 32)
    f32 = jnp.float32

    def nrm(k, shape, scale):
        return jax.random.normal(k, shape, f32) * scale

    ws = D_MODEL ** -0.5
    x = nrm(ks[0], (BATCH, SEQ, D_MODEL), 1.0)
    sb_ssm_w_in = jnp.concatenate([
        nrm(ks[1], (N_EVEN, D_MODEL, 2 * SB_WIDTH), ws),
        nrm(ks[2], (N_EVEN, D_MODEL, SB_WIDTH), ws * BETA),
        nrm(ks[3], (N_EVEN, D_MODEL, SSM_WIDTH), ws)], axis=-1)
    ssm_log_dt = jax.random.uniform(ks[4], (N_EVEN, SSM_GROUPS), f32,
                                    minval=math.log(1e-3), maxval=math.log(1e-1))
    n = jnp.arange(SSM_STATE, dtype=f32)
    ssm_lam_re = -0.5 + nrm(ks[5], (N_EVEN, SSM_GROUPS, SSM_STATE), 0.01)
    ssm_lam_im = math.pi * n + nrm(ks[6], (N_EVEN, SSM_GROUPS, SSM_STATE), 0.01)
    bsc = (2 * SSM_GROUP) ** -0.5
    ssm_b_re = nrm(ks[7], (N_EVEN, SSM_GROUPS, SSM_STATE, SSM_GROUP), bsc)
    ssm_b_im = nrm(ks[8], (N_EVEN, SSM_GROUPS, SSM_STATE, SSM_GROUP), bsc)
    csc = (2 * SSM_STATE) ** -0.5
    ssm_c_re = nrm(ks[9], (N_EVEN, SSM_GROUPS, SSM_GROUP, SSM_STATE), csc)
    ssm_c_im = nrm(ks[10], (N_EVEN, SSM_GROUPS, SSM_GROUP, SSM_STATE), csc)
    ssm_d = nrm(ks[11], (N_EVEN, SSM_GROUPS, SSM_GROUP), 1.0)
    ssm_w_glu = nrm(ks[12], (N_EVEN, SSM_WIDTH, SSM_WIDTH), SSM_WIDTH ** -0.5)
    ssm_b_glu = nrm(ks[13], (N_EVEN, SSM_WIDTH), 0.02)
    sb_ssm_w_out = nrm(ks[14], (N_EVEN, MIX_WIDTH, D_MODEL), (MIX_WIDTH ** -0.5) * BETA)
    kvw = DSA_KV_HEADS * HEAD_DIM
    dsa_w_in = jnp.concatenate([
        nrm(ks[15], (N_ODD, D_MODEL, DSA_WIDTH + kvw), ws),
        nrm(ks[16], (N_ODD, D_MODEL, kvw), ws * BETA),
        nrm(ks[17], (N_ODD, D_MODEL, IDX_HEADS * IDX_DIM + IDX_DIM + IDX_HEADS), ws)], axis=-1)
    dsa_w_out = nrm(ks[18], (N_ODD, DSA_WIDTH, D_MODEL), (DSA_WIDTH ** -0.5) * BETA)
    ln_mix_g = 1.0 + nrm(ks[19], (DEPTH, D_MODEL), 0.02)
    ln_mix_b = nrm(ks[20], (DEPTH, D_MODEL), 0.02)
    ln_ffn_g = 1.0 + nrm(ks[21], (DEPTH, D_MODEL), 0.02)
    ln_ffn_b = nrm(ks[22], (DEPTH, D_MODEL), 0.02)
    mlp_w1 = nrm(ks[23], (DEPTH, D_MODEL, D_FF), ws * BETA)
    mlp_w2 = nrm(ks[24], (DEPTH, D_FF, D_MODEL), (D_FF ** -0.5) * BETA)
    return {"x": x, "sb_ssm_w_in": sb_ssm_w_in, "ssm_log_dt": ssm_log_dt,
            "ssm_lam_re": ssm_lam_re, "ssm_lam_im": ssm_lam_im,
            "ssm_b_re": ssm_b_re, "ssm_b_im": ssm_b_im,
            "ssm_c_re": ssm_c_re, "ssm_c_im": ssm_c_im, "ssm_d": ssm_d,
            "ssm_w_glu": ssm_w_glu, "ssm_b_glu": ssm_b_glu, "sb_ssm_w_out": sb_ssm_w_out,
            "dsa_w_in": dsa_w_in, "dsa_w_out": dsa_w_out,
            "ln_mix_g": ln_mix_g, "ln_mix_b": ln_mix_b,
            "ln_ffn_g": ln_ffn_g, "ln_ffn_b": ln_ffn_b,
            "mlp_w1": mlp_w1, "mlp_w2": mlp_w2}

def second_block(x, sb_ssm_w_in, ssm_log_dt, ssm_lam_re, ssm_lam_im, ssm_b_re, ssm_b_im,
              ssm_c_re, ssm_c_im, ssm_d, ssm_w_glu, ssm_b_glu, sb_ssm_w_out,
              dsa_w_in, dsa_w_out, ln_mix_g, ln_mix_b, ln_ffn_g, ln_ffn_b, mlp_w1, mlp_w2):
    for i in range(DEPTH):
        j = i // 2
        if i % 2 == 0:
            h = mixer_sb_ssm(x, sb_ssm_w_in[j], ssm_log_dt[j], ssm_lam_re[j], ssm_lam_im[j],
                             ssm_b_re[j], ssm_b_im[j], ssm_c_re[j], ssm_c_im[j], ssm_d[j],
                             ssm_w_glu[j], ssm_b_glu[j], sb_ssm_w_out[j])
        else:
            h = mixer_dsa(x, dsa_w_in[j], dsa_w_out[j])
        x = layer_norm_2(ALPHA * x + h, ln_mix_g[i], ln_mix_b[i])
        x = layer_norm_2(ALPHA * x + sq_relu_mlp(x, mlp_w1[i], mlp_w2[i]), ln_ffn_g[i], ln_ffn_b[i])
    return x


def setup_inputs(seed=0):
    out = dict(first_inputs(seed))
    for name, value in second_inputs(seed + 1).items():
        if name != "x":
            out[name + "_2"] = value
    return out


def reference(
    x, c, ctx, c_ctx, w_mod, b_mod, ln_g, ln_b, a_w_in, a_norm_g, a_norm_b, a_w_s, a_b_s,
    a_w_out, b_w_in, b_w_gate, b_gate_bias, b_gn_g, b_w_out, p_w_q, p_keys, p_u, p_v,
    sb_ssm_w_in_2, ssm_log_dt_2, ssm_lam_re_2, ssm_lam_im_2, ssm_b_re_2, ssm_b_im_2, ssm_c_re_2,
    ssm_c_im_2, ssm_d_2, ssm_w_glu_2, ssm_b_glu_2, sb_ssm_w_out_2, dsa_w_in_2, dsa_w_out_2,
    ln_mix_g_2, ln_mix_b_2, ln_ffn_g_2, ln_ffn_b_2, mlp_w1_2, mlp_w2_2,
):
    x = first_block(
        x, c, ctx, c_ctx, w_mod, b_mod, ln_g, ln_b, a_w_in, a_norm_g, a_norm_b, a_w_s, a_b_s,
        a_w_out, b_w_in, b_w_gate, b_gate_bias, b_gn_g, b_w_out, p_w_q, p_keys, p_u, p_v,
    )
    return second_block(
        x, sb_ssm_w_in_2, ssm_log_dt_2, ssm_lam_re_2, ssm_lam_im_2, ssm_b_re_2, ssm_b_im_2,
        ssm_c_re_2, ssm_c_im_2, ssm_d_2, ssm_w_glu_2, ssm_b_glu_2, sb_ssm_w_out_2, dsa_w_in_2,
        dsa_w_out_2, ln_mix_g_2, ln_mix_b_2, ln_ffn_g_2, ln_ffn_b_2, mlp_w1_2, mlp_w2_2,
    )


_drawn_inputs = setup_inputs


def setup_inputs(seed=0):
    import zlib

    import numpy as np

    out = dict(_drawn_inputs(seed))
    spreads = {}
    factors = {'ctx': 3.944,
     'c_ctx': 4.432,
     'b_mod': 3.514,
     'a_norm_g': 32.374,
     'a_norm_b': 35.355,
     'a_b_s': 31.085,
     'b_w_gate': 3.197,
     'b_gate_bias': 8.0,
     'b_gn_g': 54.287,
     'ssm_log_dt_2': 47.056,
     'ssm_lam_re_2': 64.0,
     'ssm_lam_im_2': 54.936,
     'ssm_b_re_2': 64.0,
     'ssm_b_im_2': 52.264,
     'ssm_c_re_2': 64.0,
     'ssm_c_im_2': 64.0,
     'ssm_b_glu_2': 49.284}
    for name, (base, spread) in spreads.items():
        noise = np.random.default_rng([zlib.crc32(name.encode()), seed]).standard_normal(out[name].shape)
        drawn = base * np.exp(spread * noise) if base else spread * noise
        out[name] = __import__('jax').numpy.asarray(drawn.astype(out[name].dtype))
    for name, factor in factors.items():
        out[name] = (out[name] * factor).astype(out[name].dtype)
    return out
```

```python
from contextlib import ExitStack

import concourse.bass as bass
from concourse import mybir

F32 = mybir.dt.float32
I32 = mybir.dt.int32
U32 = mybir.dt.uint32
ALU = mybir.AluOpType
ACT = mybir.ActivationFunctionType
AX = mybir.AxisListType.X

EPS = 1e-5
ALPHA = 4.0 ** 0.25
NEG = -3.0e38
TWO_PI = 6.283185307179586
PI = 3.141592653589793


class Engine:

    def __init__(self, eng, sem):
        self.eng, self.sem, self.n, self.seen = eng, sem, 0, {}

    def free(self, *tokens):
        for sem, value in tokens:
            if self.seen.get(sem, 0) < value:
                self.eng.wait_ge(sem, value)
                self.seen[sem] = value
        return self.eng

    def at(self, *tokens):
        return self.free(*tokens, (self.sem, self.n))

    def done(self, ins):
        ins.then_inc(self.sem, 1)
        self.n += 1
        return (self.sem, self.n)

    def last(self):
        return (self.sem, self.n)


class Ring:

    def __init__(self, views, sems):
        self.views, self.sems = views, sems
        self.n = len(views)
        self.turn = 0
        self.count = [0] * self.n
        self.readers = [()] * self.n

    def take(self):
        s = self.turn
        self.turn = (s + 1) % self.n
        assert self.readers[s] is not None
        r, self.readers[s] = self.readers[s], None
        return s, self.views[s], r

    def loaded(self, s, ins):
        ins.then_inc(self.sems[s], 16)
        self.count[s] += 16
        return (self.sems[s], self.count[s])

    def release(self, s, *tokens):
        self.readers[s] = tokens


def program(nc, A, out, parts=("mod0", "mix0", "peer0", "mod1", "mix1", "peer1", "sb", "mlp0", "dsa", "mlp1")):
    ctx = ExitStack()

    def sb(name, shape, dt=F32):
        return ctx.enter_context(nc.sbuf_tensor(name, shape, dt))

    def sem(name):
        return ctx.enter_context(nc.semaphore(name))

    PE = Engine(nc.tensor, sem("s_pe"))
    V = Engine(nc.vector, sem("s_v"))
    S = Engine(nc.scalar, sem("s_act"))
    G = Engine(nc.gpsimd, sem("s_pool"))
    D = Engine(nc.sync, sem("s_sp"))

    X = sb("X", [128, 4, 1024])
    H = sb("H", [128, 4, 1024])
    HT = sb("HT", [128, 8, 512])
    BIG = sb("BIG", [128, 16384])
    WRt = sb("WR", [128, 5, 2048])
    BCt = sb("BC", [128, 5, 1024])
    NG = 12
    GRt = BIG[:, 0:NG * 1024].rearrange("p (s n) -> p s n", s=NG)
    QT = BIG[:, NG * 1024:16384].rearrange("p (h t) -> p h t", h=8)

    PSt = ctx.enter_context(nc.psum_tensor("PS", [128, 8, 512], F32))
    PS = Ring([PSt[:, i, :] for i in range(4)], [None] * 4)
    PO = Ring([PSt[:, 4 + 2 * i:6 + 2 * i, :] for i in range(2)], [None] * 2)
    WR = Ring([WRt[:, i, :] for i in range(5)], [sem(f"s_w{i}") for i in range(5)])
    BC = Ring([BCt[:, i, :] for i in range(5)], [sem(f"s_b{i}") for i in range(5)])
    GR = Ring([GRt[:, i, :] for i in range(NG)], [sem(f"s_g{i}") for i in range(NG)])

    ident = sb("ident", [128, 128])
    ones = sb("ones", [128, 128])
    iota16 = sb("iota16", [128, 16])
    kbd = sb("kbd", [128, 256])
    stat = sb("stat", [128, 4, 12])
    mv = sb("mv", [128, 4, 2])
    sd = sb("sd", [128, 4])
    rs = sb("rs", [128, 4])
    tmp = sb("tmp", [128, 512])
    scT = sb("scT", [128, 8, 2])
    scS = sb("scS", [128, 8, 2])
    mrow = sb("mrow", [2, 2, 512])
    MR = Ring([mrow[:, i, :] for i in range(2)], [sem(f"s_m{i}") for i in range(2)])
    s_ms = [sem(f"s_ms{i}") for i in range(2)]
    ms_count = [0, 0]
    one_loads = [0]
    DG = Ring([sb(f"dg{i}", [128, 128]) for i in range(3)], [None] * 3)

    V16 = sb("V16", [128, 16, 16])
    I16 = sb("I16", [128, 16, 16], U32)
    T16 = sb("T16", [128, 8, 16])
    P16 = sb("P16", [128, 8, 16], U32)
    IDX = sb("IDX", [128, 2, 128], I32)
    WT = sb("WT", [128, 2, 128])
    ACTV = sb("ACTV", [128, 2, 128])
    small = sb("small", [128, 8])
    SC = sb("SC", [128, 2048])
    cand = sb("cand", [128, 256])

    modd = nc.dram_tensor("modd", (2, 2, 6144), F32, kind="Internal").ap()

    def load_once(dst, src, *tokens):
        s = sem(f"s_one{one_loads[0]}")
        one_loads[0] += 1
        D.free(*tokens).dma_start(dst, src).then_inc(s, 16)
        return (s, 16)

    def everyone():
        return (PE.last(), V.last(), S.last(), G.last())

    def barrier():
        t = everyone()
        for e in (PE, V, S, G):
            e.free(*t)
        return t

    def load_bc(row, *tokens):
        s, view, readers = BC.take()
        t = BC.loaded(s, D.free(*readers, *tokens).dma_start(view, row.partition_broadcast(128)))
        return s, view, t

    def load_w(src, p=128):
        s, view, readers = WR.take()
        _, a, b = src.shape
        view = view[0:p, 0:a * b].rearrange("p (a b) -> p a b", a=a)
        t = WR.loaded(s, D.free(*readers).dma_start(view, src))
        return s, view, t

    def load_slab(w, n0, n, p=128, kts=8):
        wv = w.rearrange("(k p) n -> p k n", p=p)
        return [load_w(wv[:, k:k + 4, n0:n0 + n], p) for k in range(0, kts, 4)]

    def group(dst, pairs, *tokens):
        e = PE.free(*tokens)
        last = len(pairs) - 1
        for j, (lhs, rhs, *tk) in enumerate(pairs):
            PE.free(*tk)
            mm = e.matmul(dst, lhs, rhs, start=(j == 0), stop=(j == last))
        return PE.done(mm)

    def release_w(slots, t):
        for s, _, _ in slots:
            WR.release(s, t)

    def rows_proj(slab, lhs, blks, n, evac, *tokens):
        for b in blks:
            s, ps, readers = PS.take()
            t = group(ps[:, 0:n], [(lhs(k, b), slab[k // 4][1][:, k % 4, 0:n], slab[k // 4][2])
                                   for k in range(4 * len(slab))], *readers, *tokens)
            PS.release(s, evac(b, ps[:, 0:n], t))
        release_w(slab, t)

    def cols_proj(slab, cols, rhs, n, evac, *tokens):
        for name, c0, m in cols:
            s, ps, readers = PS.take()
            t = group(ps[0:m, 0:n], [(slab[k // 4][1][:, k % 4, c0:c0 + m], rhs(k), slab[k // 4][2])
                                     for k in range(4 * len(slab))], *readers, *tokens)
            PS.release(s, evac(name, ps[0:m, 0:n], t))
        release_w(slab, t)

    flip = [0]

    def copy_out(dst, src, t, *tokens):
        flip[0] ^= 1
        if flip[0]:
            return S.done(S.free(t, *tokens).activation(dst, src, ACT.Copy))
        return V.done(V.free(t, *tokens).tensor_copy(dst, src))

    def to_HT(src, blks, *tokens):
        done = []
        for b in blks:
            for g in range(2):
                s, ps, readers = PS.take()
                e = PE.free(*readers, *tokens)
                for j in range(4):
                    k = 4 * g + j
                    mm = e.transpose(ps[:, j * 128:(j + 1) * 128], src[:, b, k * 128:(k + 1) * 128], ident[:, :])
                t = PE.done(mm)
                t = copy_out(HT[:, 4 * g:4 * g + 4, b * 128:(b + 1) * 128],
                             ps.rearrange("p (a b) -> p a b", a=4), t)
                PS.release(s, t)
                done.append(t)
        return done

    def normalize(src, dst, i, n, *tokens):
        w = min(n, 512)
        for j in range(n // w):
            V.done(V.at(*tokens).bn_stats(stat[:, i, 6 * j:6 * j + 6], src[:, j * w:(j + 1) * w]))
        V.done(V.at().bn_aggr(mv[:, i, :], stat[:, i, 0:6 * (n // w)]))
        t = V.done(V.at().tensor_scalar(mv[:, i, 1:2], mv[:, i, 1:2], EPS, None, ALU.add))
        t = S.done(S.at(t).activation(sd[:, i:i + 1], mv[:, i, 1:2], ACT.Sqrt))
        V.done(V.at(t).reciprocal(rs[:, i:i + 1], sd[:, i:i + 1]))
        return V.done(V.at().tensor_scalar(dst, src, mv[:, i, 0:1], rs[:, i:i + 1], ALU.subtract, ALU.mult))

    def layer_norm(pairs, g_row, b_row, *tokens):
        sg, gv, tg = load_bc(g_row)
        sb_, bv, tb = load_bc(b_row)
        for i, (src, dst) in enumerate(pairs):
            normalize(src, dst, i % 4, 1024, *tokens)
            V.done(V.at(tg).tensor_tensor(dst, dst, gv, ALU.mult))
            t = V.done(V.at(tb).tensor_tensor(dst, dst, bv, ALU.add))
        BC.release(sg, t)
        BC.release(sb_, t)
        return t

    def residual(b, n0, ps, t, gate=None):
        xs = X[:, b, n0:n0 + 512]
        if gate is None:
            return V.done(V.at(t).scalar_tensor_tensor(xs, xs, ALPHA, ps, ALU.mult, ALU.add))
        view, tg = gate
        t = V.done(V.at(t, tg).tensor_tensor(tmp[:, :], ps, view[:, n0:n0 + 512], ALU.mult))
        return V.done(V.at(t).scalar_tensor_tensor(xs, xs, ALPHA, tmp[:, :], ALU.mult, ALU.add)), t

    streams = {0: 0, 1: 0, 2: 1, 3: 1}
    mod_done = {}

    def mod_row(l, j, st):
        return modd[l, st, j * 1024:(j + 1) * 1024]

    def modulated(l, j_shift, j_scale, blks):
        for st in (0, 1):
            own = [b for b in blks if streams[b] == st]
            if not own:
                continue
            s1, sc_v, t1 = load_bc(mod_row(l, j_scale, st), *mod_done[l])
            s2, sh_v, t2 = load_bc(mod_row(l, j_shift, st), *mod_done[l])
            for b in own:
                V.done(V.at(t1).scalar_tensor_tensor(H[:, b, :], sc_v, 1.0, X[:, b, :], ALU.add, ALU.mult))
                t = V.done(V.at(t2).tensor_tensor(H[:, b, :], H[:, b, :], sh_v, ALU.add))
            BC.release(s1, t)
            BC.release(s2, t)
        return t

    t_x = []
    xv = A["x"][0].rearrange("(b p) d -> p b d", p=128)
    cv = A["ctx"][0].rearrange("(b p) d -> p b d", p=128)
    t_x.append(load_once(X[:, 0:2, :], xv))
    t_x.append(load_once(X[:, 2:4, :], cv))
    t_sc = load_once(scT[:, :, :], A["cT"])
    G.done(G.at().memset(ones[:, :], 1.0))
    t_ones = G.last()
    G.done(G.at().affine_select(out=ident[:, :], in_=ones[:, :], compare_op=ALU.is_equal, fill=0.0, base=0,
                                pattern=[[-1, 128]], channel_multiplier=1))
    G.done(G.at().iota(iota16[:, :], pattern=[[1, 16]], base=0, channel_multiplier=0,
                       allow_small_or_imprecise_dtypes=True))
    t_const = G.done(G.at().memset(kbd[:, :], 0.0))
    barrier()

    def modulation(l):
        w = A["w_mod"][l]
        last = []
        for n in range(12):
            slab = load_slab(w, n * 512, 512)
            m, row, readers = MR.take()
            t_b = MR.loaded(m, D.free(*readers).dma_start(
                row, A["b_mod"][l, n * 512:(n + 1) * 512].partition_broadcast(2)))
            s, ps, readers = PS.take()
            t = group(ps[0:2, :], [(scS[:, k, :], slab[k // 4][1][:, k % 4, :], slab[k // 4][2])
                                   for k in range(8)], *readers, *t_silu)
            release_w(slab, t)
            t = V.done(V.at(t, t_b).tensor_tensor(row, row, ps[0:2, :], ALU.add))
            PS.release(s, t)
            S.free(t).dma_start(modd[l, :, n * 512:(n + 1) * 512], row).then_inc(s_ms[m], 16)
            ms_count[m] += 16
            MR.release(m, (s_ms[m], ms_count[m]))
        mod_done[l] = [(s_ms[0], ms_count[0]), (s_ms[1], ms_count[1])]

    def chunk_mlp():
        blks = range(4)
        t = modulated(0, 0, 1, blks)
        t_h = to_HT(H, blks, t)
        U = BIG[:, 0:4096].rearrange("p (b n) -> p b n", b=4)
        Vv = BIG[:, 4096:8192].rearrange("p (b n) -> p b n", b=4)
        bs = small[:, 0:8]
        t_bs = load_once(bs, A["a_b_sT"])
        t_w = []
        for n in (2, 3, 0, 1):
            slab = load_slab(A["a_w_in"][0], n * 512, 512)
            dst = (U, Vv)[n // 2]

            def evac(b, ps, t):
                return S.done(S.free(t).activation(dst[:, b, (n % 2) * 512:(n % 2) * 512 + 512], ps,
                                                   ACT.Gelu_apprx_tanh))

            rows_proj(slab, lambda k, b: HT[:, k, b * 128:(b + 1) * 128], blks, 512, evac, *t_h)
        t_u = S.last()
        t_v = layer_norm([(Vv[:, b, :], Vv[:, b, :]) for b in blks], A["a_norm_g"][0], A["a_norm_b"][0], t_u)
        ws, wsv, wst = load_w(A["a_w_sT"])
        for b in blks:
            for hh in range(2):
                s, ps, readers = PS.take()
                e = PE.free(t_v, wst, *readers)
                for j in range(4):
                    h = 4 * hh + j
                    mm = e.matmul(ps[:, j * 128:(j + 1) * 128], wsv[:, h, :], Vv[:, b, h * 128:(h + 1) * 128],
                                  start=True, stop=True)
                t = PE.done(mm)
                for j in range(4):
                    h = 4 * hh + j
                    us = U[:, b, h * 128:(h + 1) * 128]
                    t2 = V.done(V.at(t, t_bs).scalar_tensor_tensor(us, ps[:, j * 128:(j + 1) * 128], bs[:, h:h + 1],
                                                                   us, ALU.add, ALU.mult))
                PS.release(s, t2)
        WR.release(ws, t)
        t_h = to_HT(U, blks, V.last(), PE.last())
        mixer_out(A["a_w_out"][0], 0, blks, t_h)

    def mixer_out(w, l, blks, t_h):
        gates = {}
        for st in sorted({streams[b] for b in blks}):
            gates[st] = load_bc(mod_row(l, 2, st), *mod_done[l])
        for n in range(2):
            slab = load_slab(w, n * 512, 512)

            def evac(b, ps, t):
                _, view, tg = gates[streams[b]]
                return residual(b, n * 512, ps, t, (view, tg))[1]

            rows_proj(slab, lambda k, b: HT[:, k, b * 128:(b + 1) * 128], blks, 512, evac, *t_h)
        for s, _, _ in gates.values():
            BC.release(s, V.last())
        layer_norm([(X[:, b, :], X[:, b, :]) for b in blks], A["ln_g"][l, 0], A["ln_b"][l, 0])

    def peer(l, blks):
        barrier()
        t_k = [load_once(kbd[0:64, 0:128], A["keysT"][l, 0], *everyone()),
               load_once(kbd[64:128, 128:256], A["keysT"][l, 1])]
        t = modulated(l, 3, 4, blks)
        t_h = to_HT(H, blks, t)
        nt = 128 * len(blks)
        for n in range(2):
            slab = load_slab(A["p_w_q"][l], n * 512, 512)

            def evac(h, ps, t):
                return copy_out(QT[:, h, 0:nt], ps, t)

            cols_proj(slab, [(4 * n + j, j * 128, 128) for j in range(4)], lambda k: HT[:, k, 0:nt], nt, evac, *t_h)
        t_q = (V.last(), S.last())
        barrier()
        ready = {}
        IV = I16[:, :, :]
        used = {0: (), 1: ()}

        def route(b):
            i = b % 2
            t_s = []
            for q in range(4):
                s, ps, readers = PS.take()
                e = PE.free(*t_k, *t_q, *readers)
                for j in range(2):
                    mm = e.matmul(ps[:, j * 256:(j + 1) * 256], QT[:, 2 * q + j, b * 128:(b + 1) * 128], kbd[:, :],
                                  start=True, stop=True)
                t = PE.done(mm)
                t = S.done(S.free(t, V.last()).activation(SC[:, q * 512:(q + 1) * 512], ps, ACT.Copy))
                PS.release(s, t)
                t_s.append(t)
            yield
            for r in range(16):
                sc = SC[:, r * 128:(r + 1) * 128]
                V.done(V.at(t_s[r // 4]).max(V16[:, r, 0:8], sc))
                V.done(V.at().max_index(I16[:, r, 0:8], V16[:, r, 0:8], sc))
                yield
                V.done(V.at().match_replace(sc, V16[:, r, 0:8], sc, NEG))
                V.done(V.at().max(V16[:, r, 8:16], sc))
                yield
                V.done(V.at().max_index(I16[:, r, 8:16], V16[:, r, 8:16], sc))
            yield
            c3 = cand[:, :].rearrange("p (a b) -> p a b", a=16)
            for h in range(8):
                V.done(V.at().tensor_tensor(c3, V16[:, 2 * h, :].unsqueeze(2).to_broadcast([128, 16, 16]),
                                            V16[:, 2 * h + 1, :].unsqueeze(1).to_broadcast([128, 16, 16]), ALU.add))
                V.done(V.at().max(T16[:, h, 0:8], cand[:, :]))
                yield
                V.done(V.at().max_index(P16[:, h, 0:8], T16[:, h, 0:8], cand[:, :]))
                V.done(V.at().match_replace(cand[:, :], T16[:, h, 0:8], cand[:, :], NEG))
                yield
                V.done(V.at().max(T16[:, h, 8:16], cand[:, :]))
                V.done(V.at().max_index(P16[:, h, 8:16], T16[:, h, 8:16], cand[:, :]))
                yield
            If = cand[:, :].rearrange("p (h q a) -> p h q a", h=8, q=2)
            V.done(V.at().tensor_copy(cand[:, :], I16[:, :, :].rearrange("p r a -> p (r a)")))
            pos = P16[:, :, :].rearrange("p h k -> p (h k)")
            half = V16[:, 0:8, :].rearrange("p h k -> p (h k)")
            other = V16[:, 8:16, :].rearrange("p h k -> p (h k)")
            halfu = half.bitcast(U32)
            picked = I16[:, 0:8, :].rearrange("p h k -> p (h k)").bitcast(F32)
            oh4 = SC[:, :].rearrange("p (h k a) -> p h k a", h=8, k=16)
            for q, (op, arg) in enumerate(((ALU.logical_shift_right, 4), (ALU.bitwise_and, 15))):
                V.done(V.at().tensor_scalar(halfu, pos, arg, None, op))
                V.done(V.at().tensor_copy(other, halfu))
                yield
                V.done(V.at().tensor_tensor(oh4, V16[:, 8:16, :].unsqueeze(3).to_broadcast([128, 8, 16, 16]),
                                            iota16[:, :].unsqueeze(1).unsqueeze(1).to_broadcast([128, 8, 16, 16]),
                                            ALU.is_equal))
                yield
                V.done(V.at().tensor_tensor(oh4, oh4, If[:, :, q, :].unsqueeze(2).to_broadcast([128, 8, 16, 16]),
                                            ALU.mult))
                yield
                dst = (picked, other)[q]
                V.done(V.at().tensor_reduce(dst, SC[:, :].rearrange("p (k a) -> p k a", a=16), AX, ALU.add))
                yield
            V.done(V.at().tensor_scalar(picked, picked, 128.0, float(l * 16384), ALU.mult, ALU.add))
            V.done(V.at(*used[i]).tensor_tensor(IDX[:, i, :], picked, other, ALU.add))
            t_idx = V.last()
            w3 = WT[:, i, :].rearrange("p (h k) -> p h k", h=8)
            t = V.done(V.at().tensor_tensor(w3, T16[:, :, :], T16[:, :, 0:1].to_broadcast([128, 8, 16]), ALU.subtract))
            t = S.done(S.at(t).activation(WT[:, i, :], WT[:, i, :], ACT.Exp))
            V.done(V.at(t).tensor_reduce(small[:, 0:8], w3, AX, ALU.add))
            V.done(V.at().reciprocal(small[:, 0:8], small[:, 0:8]))
            V.done(V.at().tensor_tensor(w3, w3, small[:, 0:8].unsqueeze(2).to_broadcast([128, 8, 16]), ALU.mult))
            ready[b] = (t_idx, V.last())

        def gather(table, b, j):
            s, view, readers = GR.take()
            e = G.free(*readers, ready[b][0])
            t = GR.loaded(s, e.indirect_dma_start(view, None, table, bass.IndirectOffsetOnAxis(
                ap=IDX[:, b % 2, j:j + 1], axis=0)))
            return s, view, t

        sg, gv, tg = load_bc(A["ln_g"][l, 1])
        sb_, bv, tb = load_bc(A["ln_b"][l, 1])
        gates = {st: load_bc(mod_row(l, 5, st), *mod_done[l]) for st in sorted({streams[b] for b in blks})}
        for _ in route(blks[0]):
            pass
        for b in blks:
            i = b % 2
            nxt = route(b + 1) if b + 1 in blks else iter(())
            av = ACTV[:, i, :]
            for j in range(128):
                s, view, t = gather(A["p_u"], b, j)
                t = V.done(V.free(t).tensor_tensor_reduce(view, view, H[:, b, :], 1.0, 0.0, ALU.mult, ALU.add,
                                                          av[:, j:j + 1]))
                GR.release(s, t)
            t = S.done(S.at(V.last()).activation(av, av, ACT.Gelu_apprx_tanh))
            t_a = V.done(V.at(t, ready[b][1]).tensor_tensor(av, av, WT[:, i, :], ALU.mult))
            so, po, readers = PO.take()
            PE.free(*readers)
            for j in range(128):
                s, view, t = gather(A["p_v"], b, j)
                sdg, dg, dr = DG.take()
                td = S.done(S.free(t_a, *dr).activation(dg[:, :], ident[:, :], ACT.Copy, scale=av[:, j:j + 1]))
                for half in range(2):
                    mm = PE.free(t, td).matmul(po[:, half, :], dg[:, :], view[:, half * 512:(half + 1) * 512],
                                               start=(j == 0), stop=(j == 127))
                t = PE.done(mm)
                GR.release(s, t)
                DG.release(sdg, t)
                next(nxt, None)
            used[i] = ((GR.sems[s], GR.count[s]),) + tuple((GR.sems[k], GR.count[k]) for k in range(NG))
            for _ in nxt:
                pass
            _, view, tgate = gates[streams[b]]
            for half in range(2):
                _, tp = residual(b, half * 512, po[:, half, :], t, (view, tgate))
            PO.release(so, tp)
            normalize(X[:, b, :], X[:, b, :], 0, 1024)
            V.done(V.at(tg).tensor_tensor(X[:, b, :], X[:, b, :], gv, ALU.mult))
            V.done(V.at(tb).tensor_tensor(X[:, b, :], X[:, b, :], bv, ALU.add))
        for s in [sg, sb_] + [g[0] for g in gates.values()]:
            BC.release(s, V.last())
        barrier()

    def gla():
        barrier()
        tri = [SC[:, 0:128], SC[:, 128:256]]
        glT = SC[0:17, 256:1280].rearrange("p (j t) -> p j t", j=2)
        q_ = BIG[:, 0:1024].rearrange("p (h t) -> p h t", h=4)
        k_ = BIG[:, 1024:3072].rearrange("p (h t) -> p h t", h=4)
        v_ = BIG[:, 3072:7168].rearrange("p (b n) -> p b n", b=4)
        bT = BIG[:, 7168:11264].rearrange("p (u t) -> p u t", u=8)
        o = 11264
        EB, EN = BIG[:, o:o + 256], BIG[:, o + 256:o + 512]
        KD = BIG[:, o + 512:o + 1024]
        QI, KI = BIG[:, o + 1024:o + 1280], BIG[:, o + 1280:o + 1536]
        QP = BIG[:, o + 1536:o + 2048].rearrange("p (a b t) -> p a b t", a=2, b=2)
        KE = BIG[:, o + 2048:o + 3072].rearrange("p (a b t) -> p a b t", a=2, b=4)
        ATT = BIG[:, o + 3072:o + 3584].rearrange("p (a b t) -> p a b t", a=2, b=2)
        SS = BIG[:, o + 3584:o + 4608].rearrange("p (a n) -> p a n", a=4)
        wgt = BIG[0:17, o:o + 1024].rearrange("p (j n) -> p j n", j=2)
        r_ = H[:, 0:2, :]
        G.done(G.at().affine_select(out=tri[0], in_=ones[:, :], compare_op=ALU.is_ge, fill=0.0, base=0,
                                    pattern=[[1, 128]], channel_multiplier=-1))
        G.done(G.at().memset(SC[0:64, 64:128], 0.0))
        G.done(G.at().affine_select(out=tri[1], in_=ones[:, :], compare_op=ALU.is_ge, fill=0.0, base=0,
                                    pattern=[[-1, 128]], channel_multiplier=1))
        G.done(G.at().memset(SC[64:128, 128:192], 0.0))
        G.done(G.at().memset(SC[0:32, 256:1280], 1.0))
        G.done(G.at().memset(ATT[:, :, :, :], 0.0))
        G.done(G.at().memset(BIG[:, o + 1536:o + 3072], 0.0))
        t_g = G.last()
        t_wg = [load_once(wgt[0:16, :, :], A["b_w_gate"][0].rearrange("j r d -> r j d")),
                load_once(wgt[16:17, :, :], A["b_gate_bias"])]
        t = modulated(1, 0, 1, range(4))
        t_h = to_HT(H, range(4), t)
        barrier()
        w = A["b_w_in"][0]

        def to(dst):
            return lambda name, ps, t: copy_out(dst(name), ps, t)

        slab = load_slab(w, 0, 512)
        cols_proj(slab, [(h, h * 128, 128) for h in range(4)], lambda k: HT[:, k, 0:256], 256,
                  to(lambda h: q_[:, h, :]), *t_h)
        slab = load_slab(w, 512, 512)
        cols_proj(slab, [(h, h * 128, 128) for h in range(4)], lambda k: HT[:, k, :], 512,
                  to(lambda h: k_[:, h, :]), *t_h)
        wv = w.rearrange("(k p) n -> p k n", p=128)
        slab = [load_w(wv[:, k:k + 4, 3072:3104]) for k in (0, 4)]
        cols_proj(slab, [(j, j * 16, 16) for j in range(2)], lambda k: HT[:, k, :], 512,
                  lambda j, ps, t: S.done(S.free(t, t_g).activation(glT[0:16, j, :], ps, ACT.Copy)), *t_h)
        t_gl = S.last()
        for n in range(2):
            slab = load_slab(w, 1024 + n * 512, 512)
            rows_proj(slab, lambda k, b: HT[:, k, b * 128:(b + 1) * 128], range(4), 512,
                      lambda b, ps, t: copy_out(v_[:, b, n * 512:n * 512 + 512], ps, t), *t_h)
        for n in range(2):
            slab = load_slab(w, 2048 + n * 512, 512)
            rows_proj(slab, lambda k, b: HT[:, k, b * 128:(b + 1) * 128], range(2), 512,
                      lambda b, ps, t: S.done(S.free(t).activation(r_[:, b, n * 512:n * 512 + 512], ps, ACT.Silu)),
                      *t_h)
        prev = {}
        for b in range(4):
            gt = H[:, 2 + b % 2, :]
            for j in range(2):
                s, ps, readers = PS.take()
                t = group(ps, [(glT[0:17, j, b * 128:(b + 1) * 128], wgt[0:17, j, :])], t_gl, *t_wg, t_g, *readers)
                gs = gt[:, j * 512:(j + 1) * 512]
                S.done(S.at(t, *prev.get(b % 2, ())).activation(gs, ps, ACT.Abs))
                S.done(S.at().activation(gs, gs, ACT.Exp, scale=-1.0))
                t = S.done(S.at().activation(gs, gs, ACT.Ln, bias=1.0))
                t = V.done(V.at(t).scalar_tensor_tensor(gs, ps, 0.0, gs, ALU.min, ALU.subtract))
                PS.release(s, t)
                t_gg = t
                s, ps, readers = PS.take()
                e = PE.free(t_gg, *readers)
                for h in range(4):
                    mm = e.matmul(ps[:, h * 128:(h + 1) * 128], gs[:, h * 128:(h + 1) * 128], tri[j],
                                  start=True, stop=True)
                t = PE.done(mm)
                prev[b % 2] = (t,)
                t = S.done(S.at(t).activation(bT[:, 4 * j:4 * j + 4, b * 128:(b + 1) * 128],
                                              ps.rearrange("p (h t) -> p h t", h=4), ACT.Copy, scale=1.0 / 16.0))
                PS.release(s, t)
        barrier()
        Y = H[:, 2:4, :]
        s_turn = 0
        s_read = {}
        for h in range(4):
            so, po, readers = PO.take()
            PE.free(*readers)
            first = [True, True]
            for j in range(2):
                bt = bT[:, 4 * j + h, :]
                b3 = bt.rearrange("p (c t) -> p c t", t=64)
                end = 63 if j == 0 else 0
                t0 = PE.last()
                S.done(S.at(t0).activation(EB, bt[:, 0:256], ACT.Exp))
                S.done(S.at(V.last()).activation(EN, bt[:, 0:256], ACT.Exp, scale=-1.0))
                dc = small[:, 0:8]
                t_dc = S.done(S.at().activation(dc, b3[:, :, end], ACT.Exp))
                kd3 = KD.rearrange("p (c t) -> p c t", t=64)
                t = V.done(V.at(t0).tensor_tensor(kd3, b3[:, :, end:end + 1].to_broadcast([128, 8, 64]), b3,
                                                  ALU.subtract))
                t = S.done(S.at(t).activation(KD, KD, ACT.Exp))
                V.done(V.at(t).tensor_tensor(KD, KD, k_[:, h, :], ALU.mult))
                t_kd = V.last()
                V.done(V.at().scalar_tensor_tensor(QI, q_[:, h, :], 128.0 ** -0.5, EB, ALU.mult, ALU.mult))
                V.done(V.at().tensor_tensor(KI, k_[:, h, 0:256], EN, ALU.mult))
                q3 = QI.rearrange("p (b t) -> p b t", b=2)
                for a in range(2):
                    t_q = V.done(V.at().tensor_copy(QP[:, a, :, a * 64:a * 64 + 64], q3[:, :, a * 64:a * 64 + 64]))
                s, ps, readers = PS.take()
                e = PE.free(t_kd, *readers)
                for b in range(4):
                    mm = e.transpose(ps[:, b * 128:(b + 1) * 128], KD[:, b * 128:(b + 1) * 128], ident[:, :])
                t = PE.done(mm)
                p3 = ps.rearrange("p (b t) -> p b t", b=4)
                for a in range(2):
                    t_ke = V.done(V.at(t).tensor_copy(KE[a * 64:a * 64 + 64, a, :, :], p3[a * 64:a * 64 + 64, :, :]))
                PS.release(s, t_ke)
                s, ps, readers = PS.take()
                e = PE.free(t_q, *readers)
                for b in range(2):
                    mm = e.matmul(ps[:, b * 128:(b + 1) * 128], KI[:, b * 128:(b + 1) * 128],
                                  QI[:, b * 128:(b + 1) * 128], start=True, stop=True)
                t = PE.done(mm)
                for b in range(2):
                    t_at = V.done(V.at(t).copy_predicated(ATT[:, j, b, :], tri[j].bitcast(I32),
                                                          ps[:, b * 128:(b + 1) * 128]))
                PS.release(s, t_at)
                e = PE.free(t_at)

                def acc(b, lhs, rhs, last=False):
                    mm = e.matmul(po[:, b, 0:256], lhs, rhs, start=first[b], stop=last)
                    first[b] = False
                    return mm

                for b in range(2):
                    acc(b, ATT[:, j, b, :], v_[:, b, h * 256:(h + 1) * 256])
                order = [(2, 0), (2, 1), (3, 0), (3, 1), (0, 0), (0, 1), (1, 0), (1, 1)]
                if j == 1:
                    order = [(3, 1), (3, 0), (2, 1), (2, 0), (1, 1), (1, 0), (0, 1), (0, 0)]
                st, t_st = None, None
                left = {0: 2, 1: 2}
                for n, (b, a) in enumerate(order):
                    if b < 2:
                        PE.free(t_st)
                        left[b] -= 1
                        t = PE.done(acc(b, QP[:, a, b, :], st, last=(j == 1 and left[b] == 0)))
                        s_read[s_turn] = t
                    if n == 7:
                        break
                    s, ps, readers = PS.take()
                    t = group(ps[:, 0:256], [(KE[:, a, b, :], v_[:, b, h * 256:(h + 1) * 256])], t_ke, *readers)
                    nt = (s_turn + 1) % 4
                    new = SS[:, nt, :]
                    w_ = [s_read[nt]] if nt in s_read else []
                    if n == 0:
                        t_st = V.done(V.at(t, *w_).tensor_copy(new, ps[:, 0:256]))
                    else:
                        c = 2 * b + a
                        t_st = V.done(V.at(t, t_dc, *w_).scalar_tensor_tensor(new, st, dc[:, c:c + 1], ps[:, 0:256],
                                                                              ALU.mult, ALU.add))
                    PS.release(s, t_st)
                    st, s_turn = new, nt
            t = PE.last()
            for b in range(2):
                normalize(po[:, b, 0:256], Y[:, b, h * 256:(h + 1) * 256], b, 256, t)
            PO.release(so, V.last())
        sgn, gnv, tgn = load_bc(A["b_gn_g"][0])
        for b in range(2):
            V.done(V.at(tgn).tensor_tensor(Y[:, b, :], Y[:, b, :], gnv, ALU.mult))
            t = V.done(V.at().tensor_tensor(Y[:, b, :], Y[:, b, :], r_[:, b, :], ALU.mult))
        BC.release(sgn, t)
        t_h = to_HT(Y, range(2), t, PE.last())
        mixer_out(A["b_w_out"][0], 1, range(2), t_h)

    def sb_ssm():
        barrier()
        t_h = to_HT(X, range(2))
        ZZ = BIG[:, 0:4096].rearrange("p (h n) -> p h n", h=8)
        LL = BIG[:, 4096:8192].rearrange("p (h n) -> p h n", h=8)
        NN = BIG[:, 8192:12288].rearrange("p (h n) -> p h n", h=8)
        q_ = BIG[0:64, 12288:14336].rearrange("p (h t) -> p h t", h=8)
        k_ = BIG[0:64, 14336:16384].rearrange("p (h t) -> p h t", h=8)
        v_ = H[:, 0, :].rearrange("p (b n) -> p b n", b=2)
        uT = H[:, 1, :].rearrange("p (c t) -> p c t", c=4)
        yT = H[:, 2, :].rearrange("p (c t) -> p c t", c=4)
        zT = H[:, 3, :].rearrange("p (c t) -> p c t", c=4)
        strict = SC[:, 0:128]
        mask = SC[:, 128:640].rearrange("p (b q) -> p b q", b=2)
        G.done(G.at().affine_select(out=strict, in_=ones[:, :], compare_op=ALU.is_gt, fill=0.0, base=0,
                                    pattern=[[-1, 128]], channel_multiplier=1))
        G.done(G.at().memset(SC[:, 128:640], 1.0))
        t_m = G.done(G.at().affine_select(out=mask, in_=mask, compare_op=ALU.is_gt, fill=0.0, base=0,
                                          pattern=[[-128, 2], [1, 256]], channel_multiplier=-1))
        w = A["sb_ssm_w_in_2"][0]
        hT = lambda k: HT[:, k, 0:256]
        slab = load_slab(w, 0, 512)
        cols_proj(slab, [(h, h * 64, 64) for h in range(8)], hT, 256, lambda h, ps, t: copy_out(q_[:, h, :], ps, t), *t_h)
        slab = load_slab(w, 512, 512)
        cols_proj(slab, [(h, h * 64, 64) for h in range(8)], hT, 256, lambda h, ps, t: copy_out(k_[:, h, :], ps, t), *t_h)
        slab = load_slab(w, 1024, 512)
        rows_proj(slab, lambda k, b: HT[:, k, b * 128:(b + 1) * 128], range(2), 512,
                  lambda b, ps, t: copy_out(v_[:, b, :], ps, t), *t_h)
        slab = load_slab(w, 1536, 512)
        cols_proj(slab, [(c, c * 128, 128) for c in range(4)], hT, 256, lambda c, ps, t: copy_out(uT[:, c, :], ps, t), *t_h)
        t_p = (V.last(), S.last())
        for h in range(8):
            s, ps, readers = PS.take()
            e = PE.free(*t_p, *readers)
            for sbk in range(2):
                mm = e.matmul(ps[:, sbk * 256:(sbk + 1) * 256], k_[:, h, sbk * 128:(sbk + 1) * 128], q_[:, h, :],
                              start=True, stop=True)
            t = PE.done(mm)
            t = S.done(S.free(t).activation(ZZ[:, h, :], ps, ACT.Copy, scale=0.125))
            PS.release(s, t)
        nn, ll, zz = BIG[:, 8192:12288], BIG[:, 4096:8192], BIG[:, 0:4096]
        S.done(S.at().activation(nn, zz, ACT.Abs))
        S.done(S.at().activation(nn, nn, ACT.Exp, scale=-1.0))
        t_n = S.done(S.at().activation(nn, nn, ACT.Ln, bias=1.0))
        V.done(V.at(t_n).scalar_tensor_tensor(ll, zz, 0.0, nn, ALU.min, ALU.subtract))
        V.done(V.at().tensor_tensor(nn, ll, zz, ALU.subtract))
        m8 = SC[:, 128:640].unsqueeze(1).to_broadcast([128, 8, 512])
        t_n = V.done(V.at(t_m).tensor_tensor(NN, NN, m8, ALU.mult))
        for h in range(8):
            s, ps, readers = PS.take()
            PE.free(t_n, *readers)
            nh = NN[:, h, :]
            group(ps[:, 0:256], [(strict, nh[:, 0:256]), (ones[:, :], nh[:, 256:512])])
            t = group(ps[:, 256:512], [(strict, nh[:, 256:512])])
            t = V.done(V.free(t).tensor_tensor(LL[:, h, :], LL[:, h, :], ps, ALU.add))
            PS.release(s, t)
        t = S.done(S.at(t).activation(ll, ll, ACT.Exp))
        t_w = V.done(V.at(t).tensor_tensor(LL, LL, m8, ALU.mult))
        AO = q_
        for h in range(8):
            s, ps, readers = PS.take()
            PE.free(t_w, *readers)
            t = group(ps[0:64, 0:256], [(v_[:, b, h * 64:(h + 1) * 64], LL[:, h, b * 256:(b + 1) * 256])
                                        for b in range(2)])
            PS.release(s, S.done(S.free(t).activation(AO[:, h, :], ps[0:64, 0:256], ACT.Copy)))
        barrier()

        c_ = sb("s5c", [128, 14, 16])
        cl = [c_[:, i, :] for i in range(14)]
        t_l = [load_once(cl[0], A["ldt"], *everyone()), load_once(cl[1], A["lre"]), load_once(cl[2], A["lim"])]
        dT = sb("s5d", [128, 4])
        bglu = sb("bglu", [128, 4])
        t_d = load_once(dT[:, :], A["s5dT"])
        t_bg = load_once(bglu[:, :], A["bgluT"])

        def vt(o, a, b, op):
            return V.done(V.at().tensor_tensor(o, a, b, op))

        def vs(o, a, s1, s2, o1, o2=None):
            if o2 is None:
                return V.done(V.at().tensor_scalar(o, a, s1, None, o1))
            return V.done(V.at().tensor_scalar(o, a, s1, s2, o1, o2))

        dt, lr, li, ar, ai, cr, ci, den, x0, x1, x2, x3 = cl[0:12]
        t = S.done(S.at(*t_l).activation(dt, dt, ACT.Exp))
        V.free(t)
        t = vt(x0, lr, dt, ALU.mult)
        t = S.done(S.at(t).activation(x0, x0, ACT.Exp))
        V.free(t)
        vt(x1, li, dt, ALU.mult)
        vs(x2, x1, 1.0 / TWO_PI, 12582912.0, ALU.mult, ALU.add)
        vs(x2, x2, -12582912.0, None, ALU.add)
        for c in (6.28125, 0.0019350051879882812, 3.0199159819567e-07):
            V.done(V.at().scalar_tensor_tensor(x1, x2, -c, x1, ALU.mult, ALU.add))
        vs(x1, x1, PI - 1e-6, -(PI - 1e-6), ALU.min, ALU.max)
        t = V.last()
        t = S.done(S.at(t).activation(x2, x1, ACT.Abs))
        V.free(t)
        t = vs(x2, x2, -1.0, PI / 2, ALU.mult, ALU.add)
        S.done(S.at(t).activation(x2, x2, ACT.Sin))
        t = S.done(S.at().activation(x1, x1, ACT.Sin))
        V.free(t)
        vt(ar, x0, x2, ALU.mult)
        vt(ai, x0, x1, ALU.mult)
        vt(x0, lr, lr, ALU.mult)
        vt(x1, li, li, ALU.mult)
        vt(den, x0, x1, ALU.add)
        V.done(V.at().reciprocal(den, den))
        vs(x3, ar, -1.0, None, ALU.add)
        vt(x0, x3, lr, ALU.mult)
        vt(x1, ai, li, ALU.mult)
        vt(x0, x0, x1, ALU.add)
        vt(cr, x0, den, ALU.mult)
        vt(x0, ai, lr, ALU.mult)
        vt(x1, x3, li, ALU.mult)
        vt(x0, x0, x1, ALU.subtract)
        t_co = vt(ci, x0, den, ALU.mult)

        XR = BIG[:, 0:4096].rearrange("p (j t) -> p j t", j=16)
        XI = BIG[:, 4096:8192].rearrange("p (j t) -> p j t", j=16)
        t1 = BIG[:, 8192:8448]
        t2 = BIG[:, 8448:8704]
        wb = [load_w(A["s5_br"]), load_w(A["s5_bi"])]
        for j in range(16):
            s, ps, readers = PS.take()
            PE.free(*readers)
            for i in range(2):
                t = group(ps[:, i * 256:(i + 1) * 256], [(wb[i][1][:, j, :], uT[:, j // 4, :])], wb[i][2])
            P, Q = ps[:, 0:256], ps[:, 256:512]
            V.done(V.at(t).tensor_scalar(t1, Q, ci[:, j:j + 1], None, ALU.mult))
            V.done(V.at().scalar_tensor_tensor(XR[:, j, :], P, cr[:, j:j + 1], t1, ALU.mult, ALU.subtract))
            V.done(V.at().tensor_scalar(t2, P, ci[:, j:j + 1], None, ALU.mult))
            t = V.done(V.at().scalar_tensor_tensor(XI[:, j, :], Q, cr[:, j:j + 1], t2, ALU.mult, ALU.add))
            PS.release(s, t)
        release_w(wb, PE.last())
        XR4 = BIG[:, 0:4096].rearrange("p (j c t) -> p j c t", j=16, c=16)
        XI4 = BIG[:, 4096:8192].rearrange("p (j c t) -> p j c t", j=16, c=16)
        PW = BIG[:, 8704:9216].rearrange("p (i t j) -> p i t j", i=2, t=16)
        V.done(V.at().tensor_copy(PW[:, 0, 0, :], ar))
        V.done(V.at().tensor_copy(PW[:, 1, 0, :], ai))
        for n in range(1, 16):
            pr, pi = PW[:, 0, n - 1, :], PW[:, 1, n - 1, :]
            vt(x0, pr, ar, ALU.mult)
            vt(x1, pi, ai, ALU.mult)
            vt(PW[:, 0, n, :], x0, x1, ALU.subtract)
            vt(x0, pr, ai, ALU.mult)
            vt(x1, pi, ar, ALU.mult)
            vt(PW[:, 1, n, :], x0, x1, ALU.add)

        def cmadd(dr, di, pr, pi, sr, si, u1, u2):
            vt(u1, sr, pr, ALU.mult)
            vt(u2, si, pi, ALU.mult)
            vt(u1, u1, u2, ALU.subtract)
            vt(u2, sr, pi, ALU.mult)
            vt(dr, dr, u1, ALU.add)
            vt(u1, si, pr, ALU.mult)
            vt(u2, u2, u1, ALU.add)
            return vt(di, di, u2, ALU.add)

        u1 = t1.rearrange("p (j c) -> p j c", j=16)
        u2 = t2.rearrange("p (j c) -> p j c", j=16)
        bc = lambda ap, n: ap.unsqueeze(2).to_broadcast([128, 16, n])
        for n in range(1, 16):
            cmadd(XR4[:, :, :, n], XI4[:, :, :, n], bc(ar, 16), bc(ai, 16), XR4[:, :, :, n - 1], XI4[:, :, :, n - 1], u1, u2)
        for c in range(1, 16):
            cmadd(XR4[:, :, c, 15], XI4[:, :, c, 15], PW[:, 0, 15, :], PW[:, 1, 15, :], XR4[:, :, c - 1, 15],
                  XI4[:, :, c - 1, 15], x0, x1)
        for n in range(15):
            t = cmadd(XR4[:, :, 1:16, n], XI4[:, :, 1:16, n], bc(PW[:, 0, n, :], 15), bc(PW[:, 1, n, :], 15),
                      XR4[:, :, 0:15, 15], XI4[:, :, 0:15, 15], u1[:, :, 0:15], u2[:, :, 0:15])
        t_x = t
        wc = [load_w(A["s5_cr"]), load_w(A["s5_ci"])]
        for c in range(4):
            s, ps, readers = PS.take()
            PE.free(t_x, *readers)
            for i, xx in enumerate((XR, XI)):
                t = group(ps[:, i * 256:(i + 1) * 256],
                          [(wc[i][1][:, 4 * c + m, :], xx[:, 4 * c + m, :]) for m in range(4)], wc[i][2])
            V.done(V.at(t, t_d).scalar_tensor_tensor(yT[:, c, :], uT[:, c, :], dT[:, c:c + 1], ps[:, 0:256],
                                                     ALU.mult, ALU.add))
            t = V.done(V.at().tensor_tensor(yT[:, c, :], yT[:, c, :], ps[:, 256:512], ALU.subtract))
            PS.release(s, t)
        release_w(wc, PE.last())
        t_y = S.done(S.at(t).activation(H[:, 2, :], H[:, 2, :], ACT.Gelu_apprx_tanh))
        slab = load_slab(A["ssm_w_glu_2"][0], 0, 512, kts=4)

        def evac(c, ps, t):
            return S.done(S.free(t, t_bg).activation(zT[:, c, :], ps, ACT.Sigmoid, bias=bglu[:, c:c + 1]))

        cols_proj(slab, [(c, c * 128, 128) for c in range(4)], lambda k: yT[:, k, :], 256, evac, t_y)
        t_z = V.done(V.at(S.last(), PE.last()).tensor_tensor(H[:, 2, :], H[:, 2, :], H[:, 3, :], ALU.mult))
        wo = A["sb_ssm_w_out_2"][0]
        for n in range(2):
            s0 = load_slab(wo[0:512, :], n * 512, 512, p=64, kts=8)
            s1 = load_slab(wo[512:1024, :], n * 512, 512, kts=4)
            for b in range(2):
                s, ps, readers = PS.take()
                bl = slice(b * 128, (b + 1) * 128)
                t = group(ps, [(AO[:, k, bl], s0[k // 4][1][:, k % 4, :], s0[k // 4][2]) for k in range(8)]
                          + [(yT[:, k, bl], s1[0][1][:, k, :], s1[0][2]) for k in range(4)], t_z, *readers)
                PS.release(s, residual(b, n * 512, ps, t))
            release_w(s0 + s1, PE.last())
        layer_norm([(X[:, b, :], X[:, b, :]) for b in range(2)], A["ln_mix_g_2"][0], A["ln_mix_b_2"][0])

    def mlp(l):
        barrier()
        t_h = to_HT(X, range(2))
        F = BIG[:, 0:8192].rearrange("p (f t) -> p f t", f=32)
        RL = Ring([BIG[:, 8192 + 256 * i:8448 + 256 * i] for i in range(4)], [None] * 4)
        for n in range(8):
            slab = load_slab(A["mlp_w1_2"][l], n * 512, 512)

            def evac(f, ps, t):
                sr, rl, rr = RL.take()
                t = S.done(S.free(t, *rr).activation(rl, ps, ACT.Relu))
                t2 = V.done(V.free(t).tensor_tensor(F[:, f, :], rl, rl, ALU.mult))
                RL.release(sr, t2)
                return t

            cols_proj(slab, [(4 * n + j, j * 128, 128) for j in range(4)], lambda k: HT[:, k, 0:256], 256, evac, *t_h)
        t_f = V.last()
        w2 = A["mlp_w2_2"][l].rearrange("(k p) n -> p k n", p=128)
        acc = []
        for b in range(2):
            so, po, readers = PO.take()
            PE.free(*readers)
            acc.append((so, po))
        for k in range(0, 32, 2):
            ws, wv, wt = load_w(w2[:, k:k + 2, :])
            e = PE.free(t_f, wt)
            for kk in range(2):
                for b in range(2):
                    for n in range(2):
                        mm = e.matmul(acc[b][1][:, n, :], F[:, k + kk, b * 128:(b + 1) * 128],
                                      wv[:, kk, n * 512:(n + 1) * 512], start=(k + kk == 0), stop=(k + kk == 31))
            t = PE.done(mm)
            WR.release(ws, t)
        for b in range(2):
            for n in range(2):
                t2 = residual(b, n * 512, acc[b][1][:, n, :], t)
            PO.release(acc[b][0], t2)
        layer_norm([(X[:, b, :], X[:, b, :]) for b in range(2)], A["ln_ffn_g_2"][l], A["ln_ffn_b_2"][l])

    def dsa():
        barrier()
        t_h = to_HT(X, range(2))
        q_ = BIG[0:64, 0:4096].rearrange("p (h t) -> p h t", h=16)
        k_ = BIG[0:64, 4096:5120].rearrange("p (h t) -> p h t", h=4)
        qi = BIG[0:32, 5120:7168].rearrange("p (h t) -> p h t", h=8)
        ki = BIG[0:32, 7168:7424]
        v_ = BIG[:, 7424:7936].rearrange("p (b n) -> p b n", b=2)
        wi = BIG[:, 7936:7952].rearrange("p (b n) -> p b n", b=2)
        score = BIG[:, 8192:8704]
        work = BIG[:, 8704:9216]
        nd = BIG[:, 9216:9728]
        mn = BIG[:, 9728:10240]
        RL = Ring([BIG[:, 10240 + 256 * i:10496 + 256 * i] for i in range(2)], [None] * 2)
        LG = Ring([BIG[:, 10752 + 512 * i:11264 + 512 * i] for i in range(2)], [None] * 2)
        PT = Ring([BIG[:, 11776 + 256 * i:12032 + 256 * i] for i in range(0, 0)], [])
        ptb = H[:, 2:4, :].rearrange("p b n -> p (b n)")
        PT = Ring([ptb[:, i * 512:(i + 1) * 512] for i in range(4)], [None] * 4)
        OT = BIG[0:64, 12288:16384].rearrange("p (h t) -> p h t", h=16)
        m8 = BIG[:, 11776:11784]
        nm = BIG[:, 11784:11848]
        t_nd = G.done(G.at().iota(nd.rearrange("p (b s) -> p b s", b=2), pattern=[[-128, 2], [1, 256]], base=0,
                                  channel_multiplier=-1, allow_small_or_imprecise_dtypes=True))
        w = A["dsa_w_in_2"][0]
        hT = lambda k: HT[:, k, 0:256]
        rows = lambda k, b: HT[:, k, b * 128:(b + 1) * 128]

        def to(dst):
            return lambda name, ps, t: copy_out(dst(name), ps, t)

        wv = w.rearrange("(k p) n -> p k n", p=128)
        slab = [load_w(wv[:, k:k + 4, 1536:1832]) for k in (0, 4)]
        cols_proj(slab, [(h, h * 32, 32) for h in range(8)], hT, 256, to(lambda h: qi[:, h, :]), *t_h)
        cols_proj(slab, [(0, 256, 32)], hT, 256, to(lambda h: ki), *t_h)
        for b in range(2):
            s, ps, readers = PS.take()
            t = group(ps[:, 0:8], [(rows(k, b), slab[k // 4][1][:, k % 4, 288:296]) for k in range(8)], *readers)
            PS.release(s, copy_out(wi[:, b, :], ps[:, 0:8], t))
        release_w(slab, PE.last())
        t_i = (V.last(), S.last())
        for b in range(2):
            sc = score[:, b * 256:(b + 1) * 256]
            for h in range(8):
                s, ps, readers = PS.take()
                t = group(ps[:, 0:256], [(qi[:, h, b * 128:(b + 1) * 128], ki)], *t_i, *readers)
                sr, rl, rr = RL.take()
                t = S.done(S.free(t, *rr).activation(rl, ps[:, 0:256], ACT.Relu))
                PS.release(s, t)
                if h == 0:
                    t = V.done(V.at(t, *t_i).tensor_scalar(sc, rl, wi[:, b, h:h + 1], None, ALU.mult))
                else:
                    t = V.done(V.at(t).scalar_tensor_tensor(sc, rl, wi[:, b, h:h + 1], sc, ALU.mult, ALU.add))
                RL.release(sr, t)
        slab = load_slab(w, 1024, 512)
        cols_proj(slab, [(h, h * 64, 64) for h in range(4)], hT, 256, to(lambda h: k_[:, h, :]), *t_h)
        for b in range(2):
            s, ps, readers = PS.take()
            t = group(ps[:, 0:256], [(rows(k, b), slab[k // 4][1][:, k % 4, 256:512]) for k in range(8)], *readers)
            PS.release(s, copy_out(v_[:, b, :], ps[:, 0:256], t))
        release_w(slab, PE.last())
        for n in range(2):
            slab = load_slab(w, n * 512, 512)
            cols_proj(slab, [(8 * n + h, h * 64, 64) for h in range(8)], hT, 256, to(lambda h: q_[:, h, :]), *t_h)
        t_p = (V.last(), S.last())
        t = V.done(V.at().tensor_scalar(score, score, (32.0 ** -0.5) * (8.0 ** -0.5), None, ALU.mult))
        s3 = score.rearrange("p (b s) -> p b s", b=2)
        t = G.done(G.at(t).affine_select(out=s3, in_=s3, compare_op=ALU.is_ge, fill=-1.0e38, base=0,
                                         pattern=[[128, 2], [-1, 256]], channel_multiplier=1))
        V.free(t)
        for b in range(2):
            sc = score[:, b * 256:(b + 1) * 256]
            for r in range(8):
                V.done(V.at().max(m8, sc))
                V.done(V.at().match_replace(sc, m8, sc, NEG))
        V.done(V.at().tensor_scalar(mn, score, -2.0e38, -1.0e30, ALU.is_gt, ALU.mult))
        t = V.last()
        m3 = mn.rearrange("p (b s) -> p b s", b=2)
        t_mn = G.done(G.at(t).affine_select(out=m3, in_=m3, compare_op=ALU.is_ge, fill=-1.0e30, base=0,
                                            pattern=[[128, 2], [-1, 256]], channel_multiplier=1))
        for h in range(16):
            slope = 2.0 ** (-8.0 * (h + 1) / 16)
            s, ps, readers = PS.take()
            PE.free(*t_p, *readers)
            for b in range(2):
                t = group(ps[:, b * 256:(b + 1) * 256], [(q_[:, h, b * 128:(b + 1) * 128], k_[:, h // 4, :])])
            sl, lg, lr_ = LG.take()
            V.done(V.at(t_mn, t_nd, *lr_).scalar_tensor_tensor(lg, nd, slope, mn, ALU.mult, ALU.add))
            t = V.done(V.at(t).scalar_tensor_tensor(lg, ps, 0.125, lg, ALU.mult, ALU.add))
            PS.release(s, t)
            c = nm[:, 2 * h:2 * h + 2]
            z = nm[:, 32 + 2 * h:34 + 2 * h]
            lg3 = lg.rearrange("p (b s) -> p b s", b=2)
            t = V.done(V.at().tensor_reduce(c, lg3, AX, ALU.max, negate=True))
            for b in range(2):
                t = S.done(S.at(t).activation(lg3[:, b, :], lg3[:, b, :], ACT.Exp, bias=c[:, b:b + 1],
                                              accum_out=z[:, b:b + 1]))
            V.done(V.at(t).reciprocal(z, z))
            t = V.done(V.at().tensor_tensor(lg3, lg3, z.unsqueeze(2).to_broadcast([128, 2, 256]), ALU.mult))
            s, ps, readers = PS.take()
            e = PE.free(t, *readers)
            for b in range(2):
                for sk in range(2):
                    mm = e.transpose(ps[:, sk * 256 + b * 128:sk * 256 + b * 128 + 128],
                                     lg[:, b * 256 + sk * 128:b * 256 + sk * 128 + 128], ident[:, :])
            t = PE.done(mm)
            LG.release(sl, t)
            sp_, pt, pr_ = PT.take()
            t = S.done(S.free(t, *pr_).activation(pt, ps, ACT.Copy))
            PS.release(s, t)
            s, ps, readers = PS.take()
            kv = h // 4
            t = group(ps[0:64, 0:256], [(v_[:, sk, kv * 64:(kv + 1) * 64], pt[:, sk * 256:(sk + 1) * 256])
                                        for sk in range(2)], t, *readers)
            PT.release(sp_, t)
            PS.release(s, S.done(S.free(t).activation(OT[:, h, :], ps[0:64, 0:256], ACT.Copy)))
        t_o = S.last()
        wo = A["dsa_w_out_2"][0]
        for n in range(2):
            slab = load_slab(wo, n * 512, 512, p=64, kts=16)
            rows_proj(slab, lambda k, b: OT[:, k, b * 128:(b + 1) * 128], range(2), 512,
                      lambda b, ps, t: residual(b, n * 512, ps, t), t_o)
        layer_norm([(X[:, b, :], X[:, b, :]) for b in range(2)], A["ln_mix_g_2"][1], A["ln_mix_b_2"][1])

    V.free(*t_x)
    PE.free(*t_x)
    t_silu = ()
    if "mod0" in parts or "mod1" in parts:
        t = S.done(S.at(t_sc).activation(scS[:, :, :], scT[:, :, :], ACT.Sigmoid))
        t_silu = (V.done(V.at(t).tensor_tensor(scS[:, :, :], scS[:, :, :], scT[:, :, :], ALU.mult)),)
    if "mod0" in parts:
        modulation(0)
    if "mix0" in parts:
        chunk_mlp()
    if "peer0" in parts:
        peer(0, [0, 1, 2, 3])
    if "mod1" in parts:
        modulation(1)
    if "mix1" in parts:
        gla()
    if "peer1" in parts:
        peer(1, [0, 1])
    if "sb" in parts:
        sb_ssm()
    if "mlp0" in parts:
        mlp(0)
    if "dsa" in parts:
        dsa()
    if "mlp1" in parts:
        mlp(1)
    s_out = sem("s_out")
    D.free(V.last()).dma_start(out[0].rearrange("(b p) d -> p b d", p=128), X[:, 0:2, :]).then_inc(s_out, 16)
    nc.sync.wait_ge(s_out, 16)
    for i in range(2):
        if ms_count[i]:
            nc.sync.wait_ge(s_ms[i], ms_count[i])
    ctx.close()


_OUTS = [((1, 256, 1024), 'float32')]


def layout(inputs):
    import numpy as np

    def c(a):
        return np.ascontiguousarray(a)

    a = {k: np.asarray(v) for k, v in inputs.items()}
    o = {}
    for k in ("x", "ctx", "w_mod", "b_mod", "ln_g", "ln_b", "a_w_in", "a_norm_g", "a_norm_b", "a_w_out", "b_w_in",
              "b_w_gate", "b_gate_bias", "b_gn_g", "b_w_out", "p_w_q", "sb_ssm_w_in_2", "ssm_w_glu_2",
              "sb_ssm_w_out_2", "dsa_w_in_2", "dsa_w_out_2", "ln_mix_g_2", "ln_mix_b_2", "ln_ffn_g_2", "ln_ffn_b_2",
              "mlp_w1_2", "mlp_w2_2"):
        o[k] = c(a[k])
    o["p_u"] = c(a["p_u"].reshape(32768, 1024))
    o["p_v"] = c(a["p_v"].reshape(32768, 1024))
    cc = np.stack([a["c"][0], a["c_ctx"]])
    o["cT"] = c(cc.reshape(2, 8, 128).transpose(2, 1, 0))
    o["a_b_sT"] = c(a["a_b_s"][0].T)
    o["a_w_sT"] = c(a["a_w_s"][0].transpose(2, 0, 1))
    o["keysT"] = c(a["p_keys"].transpose(0, 1, 3, 2))
    o["ldt"] = c(np.repeat(a["ssm_log_dt_2"][0], 64).reshape(16, 128).T)
    o["lre"] = c(a["ssm_lam_re_2"][0].reshape(16, 128).T)
    o["lim"] = c(a["ssm_lam_im_2"][0].reshape(16, 128).T)
    o["s5dT"] = c(a["ssm_d_2"][0].reshape(4, 128).T)
    o["bgluT"] = c(a["ssm_b_glu_2"][0].reshape(4, 128).T)
    for name, key in (("s5_br", "ssm_b_re_2"), ("s5_bi", "ssm_b_im_2")):
        w = np.zeros((128, 16, 128), np.float32)
        for g in range(32):
            w[(g % 8) * 16:(g % 8) * 16 + 16, g // 2, (g % 2) * 64:(g % 2) * 64 + 64] = a[key][0, g].T
        o[name] = w
    for name, key in (("s5_cr", "ssm_c_re_2"), ("s5_ci", "ssm_c_im_2")):
        w = np.zeros((128, 16, 128), np.float32)
        for g in range(32):
            w[(g % 2) * 64:(g % 2) * 64 + 64, g // 2, (g % 8) * 16:(g % 8) * 16 + 16] = a[key][0, g].T
        o[name] = w
    return o


def kernel(**inputs):
    import numpy as _np
    import concourse.bacc as _bacc
    from concourse import mybir as _mybir
    from concourse.bass_utils import run_bass_kernel_spmd as _run

    nc = _bacc.Bacc("TRN2", target_bir_lowering=False, num_devices=1)
    arrays, args = {}, {}
    for name, a in layout(inputs).items():
        arrays[f"in_{name}_dram"] = a
        args[name] = nc.dram_tensor(f"in_{name}_dram", a.shape, _mybir.dt.from_np(a.dtype), kind="ExternalInput").ap()
    shape, dtype = _OUTS[0]
    out = nc.dram_tensor("out_0_dram", shape, _mybir.dt.from_np(_np.dtype(dtype)), kind="ExternalOutput").ap()
    program(nc, args, out)
    r = _run(nc, [arrays], core_ids=[0])
    return r.results[0]["out_0_dram"]
```

```python
from contextlib import ExitStack

import concourse.bass as bass
from concourse import mybir

F32 = mybir.dt.float32
I32 = mybir.dt.int32
U32 = mybir.dt.uint32
ALU = mybir.AluOpType
ACT = mybir.ActivationFunctionType
AX = mybir.AxisListType.X

EPS = 1e-5
ALPHA = 4.0 ** 0.25
NEG = -3.0e38
TWO_PI = 6.283185307179586
PI = 3.141592653589793




class Engine:

    def __init__(self, eng, sem):
        self.eng, self.sem, self.n, self.seen = eng, sem, 0, {}

    def free(self, *tokens):
        for sem, value in tokens:
            if self.seen.get(sem, 0) < value:
                self.eng.wait_ge(sem, value)
                self.seen[sem] = value
        return self.eng

    def at(self, *tokens):
        return self.free(*tokens, (self.sem, self.n))

    def done(self, ins):
        ins.then_inc(self.sem, 1)
        self.n += 1
        return (self.sem, self.n)

    def last(self):
        return (self.sem, self.n)


def in_turn(*works):
    works = list(works)
    while works:
        for w in list(works):
            if next(w, 0) == 0:
                works.remove(w)


class Ring:

    def __init__(self, views, sems):
        self.views, self.sems = views, sems
        self.n = len(views)
        self.turn = 0
        self.count = [0] * self.n
        self.readers = [()] * self.n

    def take(self):
        s = self.turn
        self.turn = (s + 1) % self.n
        assert self.readers[s] is not None
        r, self.readers[s] = self.readers[s], None
        return s, self.views[s], r

    def loaded(self, s, ins):
        ins.then_inc(self.sems[s], 16)
        self.count[s] += 16
        return (self.sems[s], self.count[s])

    def release(self, s, *tokens):
        self.readers[s] = tokens


def program(nc, A, out, parts=("mod0", "mix0", "peer0", "mod1", "mix1", "peer1", "sb", "mlp0", "dsa", "mlp1")):
    ctx = ExitStack()

    def sb(name, shape, dt=F32):
        return ctx.enter_context(nc.sbuf_tensor(name, shape, dt))

    def sem(name):
        return ctx.enter_context(nc.semaphore(name))

    PE = Engine(nc.tensor, sem("s_pe"))
    V = Engine(nc.vector, sem("s_v"))
    S = Engine(nc.scalar, sem("s_act"))
    G = Engine(nc.gpsimd, sem("s_pool"))
    D = Engine(nc.sync, sem("s_sp"))


    X = sb("X", [128, 4, 1024])
    H = sb("H", [128, 4, 1024])
    HT = sb("HT", [128, 8, 512])
    BIG = sb("BIG", [128, 16384])
    WRt = sb("WR", [128, 5, 2048])
    BCt = sb("BC", [128, 5, 1024])
    NG = 12
    GRt = BIG[:, 0:NG * 1024].rearrange("p (s n) -> p s n", s=NG)
    QT = BIG[:, NG * 1024:16384].rearrange("p (b h t) -> p b h t", b=4, h=8)

    PSt = ctx.enter_context(nc.psum_tensor("PS", [128, 8, 512], F32))
    PS = Ring([PSt[:, i, :] for i in range(4)], [None] * 4)
    PO = Ring([PSt[:, 4 + 2 * i:6 + 2 * i, :] for i in range(2)], [None] * 2)
    WR = Ring([WRt[:, i, :] for i in range(5)], [sem(f"s_w{i}") for i in range(5)])
    BC = Ring([BCt[:, i, :] for i in range(5)], [sem(f"s_b{i}") for i in range(5)])
    GR = Ring([GRt[:, i, :] for i in range(NG)], [sem(f"s_g{i}") for i in range(NG)])

    ident = sb("ident", [128, 128])
    ones = sb("ones", [128, 128])
    iota16 = sb("iota16", [128, 16])
    kbd = sb("kbd", [128, 256])
    stat = sb("stat", [128, 4, 12])
    mv = sb("mv", [128, 4, 2])
    sd = sb("sd", [128, 4])
    rs = sb("rs", [128, 4])
    tmp = sb("tmp", [128, 512])
    scT = sb("scT", [128, 8, 2])
    scS = sb("scS", [128, 8, 2])
    mrow = sb("mrow", [2, 2, 512])
    MR = Ring([mrow[:, i, :] for i in range(2)], [sem(f"s_m{i}") for i in range(2)])
    s_ms = [sem(f"s_ms{i}") for i in range(2)]
    ms_count = [0, 0]
    BRt = sb("BR", [128, 1024])
    BR = Ring([BRt[32 * i:32 * i + 1, :] for i in range(4)], [sem(f"s_r{i}") for i in range(4)])
    one_loads = [0]
    DG = Ring([sb(f"dg{i}", [128, 128]) for i in range(3)], [None] * 3)

    V16 = sb("V16", [128, 2, 16])
    I16 = sb("I16", [128, 2, 16], U32)
    I16f = sb("I16f", [128, 2, 16])
    T16 = sb("T16", [128, 16])
    P16 = sb("P16", [128, 16], U32)
    AB = sb("AB", [128, 2, 16], U32)
    ABf = sb("ABf", [128, 2, 16])
    SCU = sb("SCU", [128, 2, 256])
    OH = sb("OH", [128, 2, 16, 16])
    sums = sb("sums", [128, 2])
    IDX = sb("IDX", [128, 4, 16], I32)
    WT = sb("WT", [128, 4, 16])
    ACTV = sb("ACTV", [128, 4, 16])
    small = sb("small", [128, 8])
    SC = sb("SC", [128, 2048])
    cand = sb("cand", [128, 256])

    modd = nc.dram_tensor("modd", (2, 2, 6144), F32, kind="Internal").ap()

    def load_once(dst, src, *tokens, by=None):
        s = sem(f"s_one{one_loads[0]}")
        one_loads[0] += 1
        (by or D).free(*tokens).dma_start(dst, src).then_inc(s, 16)
        return (s, 16)

    def everyone():
        return (PE.last(), V.last(), S.last(), G.last())

    def barrier():
        t = everyone()
        for e in (PE, V, S, G):
            e.free(*t)
        return t

    def load_bc(row, *tokens):
        s, view, readers = BC.take()
        t = BC.loaded(s, D.free(*readers, *tokens).dma_start(view, row.partition_broadcast(128)))
        return s, view, t

    def spread_bc(row, *tokens):
        r, line, readers = BR.take()
        t_r = BR.loaded(r, D.free(*readers, *tokens).dma_start(line, row.unsqueeze(0)))
        s, view, readers = BC.take()
        for n in range(2):
            p, ps, pr = PS.take()
            t = PE.done(PE.free(t_r, *pr).matmul(ps, ones[32 * r:32 * r + 1, :], line[:, n * 512:(n + 1) * 512],
                                                 start=True, stop=True))
            t = S.done(S.free(t, *readers).activation(view[:, n * 512:(n + 1) * 512], ps, ACT.Copy))
            PS.release(p, t)
        BR.release(r, PE.last())
        return s, view, t

    def load_w(src, p=128):
        s, view, readers = WR.take()
        _, a, b = src.shape
        view = view[0:p, 0:a * b].rearrange("p (a b) -> p a b", a=a)
        t = WR.loaded(s, D.free(*readers).dma_start(view, src))
        return s, view, t

    def load_slab(w, n0, n, p=128, kts=8):
        wv = w.rearrange("(k p) n -> p k n", p=p)
        return [load_w(wv[:, k:k + 4, n0:n0 + n], p) for k in range(0, kts, 4)]

    def group(dst, pairs, *tokens):
        e = PE.free(*tokens)
        last = len(pairs) - 1
        for j, (lhs, rhs, *tk) in enumerate(pairs):
            PE.free(*tk)
            mm = e.matmul(dst, lhs, rhs, start=(j == 0), stop=(j == last))
        return PE.done(mm)

    def release_w(slots, t):
        for s, _, _ in slots:
            WR.release(s, t)

    def rows_proj(slab, lhs, blks, n, evac, *tokens):
        for b in blks:
            s, ps, readers = PS.take()
            t = group(ps[:, 0:n], [(lhs(k, b), slab[k // 4][1][:, k % 4, 0:n], slab[k // 4][2])
                                   for k in range(4 * len(slab))], *readers, *tokens)
            PS.release(s, evac(b, ps[:, 0:n], t))
        release_w(slab, t)

    def cols_proj(slab, cols, rhs, n, evac, *tokens):
        for name, c0, m in cols:
            s, ps, readers = PS.take()
            t = group(ps[0:m, 0:n], [(slab[k // 4][1][:, k % 4, c0:c0 + m], rhs(k), slab[k // 4][2])
                                     for k in range(4 * len(slab))], *readers, *tokens)
            PS.release(s, evac(name, ps[0:m, 0:n], t))
        release_w(slab, t)

    flip = [0]

    def copy_out(dst, src, t, *tokens):
        flip[0] ^= 1
        if flip[0]:
            return S.done(S.free(t, *tokens).activation(dst, src, ACT.Copy))
        return V.done(V.free(t, *tokens).tensor_copy(dst, src))

    def to_HT(src, blks, *tokens):
        done = []
        for b in blks:
            for g in range(2):
                s, ps, readers = PS.take()
                e = PE.free(*readers, *tokens)
                for j in range(4):
                    k = 4 * g + j
                    mm = e.transpose(ps[:, j * 128:(j + 1) * 128], src[:, b, k * 128:(k + 1) * 128], ident[:, :])
                t = PE.done(mm)
                t = copy_out(HT[:, 4 * g:4 * g + 4, b * 128:(b + 1) * 128],
                             ps.rearrange("p (a b) -> p a b", a=4), t)
                PS.release(s, t)
                done.append(t)
        return done

    def normalize(src, dst, i, n, *tokens):
        w = min(n, 512)
        for j in range(n // w):
            V.done(V.at(*tokens).bn_stats(stat[:, i, 6 * j:6 * j + 6], src[:, j * w:(j + 1) * w]))
        V.done(V.at().bn_aggr(mv[:, i, :], stat[:, i, 0:6 * (n // w)]))
        t = V.done(V.at().tensor_scalar(mv[:, i, 1:2], mv[:, i, 1:2], EPS, None, ALU.add))
        t = S.done(S.at(t).activation(sd[:, i:i + 1], mv[:, i, 1:2], ACT.Sqrt))
        V.done(V.at(t).reciprocal(rs[:, i:i + 1], sd[:, i:i + 1]))
        return V.done(V.at().tensor_scalar(dst, src, mv[:, i, 0:1], rs[:, i:i + 1], ALU.subtract, ALU.mult))

    def layer_norm(pairs, g_row, b_row, *tokens):
        sg, gv, tg = load_bc(g_row)
        sb_, bv, tb = load_bc(b_row)
        for i, (src, dst) in enumerate(pairs):
            normalize(src, dst, i % 4, 1024, *tokens)
            V.done(V.at(tg).tensor_tensor(dst, dst, gv, ALU.mult))
            t = V.done(V.at(tb).tensor_tensor(dst, dst, bv, ALU.add))
        BC.release(sg, t)
        BC.release(sb_, t)
        return t

    def residual(b, n0, ps, t, gate=None):
        xs = X[:, b, n0:n0 + 512]
        if gate is None:
            return V.done(V.at(t).scalar_tensor_tensor(xs, xs, ALPHA, ps, ALU.mult, ALU.add))
        view, tg = gate
        t = V.done(V.at(t, tg).tensor_tensor(tmp[:, :], ps, view[:, n0:n0 + 512], ALU.mult))
        return V.done(V.at(t).scalar_tensor_tensor(xs, xs, ALPHA, tmp[:, :], ALU.mult, ALU.add)), t

    streams = {0: 0, 1: 0, 2: 1, 3: 1}
    mod_done = {}

    def mod_row(l, j, st):
        return modd[l, st, j * 1024:(j + 1) * 1024]

    def modulated(l, j_shift, j_scale, blks, load=load_bc):
        for st in (1, 0):
            own = [b for b in blks if streams[b] == st]
            if not own:
                continue
            s1, sc_v, t1 = load(mod_row(l, j_scale, st), *mod_done[l, j_scale])
            s2, sh_v, t2 = load(mod_row(l, j_shift, st), *mod_done[l, j_shift])
            for b in own:
                V.done(V.at(t1).scalar_tensor_tensor(H[:, b, :], sc_v, 1.0, X[:, b, :], ALU.add, ALU.mult))
                t = V.done(V.at(t2).tensor_tensor(H[:, b, :], H[:, b, :], sh_v, ALU.add))
            BC.release(s1, t)
            BC.release(s2, t)
        return t

    t_x = []
    xv = A["x"][0].rearrange("(b p) d -> p b d", p=128)
    cv = A["ctx"][0].rearrange("(b p) d -> p b d", p=128)
    t_x.append(load_once(X[:, 0:2, :], xv))
    t_x.append(load_once(X[:, 2:4, :], cv))
    t_sc = load_once(scT[:, :, :], A["cT"])
    G.done(G.at().memset(ones[:, :], 1.0))
    t_ones = G.last()
    G.done(G.at().affine_select(out=ident[:, :], in_=ones[:, :], compare_op=ALU.is_equal, fill=0.0, base=0,
                                pattern=[[-1, 128]], channel_multiplier=1))
    G.done(G.at().iota(iota16[:, :], pattern=[[1, 16]], base=0, channel_multiplier=0,
                       allow_small_or_imprecise_dtypes=True))
    t_const = G.done(G.at().memset(kbd[:, :], 0.0))
    barrier()

    def modulation(l, first, slabs):
        w = A["w_mod"][l]
        for n in range(first, first + slabs):
            slab = load_slab(w, n * 512, 512)
            m, row, readers = MR.take()
            t_b = MR.loaded(m, D.free(*readers).dma_start(
                row, A["b_mod"][l, n * 512:(n + 1) * 512].partition_broadcast(2)))
            s, ps, readers = PS.take()
            e = PE.free(*readers, *t_silu)
            for k in range(8):
                PE.free(slab[k // 4][2])
                mm = e.matmul(ps[0:2, :], scS[:, k, :], slab[k // 4][1][:, k % 4, :], start=(k == 0), stop=(k == 7))
                if k == 3:
                    yield
            t = PE.done(mm)
            release_w(slab, t)
            t = V.done(V.at(t, t_b).tensor_tensor(row, row, ps[0:2, :], ALU.add))
            PS.release(s, t)
            S.free(t).dma_start(modd[l, :, n * 512:(n + 1) * 512], row).then_inc(s_ms[m], 16)
            ms_count[m] += 16
            MR.release(m, (s_ms[m], ms_count[m]))
            yield
        for j in range(first // 2, (first + slabs) // 2):
            mod_done[l, j] = ((s_ms[0], ms_count[0]), (s_ms[1], ms_count[1]))

    def chunk_mlp():
        blks = range(4)
        t = modulated(0, 0, 1, blks)
        t_h = to_HT(H, blks, t)
        U = BIG[:, 0:4096].rearrange("p (b n) -> p b n", b=4)
        Vv = BIG[:, 4096:8192].rearrange("p (b n) -> p b n", b=4)
        bs = small[:, 0:8]
        t_bs = load_once(bs, A["a_b_sT"])
        t_w = []
        for n in (2, 3, 0, 1):
            slab = load_slab(A["a_w_in"][0], n * 512, 512)
            dst = (U, Vv)[n // 2]

            def evac(b, ps, t):
                return S.done(S.free(t).activation(dst[:, b, (n % 2) * 512:(n % 2) * 512 + 512], ps,
                                                   ACT.Gelu_apprx_tanh))

            rows_proj(slab, lambda k, b: HT[:, k, b * 128:(b + 1) * 128], blks, 512, evac, *t_h)
        t_u = S.last()
        t_v = layer_norm([(Vv[:, b, :], Vv[:, b, :]) for b in blks], A["a_norm_g"][0], A["a_norm_b"][0], t_u)
        for _ in modulation(0, 4, 8):
            pass
        ws, wsv, wst = load_w(A["a_w_sT"])
        for b in blks:
            for hh in range(2):
                s, ps, readers = PS.take()
                e = PE.free(t_v, wst, *readers)
                for j in range(4):
                    h = 4 * hh + j
                    mm = e.matmul(ps[:, j * 128:(j + 1) * 128], wsv[:, h, :], Vv[:, b, h * 128:(h + 1) * 128],
                                  start=True, stop=True)
                t = PE.done(mm)
                for j in range(4):
                    h = 4 * hh + j
                    us = U[:, b, h * 128:(h + 1) * 128]
                    t2 = V.done(V.at(t, t_bs).scalar_tensor_tensor(us, ps[:, j * 128:(j + 1) * 128], bs[:, h:h + 1],
                                                                   us, ALU.add, ALU.mult))
                PS.release(s, t2)
        WR.release(ws, t)
        t_h = to_HT(U, blks, V.last(), PE.last())
        mixer_out(A["a_w_out"][0], 0, blks, t_h)

    def mixer_out(w, l, blks, t_h):
        gates = {}
        for st in sorted({streams[b] for b in blks}):
            gates[st] = load_bc(mod_row(l, 2, st), *mod_done[l, 2])
        for n in range(2):
            slab = load_slab(w, n * 512, 512)

            def evac(b, ps, t):
                _, view, tg = gates[streams[b]]
                return residual(b, n * 512, ps, t, (view, tg))[1]

            rows_proj(slab, lambda k, b: HT[:, k, b * 128:(b + 1) * 128], blks, 512, evac, *t_h)
        for s, _, _ in gates.values():
            BC.release(s, V.last())

    def peer(l, order, more=()):
        wq = [load_slab(A["p_w_q"][l], n * 512, 512) for n in range(2)]
        ready = {}
        t_q = {}
        units = [(b, h) for b in order for h in range(8)]
        used = [()] * 4

        def prepare(b):
            for r, op in ((A["ln_g"][l, 0], ALU.mult), (A["ln_b"][l, 0], ALU.add)):
                s, view, t = spread_bc(r)
                if op == ALU.mult:
                    normalize(X[:, b, :], X[:, b, :], 0, 1024)
                    yield
                BC.release(s, V.done(V.at(t).tensor_tensor(X[:, b, :], X[:, b, :], view, op)))
                yield
            t = modulated(l, 3, 4, [b], spread_bc)
            yield
            t_h = to_HT(H, [b], t)
            yield
            qrow = SC[:, 0:1024]
            t_sc = V.last()
            for n in range(2):
                s, ps, readers = PS.take()
                t = group(ps, [(HT[:, k, b * 128:(b + 1) * 128], wq[n][k // 4][1][:, k % 4, :], wq[n][k // 4][2])
                               for k in range(8)], *readers, *t_h)
                t = S.done(S.free(t, t_sc).activation(qrow[:, n * 512:(n + 1) * 512], ps, ACT.Copy))
                PS.release(s, t)
                yield
                s, ps, readers = PS.take()
                e = PE.free(t, *readers)
                for j in range(4):
                    h = 4 * n + j
                    mm = e.transpose(ps[:, j * 128:(j + 1) * 128], qrow[:, h * 128:(h + 1) * 128], ident[:, :])
                t = PE.done(mm)
                t = S.done(S.free(t).activation(QT[:, b, 4 * n:4 * n + 4, :], ps.rearrange("p (h t) -> p h t", h=4),
                                                ACT.Copy))
                PS.release(s, t)
                yield
            t_q[b] = t

        def route(u):
            b, h = units[u]
            i = u % 4
            sc = SCU[:, u % 2, :]
            s, ps, readers = PS.take()
            t = PE.done(PE.free(*t_k, t_q[b], *readers).matmul(ps[:, 0:256], QT[:, b, h, :], kbd[:, :],
                                                               start=True, stop=True))
            t = S.done(S.free(t, V.last()).activation(sc, ps[:, 0:256], ACT.Copy))
            PS.release(s, t)
            yield
            V.free(t)
            for r in range(2):
                scr = sc[:, r * 128:(r + 1) * 128]
                V.done(V.at().max(V16[:, r, 0:8], scr))
                V.done(V.at().max_index(I16[:, r, 0:8], V16[:, r, 0:8], scr))
                V.done(V.at().match_replace(scr, V16[:, r, 0:8], scr, NEG))
                yield
                V.done(V.at().max(V16[:, r, 8:16], scr))
                V.done(V.at().max_index(I16[:, r, 8:16], V16[:, r, 8:16], scr))
                yield
            V.done(V.at().tensor_copy(I16f[:, :, :], I16[:, :, :]))
            c3 = cand[:, :].rearrange("p (a b) -> p a b", a=16)
            V.done(V.at().tensor_tensor(c3, V16[:, 0, :].unsqueeze(2).to_broadcast([128, 16, 16]),
                                        V16[:, 1, :].unsqueeze(1).to_broadcast([128, 16, 16]), ALU.add))
            V.done(V.at().max(T16[:, 0:8], cand[:, :]))
            yield
            V.done(V.at().max_index(P16[:, 0:8], T16[:, 0:8], cand[:, :]))
            V.done(V.at().match_replace(cand[:, :], T16[:, 0:8], cand[:, :], NEG))
            yield
            V.done(V.at().max(T16[:, 8:16], cand[:, :]))
            V.done(V.at().max_index(P16[:, 8:16], T16[:, 8:16], cand[:, :]))
            yield
            V.done(V.at().tensor_scalar(AB[:, 0, :], P16[:, :], 4, None, ALU.logical_shift_right))
            V.done(V.at().tensor_scalar(AB[:, 1, :], P16[:, :], 15, None, ALU.bitwise_and))
            V.done(V.at().tensor_copy(ABf[:, :, :], AB[:, :, :]))
            yield
            V.done(V.at().tensor_tensor(OH[:, :, :, :], ABf[:, :, :].unsqueeze(3).to_broadcast([128, 2, 16, 16]),
                                        iota16[:, :].unsqueeze(1).unsqueeze(1).to_broadcast([128, 2, 16, 16]),
                                        ALU.is_equal))
            V.done(V.at().tensor_tensor(OH[:, :, :, :], OH[:, :, :, :],
                                        I16f[:, :, :].unsqueeze(2).to_broadcast([128, 2, 16, 16]), ALU.mult))
            yield
            V.done(V.at().tensor_reduce(ABf[:, :, :], OH[:, :, :, :], AX, ALU.add))
            V.done(V.at().tensor_scalar(ABf[:, 0, :], ABf[:, 0, :], 128.0, float(l * 16384), ALU.mult, ALU.add))
            t_idx = V.done(V.at(*used[i]).tensor_tensor(IDX[:, i, :], ABf[:, 0, :], ABf[:, 1, :], ALU.add))
            w = WT[:, i, :]
            t = V.done(V.at().tensor_scalar(w, T16[:, :], T16[:, 0:1], None, ALU.subtract))
            t = S.done(S.at(t).activation(w, w, ACT.Exp, accum_out=sums[:, 0:1]))
            ready[u] = t_idx
            yield
            V.done(V.at(t).reciprocal(sums[:, 1:2], sums[:, 0:1]))
            V.done(V.at().tensor_scalar(w, w, sums[:, 1:2], None, ALU.mult))

        def gather(table, u, j):
            s, view, readers = GR.take()
            e = G.free(*readers, ready[u])
            t = GR.loaded(s, e.indirect_dma_start(view, None, table, bass.IndirectOffsetOnAxis(
                ap=IDX[:, u % 4, j:j + 1], axis=0)))
            return s, view, t

        def prepare_rest():
            for b in order[1:]:
                yield from prepare(b)
            for slab in wq:
                release_w(slab, PE.last())

        def finish(b, po, t):
            sg, view, tgate = spread_bc(mod_row(l, 5, streams[b]), *mod_done[l, 5])
            for half in range(2):
                _, tp = residual(b, half * 512, po[1][:, half, :], t, (view, tgate))
            BC.release(sg, tp)
            PO.release(po[0], tp)
            yield
            normalize(X[:, b, :], X[:, b, :], 0, 1024)
            yield
            for r, op in ((A["ln_g"][l, 1], ALU.mult), (A["ln_b"][l, 1], ALU.add)):
                s, view, t = spread_bc(r)
                BC.release(s, V.done(V.at(t).tensor_tensor(X[:, b, :], X[:, b, :], view, op)))
                yield

        def others():
            for work in more:
                yield from work

        for _ in prepare(order[0]):
            pass
        t_k = [load_once(kbd[0:64, 0:128], A["keysT"][l, 0], PE.last(), by=S),
               load_once(kbd[64:128, 128:256], A["keysT"][l, 1], by=S)]
        for _ in route(0):
            pass
        G.free(*everyone())
        rest, extra, ends = prepare_rest(), others(), iter(())
        for u in range(len(units) + 1):
            if u == 6:
                for _ in rest:
                    pass
            nxt = route(u + 1) if u + 1 < len(units) else iter(())
            if u:
                b, h = units[u - 1]
                if h == 0:
                    po = PO.take()
                    PE.free(*po[2])
                av = ACTV[:, (u - 1) % 4, :]
                t = S.done(S.at(V.last()).activation(av, av, ACT.Gelu_apprx_tanh))
                t_a = V.done(V.at(t).tensor_tensor(av, av, WT[:, (u - 1) % 4, :], ALU.mult))
            for j in range(16):
                if u < len(units):
                    s, view, t = gather(A["p_u"], u, j)
                    t = V.done(V.free(t).tensor_tensor_reduce(view, view, H[:, units[u][0], :], 1.0, 0.0, ALU.mult,
                                                              ALU.add, ACTV[:, u % 4, j:j + 1]))
                    GR.release(s, t)
                if u:
                    s, view, t = gather(A["p_v"], u - 1, j)
                    t_last = t
                    sdg, dg, dr = DG.take()
                    td = S.done(S.free(t_a, *dr).activation(dg[:, :], ident[:, :], ACT.Copy, scale=av[:, j:j + 1]))
                    for half in range(2):
                        mm = PE.free(t, td).matmul(po[1][:, half, :], dg[:, :], view[:, half * 512:(half + 1) * 512],
                                                   start=(h == 0 and j == 0), stop=(h == 7 and j == 15))
                    t = PE.done(mm)
                    GR.release(s, t)
                    DG.release(sdg, t)
                next(nxt, None)
                for back in (ends, rest):
                    if next(back, 0) != 0:
                        break
                else:
                    next(extra, None)
            for _ in nxt:
                pass
            if u:
                used[(u - 1) % 4] = (t_last,)
                if h == 7:
                    for _ in ends:
                        pass
                    ends = finish(b, po, t)
        for _ in ends:
            pass
        for _ in extra:
            pass
        barrier()

    def gla():
        barrier()
        tri = [SC[:, 0:128], SC[:, 128:256]]
        glT = SC[0:33, 256:768]
        q_ = BIG[:, 0:1024].rearrange("p (h t) -> p h t", h=4)
        k_ = BIG[:, 1024:3072].rearrange("p (h t) -> p h t", h=4)
        v_ = BIG[:, 3072:7168].rearrange("p (b n) -> p b n", b=4)
        bT = BIG[:, 7168:11264].rearrange("p (u t) -> p u t", u=8)
        o = 11264
        wgt = BIG[0:33, o:o + 1024].rearrange("p (j n) -> p j n", j=2)
        QI = BIG[:, o + 1024:o + 2048].rearrange("p (u t) -> p u t", u=4)
        ATT = BIG[:, o + 2048:o + 3072].rearrange("p (u b t) -> p u b t", u=4, b=2)
        KE = BIG[:, o + 3072:o + 5120].rearrange("p (u b t) -> p u b t", u=4, b=4)
        Y = H[:, 2:4, :]
        SS = BIG[:, o:o + 1024].rearrange("p (u n) -> p u n", u=4)
        flat = HT[:, :, :].rearrange("p k t -> p (k t)")
        EB, EN, KI = (flat[:, 512 * i:512 * i + 512].rearrange("p (a t) -> p a t", a=2) for i in range(3))
        KD = flat[:, 1536:2560].rearrange("p (a t) -> p a t", a=2)
        S3 = flat[:, 2560:3072].rearrange("p (u n) -> p u n", u=2)
        dcs = flat[:, 3072:3104].rearrange("p (u c) -> p u c", u=4)
        gst = flat[:, 3104:3152].rearrange("p (i c) -> p i c", i=8)
        gmv = flat[:, 3152:3168].rearrange("p (i c) -> p i c", i=8)
        gsd = flat[:, 3168:3176]
        r_ = H[:, 0:2, :]
        G.done(G.at().affine_select(out=tri[0], in_=ones[:, :], compare_op=ALU.is_ge, fill=0.0, base=0,
                                    pattern=[[1, 128]], channel_multiplier=-1))
        G.done(G.at().memset(SC[0:64, 64:128], 0.0))
        G.done(G.at().affine_select(out=tri[1], in_=ones[:, :], compare_op=ALU.is_ge, fill=0.0, base=0,
                                    pattern=[[-1, 128]], channel_multiplier=1))
        G.done(G.at().memset(SC[64:128, 128:192], 0.0))
        G.done(G.at().memset(SC[32:33, 256:768], 1.0))
        t_z = G.done(G.at().memset(BIG[0:32, o:o + 1024], 0.0))
        G.done(G.at().memset(BIG[:, o + 2048:o + 3072], 0.0))
        t_g = G.last()
        t_wg = [load_once(wgt[0:16, 0, :], A["b_w_gate"][0, 0], t_z, by=S),
                load_once(wgt[16:32, 1, :], A["b_w_gate"][0, 1], by=S),
                load_once(wgt[32:33, :, :], A["b_gate_bias"], by=S)]
        t = modulated(1, 0, 1, range(4))
        t_h = to_HT(H, range(4), t)
        w = A["b_w_in"][0]

        def to(dst):
            return lambda name, ps, t: copy_out(dst(name), ps, t)

        wv = w.rearrange("(k p) n -> p k n", p=128)
        slab = [load_w(wv[:, k:k + 4, 3072:3104]) for k in (0, 4)]
        cols_proj(slab, [(0, 0, 32)], lambda k: HT[:, k, :], 512,
                  lambda j, ps, t: S.done(S.free(t, t_g).activation(glT[0:32, :], ps, ACT.Copy)), *t_h)
        t_gl = S.last()

        def gates():
            prev = {}
            for b in range(4):
                gt = H[:, 2 + b % 2, :]
                for j in range(2):
                    s, ps, readers = PS.take()
                    t = group(ps, [(glT[:, b * 128:(b + 1) * 128], wgt[:, j, :])], t_gl, *t_wg, t_g, *readers)
                    gs = gt[:, j * 512:(j + 1) * 512]
                    S.done(S.at(t, *prev.get(b % 2, ())).activation(gs, ps, ACT.Abs))
                    S.done(S.at().activation(gs, gs, ACT.Exp, scale=-1.0))
                    t = S.done(S.at().activation(gs, gs, ACT.Ln, bias=1.0))
                    t = V.done(V.at(t).scalar_tensor_tensor(gs, ps, 0.0, gs, ALU.min, ALU.subtract))
                    PS.release(s, t)
                    t_gg = t
                    yield
                    s, ps, readers = PS.take()
                    e = PE.free(t_gg, *readers)
                    for h in range(4):
                        mm = e.matmul(ps[:, h * 128:(h + 1) * 128], gs[:, h * 128:(h + 1) * 128], tri[j],
                                      start=True, stop=True)
                    t = PE.done(mm)
                    prev[b % 2] = (t,)
                    t = S.done(S.at(t).activation(bT[:, 4 * j:4 * j + 4, b * 128:(b + 1) * 128],
                                                  ps.rearrange("p (h t) -> p h t", h=4), ACT.Copy, scale=1.0 / 16.0))
                    PS.release(s, t)
                    yield

        def projections():
            slab = load_slab(w, 0, 512)
            cols_proj(slab, [(h, h * 128, 128) for h in range(4)], lambda k: HT[:, k, 0:256], 256,
                      to(lambda h: q_[:, h, :]), *t_h)
            yield
            slab = load_slab(w, 512, 512)
            cols_proj(slab, [(h, h * 128, 128) for h in range(4)], lambda k: HT[:, k, :], 512,
                      to(lambda h: k_[:, h, :]), *t_h)
            yield
            for n in range(2):
                slab = load_slab(w, 1024 + n * 512, 512)
                for b in range(4):
                    s, ps, readers = PS.take()
                    t = group(ps, [(HT[:, k, b * 128:(b + 1) * 128], slab[k // 4][1][:, k % 4, :], slab[k // 4][2])
                                   for k in range(8)], *readers)
                    PS.release(s, copy_out(v_[:, b, n * 512:n * 512 + 512], ps, t))
                    yield
                release_w(slab, t)

        in_turn(projections(), gates())
        for n in range(2):
            slab = load_slab(w, 2048 + n * 512, 512)
            rows_proj(slab, lambda k, b: HT[:, k, b * 128:(b + 1) * 128], range(2), 512,
                      lambda b, ps, t: S.done(S.free(t).activation(r_[:, b, n * 512:n * 512 + 512], ps, ACT.Silu)),
                      *t_h)
        t_all = barrier()
        tk = {}

        def prep(h):
            for j in range(2):
                i = (h % 2) * 2 + j
                bt = bT[:, 4 * j + h, :]
                b3 = bt.rearrange("p (c t) -> p c t", t=64)
                end = 63 if j == 0 else 0
                kd3 = KD[:, j, :].rearrange("p (c t) -> p c t", t=64)
                old = tk.get((h - 1, j), ())
                t1 = V.done(V.at(*old).tensor_tensor(kd3, b3[:, :, end:end + 1].to_broadcast([128, 8, 64]), b3,
                                                     ALU.subtract))
                t1 = S.done(S.at(t1).activation(KD[:, j, :], KD[:, j, :], ACT.Exp))
                t2 = S.done(S.at().activation(EB[:, j, :], bt[:, 0:256], ACT.Exp))
                t3 = S.done(S.at().activation(EN[:, j, :], bt[:, 0:256], ACT.Exp, scale=-1.0))
                t_dc = S.done(S.at().activation(dcs[:, i, :], b3[:, :, end], ACT.Exp))
                yield
                t_kd = V.done(V.at(t1).tensor_tensor(KD[:, j, :], KD[:, j, :], k_[:, h, :], ALU.mult))
                s, ps, readers = PS.take()
                e = PE.free(t_kd, *readers)
                for b in range(4):
                    mm = e.transpose(ps[:, b * 128:(b + 1) * 128], KD[:, j, b * 128:(b + 1) * 128], ident[:, :])
                t = PE.done(mm)
                t_ke = S.done(S.free(t).activation(KE[:, i, :, :], ps.rearrange("p (b t) -> p b t", b=4), ACT.Copy))
                PS.release(s, t_ke)
                yield
                V.done(V.at(t2).scalar_tensor_tensor(QI[:, i, :], q_[:, h, :], 128.0 ** -0.5, EB[:, j, :],
                                                     ALU.mult, ALU.mult))
                t = V.done(V.at(t3).tensor_tensor(KI[:, j, :], k_[:, h, 0:256], EN[:, j, :], ALU.mult))
                yield
                s, ps, readers = PS.take()
                e = PE.free(t, *readers)
                for b in range(2):
                    mm = e.matmul(ps[:, b * 128:(b + 1) * 128], KI[:, j, b * 128:(b + 1) * 128],
                                  QI[:, i, b * 128:(b + 1) * 128], start=True, stop=True)
                t = PE.done(mm)
                tk[h, j] = (t,)
                for b in range(2):
                    t_at = V.done(V.at(t).copy_predicated(ATT[:, i, b, :], tri[j].bitcast(I32),
                                                          ps[:, b * 128:(b + 1) * 128]))
                PS.release(s, t_at)
                tk[h, j, "ready"] = (t_at, t_ke, t_dc)
                yield

        orders = [[(2, 0), (2, 1), (3, 0), (3, 1), (0, 0), (0, 1), (1, 0), (1, 1)],
                  [(3, 1), (3, 0), (2, 1), (2, 0), (1, 1), (1, 0), (0, 1), (0, 0)]]

        def chain(h):
            so, po, readers = PO.take()
            PE.free(*readers)
            hv = slice(h * 256, (h + 1) * 256)
            for j in range(2):
                e = PE.free(*tk[h, j, "ready"])
                for b in range(2):
                    mm = e.matmul(po[:, b, 0:256], ATT[:, (h % 2) * 2 + j, b, :], v_[:, b, hv],
                                  start=(j == 0), stop=False, skip_group_check=True)
            t_read = [PE.done(mm)] * 2
            yield
            state = [None, None]
            bufs = [[SS[:, 0, :], SS[:, 1, :], S3[:, 0, :]], [SS[:, 2, :], SS[:, 3, :], S3[:, 1, :]]]
            reads = [{}, {}]
            for n in range(8):
                for j in range(2):
                    i = (h % 2) * 2 + j
                    b, a = orders[j][n]
                    rows = slice(64 * a, 64 * a + 64)
                    if n < 7:
                        s, ps, readers = PS.take()
                        t = group(ps[:, 0:256], [(KE[rows, i, b, :], v_[rows, b, hv])], *readers)
                    if b < 2:
                        tc = slice(b * 128 + a * 64, b * 128 + a * 64 + 64)
                        mm = PE.free(state[j][1]).matmul(po[rows, b, 0:256], QI[:, i, tc], state[j][0], start=False,
                                                         stop=False, skip_group_check=True)
                        reads[j][(n - 1) % 3] = PE.done(mm)
                    if n < 7:
                        new = bufs[j][n % 3]
                        w_ = [reads[j][n % 3]] if n % 3 in reads[j] else [t_read[j]]
                        if n == 0:
                            t_st = V.done(V.at(t, *w_).tensor_copy(new, ps[:, 0:256]))
                        else:
                            c = 2 * b + a
                            t_st = V.done(V.at(t, *w_).scalar_tensor_tensor(
                                new, state[j][0], dcs[:, i, c:c + 1], ps[:, 0:256], ALU.mult, ALU.add))
                        PS.release(s, t_st)
                        state[j] = (new, t_st)
                    yield
            t = S.done(S.at(PE.last()).activation(Y[:, :, hv], po[:, :, 0:256], ACT.Copy))
            PO.release(so, t)
            yield

        in_turn(prep(0))
        for h in range(4):
            if h < 3:
                in_turn(chain(h), prep(h + 1))
            else:
                in_turn(chain(h))
        t_y = S.last()
        for b in range(2):
            for h in range(4):
                i = 4 * b + h
                V.done(V.at(t_y).bn_stats(gst[:, i, :], Y[:, b, h * 256:(h + 1) * 256]))
        for i in range(8):
            V.done(V.at().bn_aggr(gmv[:, i, :], gst[:, i, :]))
        t = V.done(V.at().tensor_scalar(gsd, gmv[:, :, 1], EPS, None, ALU.add))
        t = S.done(S.at(t).activation(gsd, gsd, ACT.Sqrt))
        V.done(V.at(t).reciprocal(gsd, gsd))
        sgn, gnv, tgn = load_bc(A["b_gn_g"][0])
        for b in range(2):
            for h in range(4):
                i = 4 * b + h
                y = Y[:, b, h * 256:(h + 1) * 256]
                V.done(V.at().tensor_scalar(y, y, gmv[:, i, 0:1], gsd[:, i:i + 1], ALU.subtract, ALU.mult))
            V.done(V.at(tgn).tensor_tensor(Y[:, b, :], Y[:, b, :], gnv, ALU.mult))
            t = V.done(V.at().tensor_tensor(Y[:, b, :], Y[:, b, :], r_[:, b, :], ALU.mult))
        BC.release(sgn, t)
        t_h = to_HT(Y, range(2), t, PE.last())
        mixer_out(A["b_w_out"][0], 1, range(2), t_h)

    def sb_ssm():
        barrier()
        t_h = to_HT(X, range(2))
        zz, ll, nn = (BIG[:, 2048 * i:2048 * i + 2048] for i in range(3))
        ZZ, LL, NN = (a.rearrange("p (h n) -> p h n", h=4) for a in (zz, ll, nn))
        q_ = BIG[:, 6144:7168].rearrange("p (h t) -> p h t", h=4)
        k_ = BIG[:, 7168:8192].rearrange("p (h t) -> p h t", h=4)
        XR = BIG[:, 8192:12288].rearrange("p (j t) -> p j t", j=16)
        XI = BIG[:, 12288:16384].rearrange("p (j t) -> p j t", j=16)
        XR4 = BIG[:, 8192:12288].rearrange("p (j c t) -> p j c t", j=16, c=16)
        XI4 = BIG[:, 12288:16384].rearrange("p (j c t) -> p j c t", j=16, c=16)
        AO = X[:, 2, :].rearrange("p (h t) -> p h t", h=4)
        TT = Ring([X[:, 3, 512 * i:512 * i + 512] for i in range(2)], [None] * 2)
        v_ = H[:, 0, :].rearrange("p (b n) -> p b n", b=2)
        uT = H[:, 1, :].rearrange("p (c t) -> p c t", c=4)
        yT = H[:, 2, :].rearrange("p (c t) -> p c t", c=4)
        zT = H[:, 3, :].rearrange("p (c t) -> p c t", c=4)
        strict = SC[:, 0:128]
        u1, u2 = (SC[:, 128 + 256 * i:384 + 256 * i].rearrange("p (j c) -> p j c", j=16) for i in range(2))
        PW = SC[:, 640:1152].rearrange("p (i t j) -> p i t j", i=2, t=16)
        t_m = G.done(G.at().affine_select(out=strict, in_=ones[:, :], compare_op=ALU.is_gt, fill=0.0, base=0,
                                          pattern=[[-1, 128]], channel_multiplier=1))
        c_ = sb("s5c", [128, 13, 16])
        cl = [c_[:, i, :] for i in range(13)]
        dT = sb("s5d", [128, 4])
        bglu = sb("bglu", [128, 4])
        t_l = [load_once(cl[0], A["ldt"]), load_once(cl[1], A["lre"]), load_once(cl[2], A["lim"])]
        t_d = load_once(dT[:, :], A["s5dT"])
        t_bg = load_once(bglu[:, :], A["bgluT"])
        w = A["sb_ssm_w_in_2"][0]
        hT = lambda k: HT[:, k, 0:256]

        def evac(dst):
            return lambda i, ps, t: S.done(S.free(t).activation(dst(i), ps, ACT.Copy))

        quarters = [(i, i * 128, 128) for i in range(4)]
        cols_proj(load_slab(w, 1536, 512), quarters, hT, 256, evac(lambda i: uT[:, i, :]), *t_h)
        t_u = S.last()

        def vt(o, a, b, op):
            return V.done(V.at().tensor_tensor(o, a, b, op))

        def vs(o, a, s1, s2, o1, o2=None):
            if o2 is None:
                return V.done(V.at().tensor_scalar(o, a, s1, None, o1))
            return V.done(V.at().tensor_scalar(o, a, s1, s2, o1, o2))

        dt, lr, li, ar, ai, cr, ci, den, x0, x1, x2, x3 = cl[0:12]
        t = S.done(S.at(*t_l).activation(dt, dt, ACT.Exp))
        V.free(t, *t_l)
        t = vt(x0, lr, dt, ALU.mult)
        t = S.done(S.at(t).activation(x0, x0, ACT.Exp))
        V.free(t)
        vt(x1, li, dt, ALU.mult)
        vs(x2, x1, 1.0 / TWO_PI, 12582912.0, ALU.mult, ALU.add)
        vs(x2, x2, -12582912.0, None, ALU.add)
        for c in (6.28125, 0.0019350051879882812, 3.0199159819567e-07):
            V.done(V.at().scalar_tensor_tensor(x1, x2, -c, x1, ALU.mult, ALU.add))
        vs(x1, x1, PI - 1e-6, -(PI - 1e-6), ALU.min, ALU.max)
        t = V.last()
        t = S.done(S.at(t).activation(x2, x1, ACT.Abs))
        V.free(t)
        t = vs(x2, x2, -1.0, PI / 2, ALU.mult, ALU.add)
        S.done(S.at(t).activation(x2, x2, ACT.Sin))
        t = S.done(S.at().activation(x1, x1, ACT.Sin))
        V.free(t)
        vt(ar, x0, x2, ALU.mult)
        vt(ai, x0, x1, ALU.mult)
        vt(x0, lr, lr, ALU.mult)
        vt(x1, li, li, ALU.mult)
        vt(den, x0, x1, ALU.add)
        V.done(V.at().reciprocal(den, den))
        vs(x3, ar, -1.0, None, ALU.add)
        vt(x0, x3, lr, ALU.mult)
        vt(x1, ai, li, ALU.mult)
        vt(x0, x0, x1, ALU.add)
        vt(cr, x0, den, ALU.mult)
        vt(x0, ai, lr, ALU.mult)
        vt(x1, x3, li, ALU.mult)
        vt(x0, x0, x1, ALU.subtract)
        t_co = vt(ci, x0, den, ALU.mult)

        def cmadd(dr, di, pr, pi, sr, si, a1, a2):
            vt(a1, sr, pr, ALU.mult)
            vt(a2, si, pi, ALU.mult)
            vt(a1, a1, a2, ALU.subtract)
            vt(a2, sr, pi, ALU.mult)
            vt(dr, dr, a1, ALU.add)
            vt(a1, si, pr, ALU.mult)
            vt(a2, a2, a1, ALU.add)
            return vt(di, di, a2, ALU.add)

        def drive():
            wb = [load_w(A["s5_br"]), load_w(A["s5_bi"])]
            for j in range(16):
                s, ps, readers = PS.take()
                PE.free(t_u, *readers)
                for i in range(2):
                    t = group(ps[:, i * 256:(i + 1) * 256], [(wb[i][1][:, j, :], uT[:, j // 4, :])], wb[i][2])
                P, Q = ps[:, 0:256], ps[:, 256:512]
                st, tt, rr = TT.take()
                S.done(S.free(t, t_co, *rr).activation(tt[:, 0:256], Q, ACT.Copy, scale=ci[:, j:j + 1]))
                t = S.done(S.free().activation(tt[:, 256:512], P, ACT.Copy, scale=ci[:, j:j + 1]))
                V.done(V.at(t).scalar_tensor_tensor(XR[:, j, :], P, cr[:, j:j + 1], tt[:, 0:256],
                                                    ALU.mult, ALU.subtract))
                t = V.done(V.free().scalar_tensor_tensor(XI[:, j, :], Q, cr[:, j:j + 1], tt[:, 256:512],
                                                         ALU.mult, ALU.add))
                PS.release(s, t)
                TT.release(st, t)
            release_w(wb, PE.last())

        def state_space():
            V.done(V.at().tensor_copy(PW[:, 0, 0, :], ar))
            V.done(V.at().tensor_copy(PW[:, 1, 0, :], ai))
            for n in range(1, 16):
                pr, pi = PW[:, 0, n - 1, :], PW[:, 1, n - 1, :]
                vt(x0, pr, ar, ALU.mult)
                vt(x1, pi, ai, ALU.mult)
                vt(PW[:, 0, n, :], x0, x1, ALU.subtract)
                vt(x0, pr, ai, ALU.mult)
                vt(x1, pi, ar, ALU.mult)
                vt(PW[:, 1, n, :], x0, x1, ALU.add)
                if n % 2:
                    yield
            bc = lambda ap, n: ap.unsqueeze(2).to_broadcast([128, 16, n])
            for n in range(1, 16):
                cmadd(XR4[:, :, :, n], XI4[:, :, :, n], bc(ar, 16), bc(ai, 16), XR4[:, :, :, n - 1],
                      XI4[:, :, :, n - 1], u1, u2)
                yield
            for c in range(1, 16):
                cmadd(XR4[:, :, c, 15], XI4[:, :, c, 15], PW[:, 0, 15, :], PW[:, 1, 15, :], XR4[:, :, c - 1, 15],
                      XI4[:, :, c - 1, 15], x0, x1)
                if c % 2:
                    yield
            for n in range(15):
                cmadd(XR4[:, :, 1:16, n], XI4[:, :, 1:16, n], bc(PW[:, 0, n, :], 15), bc(PW[:, 1, n, :], 15),
                      XR4[:, :, 0:15, 15], XI4[:, :, 0:15, 15], u1[:, :, 0:15], u2[:, :, 0:15])
                yield

        def attention():
            cols_proj(load_slab(w, 0, 512), quarters, hT, 256, evac(lambda i: q_[:, i, :]))
            yield
            cols_proj(load_slab(w, 512, 512), quarters, hT, 256, evac(lambda i: k_[:, i, :]))
            yield
            rows_proj(load_slab(w, 1024, 512), lambda k, b: HT[:, k, b * 128:(b + 1) * 128], range(2), 512,
                      evac(lambda b: v_[:, b, :]))
            t_p = S.last()
            yield
            keep = dict(compare_op=ALU.is_gt, fill=0.0, base=0, pattern=[[0, 4], [-128, 2], [1, 256]],
                        channel_multiplier=-1)
            t_old = ()
            for g in range(2):
                for i in range(4):
                    h = 4 * g + i
                    p = slice(64 * (h % 2), 64 * (h % 2) + 64)
                    s, ps, readers = PS.take()
                    e = PE.free(t_p, *readers)
                    for sk in range(2):
                        mm = e.matmul(ps[:, sk * 256:(sk + 1) * 256], k_[p, h // 2, sk * 128:(sk + 1) * 128],
                                      q_[p, h // 2, :], start=True, stop=True)
                    t = PE.done(mm)
                    t_z = S.done(S.free(t, *t_old).activation(ZZ[:, i, :], ps, ACT.Copy, scale=0.125))
                    PS.release(s, t_z)
                yield
                S.done(S.at(*t_old).activation(nn, zz, ACT.Abs))
                S.done(S.at().activation(nn, nn, ACT.Exp, scale=-1.0))
                t_n = S.done(S.at().activation(nn, nn, ACT.Ln, bias=1.0))
                yield
                yield
                yield
                V.done(V.at(t_n, *t_old).scalar_tensor_tensor(ll, zz, 0.0, nn, ALU.min, ALU.subtract))
                t = V.done(V.at().tensor_tensor(nn, ll, zz, ALU.subtract))
                n4 = nn.rearrange("p (h b q) -> p h b q", h=4, b=2)
                l4 = ll.rearrange("p (h b q) -> p h b q", h=4, b=2)
                t_n = G.done(G.at(t).affine_select(out=n4, in_=n4, **keep))
                yield
                yield
                for i in range(4):
                    s, ps, readers = PS.take()
                    PE.free(t_n, t_m, *readers)
                    nh = NN[:, i, :]
                    group(ps[:, 0:256], [(strict, nh[:, 0:256]), (ones[:, :], nh[:, 256:512])])
                    t = group(ps[:, 256:512], [(strict, nh[:, 256:512])])
                    t = V.done(V.free(t).tensor_tensor(LL[:, i, :], LL[:, i, :], ps, ALU.add))
                    PS.release(s, t)
                    yield
                t = S.done(S.at(t).activation(ll, ll, ACT.Exp))
                t_w = G.done(G.at(t).affine_select(out=l4, in_=l4, **keep))
                yield
                yield
                for i in range(4):
                    h = 4 * g + i
                    r = slice(64 * (h % 2), 64 * (h % 2) + 64)
                    s, ps, readers = PS.take()
                    PE.free(t_w, *readers)
                    t = group(ps[r, 0:256], [(v_[:, b, h * 64:(h + 1) * 64], LL[:, i, b * 256:(b + 1) * 256])
                                             for b in range(2)])
                    PS.release(s, S.done(S.free(t).activation(AO[r, h // 2, :], ps[r, 0:256], ACT.Copy)))
                t_old = (t, t_w, V.last())
                yield

        drive()
        in_turn(state_space(), attention())
        t_x = V.last()
        wc = [load_w(A["s5_cr"]), load_w(A["s5_ci"])]
        for c in range(4):
            s, ps, readers = PS.take()
            PE.free(t_x, *readers)
            for i, xx in enumerate((XR, XI)):
                t = group(ps[:, i * 256:(i + 1) * 256],
                          [(wc[i][1][:, 4 * c + m, :], xx[:, 4 * c + m, :]) for m in range(4)], wc[i][2])
            V.done(V.at(t, t_d).scalar_tensor_tensor(yT[:, c, :], uT[:, c, :], dT[:, c:c + 1], ps[:, 0:256],
                                                     ALU.mult, ALU.add))
            t = V.done(V.at().tensor_tensor(yT[:, c, :], yT[:, c, :], ps[:, 256:512], ALU.subtract))
            PS.release(s, t)
            t_y = S.done(S.free(t).activation(yT[:, c, :], yT[:, c, :], ACT.Gelu_apprx_tanh))
        release_w(wc, PE.last())
        slab = load_slab(A["ssm_w_glu_2"][0], 0, 512, kts=4)
        cols_proj(slab, quarters, lambda k: yT[:, k, :], 256,
                  lambda c, ps, t: S.done(S.free(t, t_bg).activation(zT[:, c, :], ps, ACT.Sigmoid,
                                                                     bias=bglu[:, c:c + 1])), t_y)
        t_z = V.done(V.at(S.last(), PE.last()).tensor_tensor(H[:, 2, :], H[:, 2, :], H[:, 3, :], ALU.mult))
        for n in range(2):
            slab = load_slab(A["sb_ssm_w_out_2"][0], n * 512, 512)

            def both(k, b):
                bl = slice(b * 128, (b + 1) * 128)
                return AO[:, k, bl] if k < 4 else yT[:, k - 4, bl]

            rows_proj(slab, both, range(2), 512, lambda b, ps, t: residual(b, n * 512, ps, t), t_z, S.last())
        layer_norm([(X[:, b, :], X[:, b, :]) for b in range(2)], A["ln_mix_g_2"][0], A["ln_mix_b_2"][0])

    def mlp(l):
        barrier()
        t_h = to_HT(X, range(2))
        F = BIG[:, 0:8192].rearrange("p (f t) -> p f t", f=32)
        RL = Ring([BIG[:, 8192 + 256 * i:8448 + 256 * i] for i in range(4)], [None] * 4)
        for n in range(8):
            slab = load_slab(A["mlp_w1_2"][l], n * 512, 512)

            def evac(f, ps, t):
                sr, rl, rr = RL.take()
                t = S.done(S.free(t, *rr).activation(rl, ps, ACT.Relu))
                t2 = V.done(V.free(t).tensor_tensor(F[:, f, :], rl, rl, ALU.mult))
                RL.release(sr, t2)
                return t

            cols_proj(slab, [(4 * n + j, j * 128, 128) for j in range(4)], lambda k: HT[:, k, 0:256], 256, evac, *t_h)
        t_f = V.last()
        w2 = A["mlp_w2_2"][l].rearrange("(k p) n -> p k n", p=128)
        acc = []
        for b in range(2):
            so, po, readers = PO.take()
            PE.free(*readers)
            acc.append((so, po))
        for k in range(0, 32, 2):
            ws, wv, wt = load_w(w2[:, k:k + 2, :])
            e = PE.free(t_f, wt)
            for kk in range(2):
                for b in range(2):
                    for n in range(2):
                        mm = e.matmul(acc[b][1][:, n, :], F[:, k + kk, b * 128:(b + 1) * 128],
                                      wv[:, kk, n * 512:(n + 1) * 512], start=(k + kk == 0), stop=(k + kk == 31))
            t = PE.done(mm)
            WR.release(ws, t)
        for b in range(2):
            for n in range(2):
                t2 = residual(b, n * 512, acc[b][1][:, n, :], t)
            PO.release(acc[b][0], t2)
        layer_norm([(X[:, b, :], X[:, b, :]) for b in range(2)], A["ln_ffn_g_2"][l], A["ln_ffn_b_2"][l])

    def dsa():
        barrier()
        t_h = to_HT(X, range(2))
        q_ = BIG[:, 0:2048].rearrange("p (h t) -> p h t", h=8)
        k_ = BIG[:, 2048:3072].rearrange("p (h t) -> p h t", h=4)
        qi = BIG[:, 3072:3584].rearrange("p (h t) -> p h t", h=2)
        ki = BIG[:, 3584:3840]
        v_ = BIG[:, 3840:4352].rearrange("p (b n) -> p b n", b=2)
        wi = BIG[:, 4352:4368].rearrange("p (b n) -> p b n", b=2)
        m8 = BIG[:, 4368:4376]
        nm = BIG[:, 4376:4440]
        score = BIG[:, 4480:4992]
        nd = BIG[:, 4992:5504]
        mn = BIG[:, 5504:6016]
        OT = BIG[:, 6016:8064].rearrange("p (h t) -> p h t", h=8)
        RL = Ring([BIG[:, 8192 + 256 * i:8448 + 256 * i] for i in range(4)], [None] * 4)
        LG = Ring([BIG[:, 9216 + 512 * i:9728 + 512 * i] for i in range(4)], [None] * 4)
        PT = Ring([BIG[:, 11264 + 512 * i:11776 + 512 * i] for i in range(4)], [None] * 4)
        t_nd = G.done(G.at().iota(nd.rearrange("p (b s) -> p b s", b=2), pattern=[[-128, 2], [1, 256]], base=0,
                                  channel_multiplier=-1, allow_small_or_imprecise_dtypes=True))
        w = A["dsa_w"]
        hT = lambda k: HT[:, k, 0:256]
        rows = lambda k, b: HT[:, k, b * 128:(b + 1) * 128]
        wv = w.rearrange("(k p) n -> p k n", p=128)
        slab = load_slab(w, 1536, 512)
        last_slab = [load_w(wv[:, k:k + 4, 2048:2184]) for k in (0, 4)]
        for g in range(3):
            s, ps, readers = PS.take()
            pairs = []
            for k in range(8):
                ws = slab if g < 2 else last_slab
                c0 = 256 + g * 128 if g < 2 else 0
                pairs.append((ws[k // 4][1][:, k % 4, c0:c0 + 128], hT(k), ws[k // 4][2]))
            t = group(ps[:, 0:256], pairs, *readers, *t_h)
            PS.release(s, copy_out(qi[:, g, :] if g < 2 else ki, ps[:, 0:256], t))
        for b in range(2):
            s, ps, readers = PS.take()
            t = group(ps[:, 0:8], [(rows(k, b), last_slab[k // 4][1][:, k % 4, 128:136]) for k in range(8)], *readers)
            PS.release(s, copy_out(wi[:, b, :], ps[:, 0:8], t))
            s, ps, readers = PS.take()
            t = group(ps[:, 0:256], [(rows(k, b), slab[k // 4][1][:, k % 4, 0:256]) for k in range(8)], *readers)
            PS.release(s, copy_out(v_[:, b, :], ps[:, 0:256], t))
        release_w(slab + last_slab, PE.last())
        t_i = (V.last(), S.last())

        def select():
            for h in range(8):
                for b in range(2):
                    sc = score[:, b * 256:(b + 1) * 256]
                    p = slice(32 * (h % 4), 32 * (h % 4) + 32)
                    s, ps, readers = PS.take()
                    t = group(ps[:, 0:256], [(qi[p, h // 4, b * 128:(b + 1) * 128], ki[p, :])], *t_i, *readers)
                    sr, rl, rr = RL.take()
                    t = S.done(S.free(t, *rr).activation(rl, ps[:, 0:256], ACT.Relu))
                    PS.release(s, t)
                    if h == 0:
                        t = V.done(V.at(t, *t_i).tensor_scalar(sc, rl, wi[:, b, h:h + 1], None, ALU.mult))
                    else:
                        t = V.done(V.at(t).scalar_tensor_tensor(sc, rl, wi[:, b, h:h + 1], sc, ALU.mult, ALU.add))
                    RL.release(sr, t)
                yield
            t = V.done(V.at().tensor_scalar(score, score, (32.0 ** -0.5) * (8.0 ** -0.5), None, ALU.mult))
            s3 = score.rearrange("p (b s) -> p b s", b=2)
            t = G.done(G.at(t).affine_select(out=s3, in_=s3, compare_op=ALU.is_ge, fill=-1.0e38, base=0,
                                             pattern=[[128, 2], [-1, 256]], channel_multiplier=1))
            V.free(t)
            yield
            for b in range(2):
                sc = score[:, b * 256:(b + 1) * 256]
                for r in range(8):
                    V.done(V.at().max(m8, sc))
                    V.done(V.at().match_replace(sc, m8, sc, NEG))
                    yield
            t = V.done(V.at().tensor_scalar(mn, score, -2.0e38, -1.0e30, ALU.is_gt, ALU.mult))
            m3 = mn.rearrange("p (b s) -> p b s", b=2)
            t = G.done(G.at(t).affine_select(out=m3, in_=m3, compare_op=ALU.is_ge, fill=-1.0e30, base=0,
                                             pattern=[[128, 2], [-1, 256]], channel_multiplier=1))
            V.free(t, t_nd)
            yield

        def evac(dst, ps, t):
            return S.done(S.free(t).activation(dst, ps, ACT.Copy))

        def projections():
            slab = load_slab(w, 1024, 512)
            for h in range(4):
                s, ps, readers = PS.take()
                t = group(ps[:, 0:256], [(slab[k // 4][1][:, k % 4, h * 128:(h + 1) * 128], hT(k), slab[k // 4][2])
                                         for k in range(8)], *readers)
                PS.release(s, evac(k_[:, h, :], ps[:, 0:256], t))
                yield
            release_w(slab, PE.last())
            for n in range(2):
                slab = load_slab(w, n * 512, 512)
                for i in range(4):
                    s, ps, readers = PS.take()
                    t = group(ps[:, 0:256], [(slab[k // 4][1][:, k % 4, i * 128:(i + 1) * 128], hT(k),
                                              slab[k // 4][2]) for k in range(8)], *readers)
                    PS.release(s, evac(q_[:, 4 * n + i, :], ps[:, 0:256], t))
                    yield
                release_w(slab, PE.last())

        in_turn(select(), projections())
        t_p = (V.last(), S.last())
        lgs, pts = {}, {}

        def scores(h):
            p = slice(64 * (h % 2), 64 * (h % 2) + 64)
            s, ps, readers = PS.take()
            PE.free(*t_p, *readers)
            for b in range(2):
                t = group(ps[:, b * 256:(b + 1) * 256], [(q_[p, h // 2, b * 128:(b + 1) * 128], k_[p, h // 4, :])])
            sl, lg, lr_ = LG.take()
            V.done(V.at(*lr_).scalar_tensor_tensor(lg, nd, 2.0 ** (-8.0 * (h + 1) / 16), mn, ALU.mult, ALU.add))
            t = V.done(V.at(t).scalar_tensor_tensor(lg, ps, 0.125, lg, ALU.mult, ALU.add))
            PS.release(s, t)
            lg3 = lg.rearrange("p (b s) -> p b s", b=2)
            t = V.done(V.at().tensor_reduce(nm[:, 2 * h:2 * h + 2], lg3, AX, ALU.max, negate=True))
            for b in range(2):
                t = S.done(S.free(t).activation(lg3[:, b, :], lg3[:, b, :], ACT.Exp,
                                                bias=nm[:, 2 * h + b:2 * h + b + 1],
                                                accum_out=nm[:, 32 + 2 * h + b:33 + 2 * h + b]))
            lgs[h] = (sl, lg, lg3, t)

        def spread(h):
            sl, lg, lg3, t = lgs[h]
            z = nm[:, 32 + 2 * h:34 + 2 * h]
            V.done(V.at(t).reciprocal(z, z))
            for b in range(2):
                t = V.done(V.at().tensor_scalar(lg3[:, b, :], lg3[:, b, :], z[:, b:b + 1], None, ALU.mult))
            s, ps, readers = PS.take()
            e = PE.free(t, *readers)
            for b in range(2):
                for sk in range(2):
                    mm = e.transpose(ps[:, sk * 256 + b * 128:sk * 256 + b * 128 + 128],
                                     lg[:, b * 256 + sk * 128:b * 256 + sk * 128 + 128], ident[:, :])
            t = PE.done(mm)
            LG.release(sl, t)
            sp_, pt, pr_ = PT.take()
            t = S.done(S.free(t, *pr_).activation(pt, ps, ACT.Copy))
            PS.release(s, t)
            pts[h] = (sp_, pt, t)

        def outputs(h):
            sp_, pt, t = pts[h]
            kv = h // 4
            r = slice(64 * (h % 2), 64 * (h % 2) + 64)
            s, ps, readers = PS.take()
            t = group(ps[r, 0:256], [(v_[:, sk, kv * 64:(kv + 1) * 64], pt[:, sk * 256:(sk + 1) * 256])
                                     for sk in range(2)], t, *readers)
            PT.release(sp_, t)
            PS.release(s, S.done(S.free(t).activation(OT[r, h // 2, :], ps[r, 0:256], ACT.Copy)))

        for h in range(16 + 3):
            if h < 16:
                scores(h)
            if 2 <= h < 18:
                spread(h - 2)
            if 3 <= h:
                outputs(h - 3)
        t_o = S.last()
        wo = A["dsa_w_out_2"][0]
        for n in range(2):
            slab = load_slab(wo, n * 512, 512)
            rows_proj(slab, lambda k, b: OT[:, k, b * 128:(b + 1) * 128], range(2), 512,
                      lambda b, ps, t: residual(b, n * 512, ps, t), t_o)
        layer_norm([(X[:, b, :], X[:, b, :]) for b in range(2)], A["ln_mix_g_2"][1], A["ln_mix_b_2"][1])

    V.free(*t_x)
    PE.free(*t_x)
    t_silu = ()
    if "mod0" in parts or "mod1" in parts:
        t = S.done(S.at(t_sc).activation(scS[:, :, :], scT[:, :, :], ACT.Sigmoid))
        t_silu = (V.done(V.at(t).tensor_tensor(scS[:, :, :], scS[:, :, :], scT[:, :, :], ALU.mult)),)
    if "mod0" in parts:
        for _ in modulation(0, 0, 4):
            pass
    if "mix0" in parts:
        chunk_mlp()
    if "peer0" in parts:
        peer(0, [2, 3, 0, 1], (modulation(1, 0, 4), modulation(1, 4, 8)) if "mod1" in parts else ())
    elif "mod1" in parts:
        for g in (modulation(1, 0, 4), modulation(1, 4, 8)):
            for _ in g:
                pass
    if "mix1" in parts:
        gla()
    if "peer1" in parts:
        peer(1, [0, 1])
    if "sb" in parts:
        sb_ssm()
    if "mlp0" in parts:
        mlp(0)
    if "dsa" in parts:
        dsa()
    if "mlp1" in parts:
        mlp(1)
    s_out = sem("s_out")
    D.free(V.last()).dma_start(out[0].rearrange("(b p) d -> p b d", p=128), X[:, 0:2, :]).then_inc(s_out, 16)
    nc.sync.wait_ge(s_out, 16)
    for i in range(2):
        if ms_count[i]:
            nc.sync.wait_ge(s_ms[i], ms_count[i])
    ctx.close()


_OUTS = [((1, 256, 1024), 'float32')]


def layout(inputs):
    import numpy as np

    def c(a):
        return np.ascontiguousarray(a)

    a = {k: np.asarray(v) for k, v in inputs.items()}
    o = {}
    for k in ("x", "ctx", "w_mod", "b_mod", "ln_g", "ln_b", "a_w_in", "a_norm_g", "a_norm_b", "a_w_out", "b_w_in",
              "b_w_gate", "b_gate_bias", "b_gn_g", "b_w_out", "p_w_q", "sb_ssm_w_in_2", "ssm_w_glu_2",
              "sb_ssm_w_out_2", "dsa_w_out_2", "ln_mix_g_2", "ln_mix_b_2", "ln_ffn_g_2", "ln_ffn_b_2",
              "mlp_w1_2", "mlp_w2_2"):
        o[k] = c(a[k])
    o["p_u"] = c(a["p_u"].reshape(32768, 1024))
    o["p_v"] = c(a["p_v"].reshape(32768, 1024))
    w = a["dsa_w_in_2"][0]
    k = np.repeat(w[:, 1024:1280].reshape(1024, 4, 1, 64), 2, axis=2).reshape(1024, 512)
    ki = np.repeat(w[:, 1792:1824].reshape(1024, 1, 32), 4, axis=1).reshape(1024, 128)
    o["dsa_w"] = c(np.concatenate([w[:, 0:1024], k, w[:, 1280:1792], ki, w[:, 1824:1832]], axis=1))
    cc = np.stack([a["c"][0], a["c_ctx"]])
    o["cT"] = c(cc.reshape(2, 8, 128).transpose(2, 1, 0))
    o["a_b_sT"] = c(a["a_b_s"][0].T)
    o["a_w_sT"] = c(a["a_w_s"][0].transpose(2, 0, 1))
    o["keysT"] = c(a["p_keys"].transpose(0, 1, 3, 2))
    o["ldt"] = c(np.repeat(a["ssm_log_dt_2"][0], 64).reshape(16, 128).T)
    o["lre"] = c(a["ssm_lam_re_2"][0].reshape(16, 128).T)
    o["lim"] = c(a["ssm_lam_im_2"][0].reshape(16, 128).T)
    o["s5dT"] = c(a["ssm_d_2"][0].reshape(4, 128).T)
    o["bgluT"] = c(a["ssm_b_glu_2"][0].reshape(4, 128).T)
    for name, key in (("s5_br", "ssm_b_re_2"), ("s5_bi", "ssm_b_im_2")):
        w = np.zeros((128, 16, 128), np.float32)
        for g in range(32):
            w[(g % 8) * 16:(g % 8) * 16 + 16, g // 2, (g % 2) * 64:(g % 2) * 64 + 64] = a[key][0, g].T
        o[name] = w
    for name, key in (("s5_cr", "ssm_c_re_2"), ("s5_ci", "ssm_c_im_2")):
        w = np.zeros((128, 16, 128), np.float32)
        for g in range(32):
            w[(g % 2) * 64:(g % 2) * 64 + 64, g // 2, (g % 8) * 16:(g % 8) * 16 + 16] = a[key][0, g].T
        o[name] = w
    return o


def kernel(**inputs):
    import numpy as _np
    import concourse.bacc as _bacc
    from concourse import mybir as _mybir
    from concourse.bass_utils import run_bass_kernel_spmd as _run

    nc = _bacc.Bacc("TRN2", target_bir_lowering=False, num_devices=1)
    arrays, args = {}, {}
    for name, a in layout(inputs).items():
        arrays[f"in_{name}_dram"] = a
        args[name] = nc.dram_tensor(f"in_{name}_dram", a.shape, _mybir.dt.from_np(a.dtype), kind="ExternalInput").ap()
    shape, dtype = _OUTS[0]
    out = nc.dram_tensor("out_0_dram", shape, _mybir.dt.from_np(_np.dtype(dtype)), kind="ExternalOutput").ap()
    program(nc, args, out)
    r = _run(nc, [arrays], core_ids=[0])
    return r.results[0]["out_0_dram"]
```

```python
from contextlib import ExitStack

import concourse.bass as bass
from concourse import mybir

F32 = mybir.dt.float32
I32 = mybir.dt.int32
U32 = mybir.dt.uint32
ALU = mybir.AluOpType
ACT = mybir.ActivationFunctionType
AX = mybir.AxisListType.X

EPS = 1e-5
ALPHA = 4.0 ** 0.25
NEG = -3.0e38
TWO_PI = 6.283185307179586
PI = 3.141592653589793




class Engine:

    def __init__(self, eng, sem):
        self.eng, self.sem, self.n, self.seen = eng, sem, 0, {}

    def free(self, *tokens):
        for sem, value in tokens:
            if self.seen.get(sem, 0) < value:
                self.eng.wait_ge(sem, value)
                self.seen[sem] = value
        return self.eng

    def at(self, *tokens):
        return self.free(*tokens, (self.sem, self.n))

    def done(self, ins):
        ins.then_inc(self.sem, 1)
        self.n += 1
        return (self.sem, self.n)

    def last(self):
        return (self.sem, self.n)


def together(*works):
    works = list(works)
    while works:
        for w in list(works):
            if next(w, 0) == 0:
                works.remove(w)
        yield


def in_turn(*works):
    works = list(works)
    while works:
        for w in list(works):
            if next(w, 0) == 0:
                works.remove(w)


class Ring:

    def __init__(self, views, sems):
        self.views, self.sems = views, sems
        self.n = len(views)
        self.turn = 0
        self.count = [0] * self.n
        self.readers = [()] * self.n

    def take(self):
        s = self.turn
        while self.readers[s] is None:
            s = (s + 1) % self.n
            assert s != self.turn, "all are held"
        self.turn = (s + 1) % self.n
        r, self.readers[s] = self.readers[s], None
        return s, self.views[s], r

    def loaded(self, s, ins):
        ins.then_inc(self.sems[s], 16)
        self.count[s] += 16
        return (self.sems[s], self.count[s])

    def release(self, s, *tokens):
        self.readers[s] = tokens


def program(nc, A, out, parts=("mod0", "mix0", "peer0", "mod1", "mix1", "peer1", "sb", "mlp0", "dsa", "mlp1")):
    ctx = ExitStack()

    def sb(name, shape, dt=F32):
        return ctx.enter_context(nc.sbuf_tensor(name, shape, dt))

    def sem(name):
        return ctx.enter_context(nc.semaphore(name))

    PE = Engine(nc.tensor, sem("s_pe"))
    V = Engine(nc.vector, sem("s_v"))
    S = Engine(nc.scalar, sem("s_act"))
    G = Engine(nc.gpsimd, sem("s_pool"))
    D = Engine(nc.sync, sem("s_sp"))


    X = sb("X", [128, 4, 1024])
    H = sb("H", [128, 4, 1024])
    HT = sb("HT", [128, 8, 512])
    BIG = sb("BIG", [128, 16384])
    WRt = sb("WR", [128, 5, 2048])
    BCt = sb("BC", [128, 5, 1024])
    NG = 12
    GRt = BIG[:, 0:NG * 1024].rearrange("p (s n) -> p s n", s=NG)
    QT = BIG[:, NG * 1024:16384].rearrange("p (b h t) -> p b h t", b=4, h=8)

    PSt = ctx.enter_context(nc.psum_tensor("PS", [128, 8, 512], F32))
    PS = Ring([PSt[:, i, :] for i in range(4)], [None] * 4)
    PO = Ring([PSt[:, 4 + 2 * i:6 + 2 * i, :] for i in range(2)], [None] * 2)
    WR = Ring([WRt[:, i, :] for i in range(5)], [sem(f"s_w{i}") for i in range(5)])
    BC = Ring([BCt[:, i, :] for i in range(5)], [sem(f"s_b{i}") for i in range(5)])
    GR = Ring([GRt[:, i, :] for i in range(NG)], [sem(f"s_g{i}") for i in range(NG)])

    ident = sb("ident", [128, 128])
    ones = sb("ones", [128, 128])
    iota16 = sb("iota16", [128, 16])
    kbd = sb("kbd", [128, 256])
    stat = sb("stat", [128, 4, 12])
    mv = sb("mv", [128, 4, 2])
    sd = sb("sd", [128, 4])
    rs = sb("rs", [128, 4])
    tmp = sb("tmp", [128, 512])
    scT = sb("scT", [128, 8, 2])
    scS = sb("scS", [128, 8, 2])
    mrow = sb("mrow", [2, 2, 512])
    MR = Ring([mrow[:, i, :] for i in range(2)], [sem(f"s_m{i}") for i in range(2)])
    s_ms = [sem(f"s_ms{i}") for i in range(2)]
    ms_count = [0, 0]
    BRt = sb("BR", [128, 1024])
    BR = Ring([BRt[32 * i:32 * i + 1, :] for i in range(4)], [sem(f"s_r{i}") for i in range(4)])
    BR2 = Ring([], [])
    one_loads = [0]
    DG = Ring([sb(f"dg{i}", [128, 128]) for i in range(3)], [None] * 3)

    V16 = sb("V16", [128, 2, 16])
    I16 = sb("I16", [128, 2, 16], U32)
    I16f = sb("I16f", [128, 2, 16])
    T16 = sb("T16", [128, 16])
    P16 = sb("P16", [128, 16], U32)
    AB = sb("AB", [128, 2, 16], U32)
    ABf = sb("ABf", [128, 2, 16])
    SCU = sb("SCU", [128, 2, 256])
    OH = sb("OH", [128, 2, 16, 16])
    sums = sb("sums", [128, 2])
    IDX = sb("IDX", [128, 4, 16], I32)
    WT = sb("WT", [128, 4, 16])
    ACTV = sb("ACTV", [128, 4, 16])
    small = sb("small", [128, 8])
    SC = sb("SC", [128, 2048])
    cand = sb("cand", [128, 256])
    BR2.__init__([SC[32 * i:32 * i + 1, 1024:2048] for i in range(4)], [sem(f"s_q{i}") for i in range(4)])

    modd = nc.dram_tensor("modd", (2, 2, 6144), F32, kind="Internal").ap()

    def load_once(dst, src, *tokens, by=None):
        s = sem(f"s_one{one_loads[0]}")
        one_loads[0] += 1
        (by or D).free(*tokens).dma_start(dst, src).then_inc(s, 16)
        return (s, 16)

    def everyone():
        return (PE.last(), V.last(), S.last(), G.last())

    def barrier():
        t = everyone()
        for e in (PE, V, S, G):
            e.free(*t)
        return t

    def load_bc(row, *tokens):
        s, view, readers = BC.take()
        t = BC.loaded(s, D.free(*readers, *tokens).dma_start(view, row.partition_broadcast(128)))
        return s, view, t

    def fetch(row, *tokens, ring=BR):
        r, line, readers = ring.take()
        t_r = ring.loaded(r, D.free(*readers, *tokens).dma_start(line, row.unsqueeze(0)))
        return ring, r, line, t_r

    def spread(fetched):
        ring, r, line, t_r = fetched
        s, view, readers = BC.take()
        for n in range(2):
            p, ps, pr = PS.take()
            t = PE.done(PE.free(t_r, *pr).matmul(ps, ones[32 * r:32 * r + 1, :], line[:, n * 512:(n + 1) * 512],
                                                 start=True, stop=True))
            t = S.done(S.free(t, *readers).activation(view[:, n * 512:(n + 1) * 512], ps, ACT.Copy))
            PS.release(p, t)
        ring.release(r, PE.last())
        return s, view, t

    def spread_bc(row, *tokens):
        return spread(fetch(row, *tokens))

    def steps(n):
        for _ in range(n):
            yield

    def load_w(src, p=128):
        s, view, readers = WR.take()
        _, a, b = src.shape
        view = view[0:p, 0:a * b].rearrange("p (a b) -> p a b", a=a)
        t = WR.loaded(s, D.free(*readers).dma_start(view, src))
        return s, view, t

    def load_slab(w, n0, n, p=128, kts=8):
        wv = w.rearrange("(k p) n -> p k n", p=p)
        return [load_w(wv[:, k:k + 4, n0:n0 + n], p) for k in range(0, kts, 4)]

    def group(dst, pairs, *tokens):
        e = PE.free(*tokens)
        last = len(pairs) - 1
        for j, (lhs, rhs, *tk) in enumerate(pairs):
            PE.free(*tk)
            mm = e.matmul(dst, lhs, rhs, start=(j == 0), stop=(j == last))
        return PE.done(mm)

    def group_work(dst, pairs, *tokens, pace=0):
        e = PE.free(*tokens)
        last = len(pairs) - 1
        for j, (lhs, rhs, *tk) in enumerate(pairs):
            PE.free(*tk)
            mm = e.matmul(dst, lhs, rhs, start=(j == 0), stop=(j == last))
            if j == last // 2:
                for _ in range(pace):
                    yield
        return PE.done(mm)

    def release_w(slots, t):
        for s, _, _ in slots:
            WR.release(s, t)

    def rows_work(slab, lhs, blks, n, evac, *tokens, pace=0):
        for b in blks:
            s, ps, readers = PS.take()
            t = yield from group_work(ps[:, 0:n], [(lhs(k, b), slab[k // 4][1][:, k % 4, 0:n], slab[k // 4][2])
                                                   for k in range(4 * len(slab))], *readers, *tokens, pace=pace // 2)
            PS.release(s, evac(b, ps[:, 0:n], t))
            for _ in range(pace - pace // 2):
                yield
        release_w(slab, t)

    def rows_proj(*args):
        for _ in rows_work(*args):
            pass

    def cols_work(slab, cols, rhs, n, evac, *tokens, pace=0):
        for name, c0, m in cols:
            s, ps, readers = PS.take()
            t = yield from group_work(ps[0:m, 0:n], [(slab[k // 4][1][:, k % 4, c0:c0 + m], rhs(k), slab[k // 4][2])
                                                     for k in range(4 * len(slab))], *readers, *tokens, pace=pace // 2)
            PS.release(s, evac(name, ps[0:m, 0:n], t))
            for _ in range(pace - pace // 2):
                yield
        release_w(slab, t)

    def cols_proj(*args):
        for _ in cols_work(*args):
            pass

    flip = [0]

    def copy_out(dst, src, t, *tokens):
        flip[0] ^= 1
        if flip[0]:
            return S.done(S.free(t, *tokens).activation(dst, src, ACT.Copy))
        return V.done(V.free(t, *tokens).tensor_copy(dst, src))

    def to_HT(src, blks, *tokens):
        done = []
        for b in blks:
            for g in range(2):
                s, ps, readers = PS.take()
                e = PE.free(*readers, *tokens)
                for j in range(4):
                    k = 4 * g + j
                    mm = e.transpose(ps[:, j * 128:(j + 1) * 128], src[:, b, k * 128:(k + 1) * 128], ident[:, :])
                t = PE.done(mm)
                t = copy_out(HT[:, 4 * g:4 * g + 4, b * 128:(b + 1) * 128],
                             ps.rearrange("p (a b) -> p a b", a=4), t)
                PS.release(s, t)
                done.append(t)
        return done

    def normalize(src, dst, i, n, *tokens):
        w = min(n, 512)
        for j in range(n // w):
            V.done(V.at(*tokens).bn_stats(stat[:, i, 6 * j:6 * j + 6], src[:, j * w:(j + 1) * w]))
        V.done(V.at().bn_aggr(mv[:, i, :], stat[:, i, 0:6 * (n // w)]))
        t = V.done(V.at().tensor_scalar(mv[:, i, 1:2], mv[:, i, 1:2], EPS, None, ALU.add))
        t = S.done(S.at(t).activation(sd[:, i:i + 1], mv[:, i, 1:2], ACT.Sqrt))
        V.done(V.at(t).reciprocal(rs[:, i:i + 1], sd[:, i:i + 1]))
        return V.done(V.at().tensor_scalar(dst, src, mv[:, i, 0:1], rs[:, i:i + 1], ALU.subtract, ALU.mult))

    def layer_norm_work(pairs, g_row, b_row, *tokens):
        sg, gv, tg = g_row
        sb_, bv, tb = b_row
        for i, (src, dst) in enumerate(pairs):
            normalize(src, dst, i % 4, 1024, *tokens)
            yield
            V.done(V.at(tg).tensor_tensor(dst, dst, gv, ALU.mult))
            t = V.done(V.at(tb).tensor_tensor(dst, dst, bv, ALU.add))
            yield
        BC.release(sg, t)
        BC.release(sb_, t)

    def layer_norm(pairs, g_row, b_row, *tokens):
        for _ in layer_norm_work(pairs, load_bc(g_row), load_bc(b_row), *tokens):
            pass
        return V.last()

    def residual(b, n0, ps, t, gate=None):
        xs = X[:, b, n0:n0 + 512]
        if gate is None:
            return V.done(V.at(t).scalar_tensor_tensor(xs, xs, ALPHA, ps, ALU.mult, ALU.add))
        view, tg = gate
        t = V.done(V.at(t, tg).tensor_tensor(tmp[:, :], ps, view[:, n0:n0 + 512], ALU.mult))
        return V.done(V.at(t).scalar_tensor_tensor(xs, xs, ALPHA, tmp[:, :], ALU.mult, ALU.add)), t

    streams = {0: 0, 1: 0, 2: 1, 3: 1}
    mod_done = {}

    def mod_row(l, j, st):
        return modd[l, st, j * 1024:(j + 1) * 1024]

    def modulated_work(l, j_shift, j_scale, blks):
        for st in (1, 0):
            own = [b for b in blks if streams[b] == st]
            if not own:
                continue
            rows = [fetch(mod_row(l, j, st), *mod_done[l, j]) for j in (j_scale, j_shift)]
            yield from steps(6)
            s1, sc_v, t1 = spread(rows[0])
            yield
            s2, sh_v, t2 = spread(rows[1])
            yield
            for b in own:
                V.done(V.at(t1).scalar_tensor_tensor(H[:, b, :], sc_v, 1.0, X[:, b, :], ALU.add, ALU.mult))
                t = V.done(V.at(t2).tensor_tensor(H[:, b, :], H[:, b, :], sh_v, ALU.add))
                yield
            BC.release(s1, t)
            BC.release(s2, t)
        return t

    def modulated(l, j_shift, j_scale, blks, load=load_bc):
        for st in (1, 0):
            own = [b for b in blks if streams[b] == st]
            if not own:
                continue
            s1, sc_v, t1 = load(mod_row(l, j_scale, st), *mod_done[l, j_scale])
            s2, sh_v, t2 = load(mod_row(l, j_shift, st), *mod_done[l, j_shift])
            for b in own:
                V.done(V.at(t1).scalar_tensor_tensor(H[:, b, :], sc_v, 1.0, X[:, b, :], ALU.add, ALU.mult))
                t = V.done(V.at(t2).tensor_tensor(H[:, b, :], H[:, b, :], sh_v, ALU.add))
            BC.release(s1, t)
            BC.release(s2, t)
        return t

    t_x = []
    xv = A["x"][0].rearrange("(b p) d -> p b d", p=128)
    cv = A["ctx"][0].rearrange("(b p) d -> p b d", p=128)
    t_x.append(load_once(X[:, 0:2, :], xv))
    t_x.append(load_once(X[:, 2:4, :], cv))
    t_sc = load_once(scT[:, :, :], A["cT"])
    G.done(G.at().memset(ones[:, :], 1.0))
    t_ones = G.last()
    G.done(G.at().affine_select(out=ident[:, :], in_=ones[:, :], compare_op=ALU.is_equal, fill=0.0, base=0,
                                pattern=[[-1, 128]], channel_multiplier=1))
    G.done(G.at().iota(iota16[:, :], pattern=[[1, 16]], base=0, channel_multiplier=0,
                       allow_small_or_imprecise_dtypes=True))
    t_const = G.done(G.at().memset(kbd[:, :], 0.0))
    barrier()

    def modulation(l, first, slabs):
        w = A["w_mod"][l]
        for n in range(first, first + slabs):
            slab = load_slab(w, n * 512, 512)
            m, row, readers = MR.take()
            t_b = MR.loaded(m, D.free(*readers).dma_start(
                row, A["b_mod"][l, n * 512:(n + 1) * 512].partition_broadcast(2)))
            s, ps, readers = PS.take()
            e = PE.free(*readers, *t_silu)
            for k in range(8):
                PE.free(slab[k // 4][2])
                mm = e.matmul(ps[0:2, :], scS[:, k, :], slab[k // 4][1][:, k % 4, :], start=(k == 0), stop=(k == 7))
                if k == 3:
                    yield
                    yield
            t = PE.done(mm)
            release_w(slab, t)
            t = V.done(V.at(t, t_b).tensor_tensor(row, row, ps[0:2, :], ALU.add))
            PS.release(s, t)
            S.free(t).dma_start(modd[l, :, n * 512:(n + 1) * 512], row).then_inc(s_ms[m], 16)
            ms_count[m] += 16
            MR.release(m, (s_ms[m], ms_count[m]))
            yield
        for j in range(first // 2, (first + slabs) // 2):
            mod_done[l, j] = ((s_ms[0], ms_count[0]), (s_ms[1], ms_count[1]))

    bs = sb("bs", [128, 8])
    t_bs = load_once(bs[:, :], A["a_b_sT"])

    def chunk_mlp(blks, U, Vv, pace):
        load, ready_bc = (fetch, spread) if pace else (load_bc, lambda row: row)
        if pace:
            t = yield from modulated_work(0, 0, 1, blks)
        else:
            t = modulated(0, 0, 1, blks)
        yield
        t_h = []
        for b in blks:
            t_h += to_HT(H, [b], t)
            yield

        def halves(dst, first):
            for n in range(2):
                yield from rows_work(load_slab(A["a_w_in"][0], (first + n) * 512, 512),
                                     lambda k, b: HT[:, k, b * 128:(b + 1) * 128], blks, 512,
                                     lambda b, ps, t: S.done(S.free(t).activation(
                                         dst(b)[:, n * 512:n * 512 + 512], ps, ACT.Gelu_apprx_tanh)), *t_h, pace=pace)

        norm = [load(A[k][0]) for k in ("a_norm_g", "a_norm_b")]
        yield from halves(Vv, 2)
        t_v = S.last()
        yield from together(halves(U, 0), layer_norm_work([(Vv(b), Vv(b)) for b in blks],
                                                          *(ready_bc(row) for row in norm), t_v))
        t_v = V.last()
        gates = {st: load(mod_row(0, 2, st), *mod_done[0, 2]) for st in sorted({streams[b] for b in blks})} \
            if pace else None
        yield
        yield
        if not pace:
            for _ in modulation(0, 4, 6):
                pass
        t_u = S.last()
        ws, wsv, wst = load_w(A["a_w_sT"])
        for b in blks:
            for hh in range(2):
                s, ps, readers = PS.take()
                e = PE.free(t_v, wst, *readers)
                for j in range(4):
                    h = 4 * hh + j
                    mm = e.matmul(ps[:, j * 128:(j + 1) * 128], wsv[:, h, :], Vv(b)[:, h * 128:(h + 1) * 128],
                                  start=True, stop=True)
                t = PE.done(mm)
                for j in range(4):
                    h = 4 * hh + j
                    us = U(b)[:, h * 128:(h + 1) * 128]
                    t2 = V.done(V.at(t, t_bs, t_u).scalar_tensor_tensor(us, ps[:, j * 128:(j + 1) * 128],
                                                                        bs[:, h:h + 1], us, ALU.add, ALU.mult))
                PS.release(s, t2)
                yield
        WR.release(ws, t)
        for b in blks:
            to_HT(UV(U), [b], t2)
            yield
        if pace:
            gates = {st: spread(row) for st, row in gates.items()}
        else:
            gates = {st: load_bc(mod_row(0, 2, st), *mod_done[0, 2]) for st in sorted({streams[b] for b in blks})}
        yield from mixer_out(A["a_w_out"][0], gates, blks, [V.last(), S.last()], pace)

    class UV:

        def __init__(self, at):
            self.of = at

        def __getitem__(self, key):
            return self.of(key[1])[:, key[2]]

    def mixer_out(w, gates, blks, t_h, pace):
        for n in range(2):
            yield from rows_work(load_slab(w, n * 512, 512), lambda k, b: HT[:, k, b * 128:(b + 1) * 128], blks, 512,
                                 lambda b, ps, t: residual(b, n * 512, ps, t, gates[streams[b]][1:])[1], *t_h,
                                 pace=pace)
        for sg, _, _ in gates.values():
            BC.release(sg, V.last())

    t_qrow = []

    def peer(l, order, more=(), late=None, by_vector=(0, 0, 0, 0)):
        wq = [load_slab(A["p_w_q"][l], n * 512, 512) for n in range(2)]
        settled = set()
        ready = {}
        t_q = {}
        units = [(b, h) for b in order for h in range(8)]
        used = [()] * 4

        def prepare(b, load=fetch, spread=spread):
            rows = [load(A[k][l, 0]) for k in ("ln_g", "ln_b")] + \
                   [load(mod_row(l, j, streams[b]), *mod_done[l, j]) for j in (4, 3)]
            normalize(X[:, b, :], X[:, b, :], 0, 1024)
            yield from steps(6)
            for i in range(2):
                s, view, t = spread(rows[i])
                yield
                BC.release(s, V.done(V.at(t).tensor_tensor(X[:, b, :], X[:, b, :], view, (ALU.mult, ALU.add)[i])))
                yield
            s1, sc_v, t1 = spread(rows[2])
            yield
            s2, sh_v, t2 = spread(rows[3])
            V.done(V.at(t1).scalar_tensor_tensor(H[:, b, :], sc_v, 1.0, X[:, b, :], ALU.add, ALU.mult))
            t = V.done(V.at(t2).tensor_tensor(H[:, b, :], H[:, b, :], sh_v, ALU.add))
            BC.release(s1, t)
            BC.release(s2, t)
            yield
            yield
            t_h = to_HT(H, [b], t)
            yield
            qrow = SC[:, 0:1024]
            t_v = V.last()
            for n in range(2):
                s, ps, readers = PS.take()
                t = group(ps, [(HT[:, k, b * 128:(b + 1) * 128], wq[n][k // 4][1][:, k % 4, :], wq[n][k // 4][2])
                               for k in range(8)], *readers, *t_h)
                t = S.done(S.free(t, t_v).activation(qrow[:, n * 512:(n + 1) * 512], ps, ACT.Copy))
                PS.release(s, t)
                yield
                yield
                yield
                yield
                s, ps, readers = PS.take()
                e = PE.free(t, *readers)
                for j in range(4):
                    h = 4 * n + j
                    mm = e.transpose(ps[:, j * 128:(j + 1) * 128], qrow[:, h * 128:(h + 1) * 128], ident[:, :])
                t = PE.done(mm)
                t = S.done(S.free(t).activation(QT[:, b, 4 * n:4 * n + 4, :], ps.rearrange("p (h t) -> p h t", h=4),
                                                ACT.Copy))
                PS.release(s, t)
                yield
            t_q[b] = t

        def route(u):
            b, h = units[u]
            i = u % 4
            sc = SCU[:, u % 2, :]
            s, ps, readers = PS.take()
            t = PE.done(PE.free(*t_k, t_q[b], *readers).matmul(ps[:, 0:256], QT[:, b, h, :], kbd[:, :],
                                                               start=True, stop=True))
            t = S.done(S.free(t, V.last()).activation(sc, ps[:, 0:256], ACT.Copy))
            PS.release(s, t)
            yield
            V.free(t)
            for r in range(2):
                scr = sc[:, r * 128:(r + 1) * 128]
                V.done(V.at().max(V16[:, r, 0:8], scr))
                V.done(V.at().max_index(I16[:, r, 0:8], V16[:, r, 0:8], scr))
                V.done(V.at().match_replace(scr, V16[:, r, 0:8], scr, NEG))
                yield
                V.done(V.at().max(V16[:, r, 8:16], scr))
                V.done(V.at().max_index(I16[:, r, 8:16], V16[:, r, 8:16], scr))
                yield
            V.done(V.at().tensor_copy(I16f[:, :, :], I16[:, :, :]))
            c3 = cand[:, :].rearrange("p (a b) -> p a b", a=16)
            V.done(V.at().tensor_tensor(c3, V16[:, 0, :].unsqueeze(2).to_broadcast([128, 16, 16]),
                                        V16[:, 1, :].unsqueeze(1).to_broadcast([128, 16, 16]), ALU.add))
            V.done(V.at().max(T16[:, 0:8], cand[:, :]))
            yield
            V.done(V.at().max_index(P16[:, 0:8], T16[:, 0:8], cand[:, :]))
            V.done(V.at().match_replace(cand[:, :], T16[:, 0:8], cand[:, :], NEG))
            yield
            V.done(V.at().max(T16[:, 8:16], cand[:, :]))
            V.done(V.at().max_index(P16[:, 8:16], T16[:, 8:16], cand[:, :]))
            yield
            V.done(V.at().tensor_scalar(AB[:, 0, :], P16[:, :], 4, None, ALU.logical_shift_right))
            V.done(V.at().tensor_scalar(AB[:, 1, :], P16[:, :], 15, None, ALU.bitwise_and))
            V.done(V.at().tensor_copy(ABf[:, :, :], AB[:, :, :]))
            yield
            V.done(V.at().tensor_tensor(OH[:, :, :, :], ABf[:, :, :].unsqueeze(3).to_broadcast([128, 2, 16, 16]),
                                        iota16[:, :].unsqueeze(1).unsqueeze(1).to_broadcast([128, 2, 16, 16]),
                                        ALU.is_equal))
            V.done(V.at().tensor_tensor(OH[:, :, :, :], OH[:, :, :, :],
                                        I16f[:, :, :].unsqueeze(2).to_broadcast([128, 2, 16, 16]), ALU.mult))
            yield
            V.done(V.at().tensor_reduce(ABf[:, :, :], OH[:, :, :, :], AX, ALU.add))
            V.done(V.at().tensor_scalar(ABf[:, 0, :], ABf[:, 0, :], 128.0, float(l * 16384), ALU.mult, ALU.add))
            t_idx = V.done(V.at(*used[i]).tensor_tensor(IDX[:, i, :], ABf[:, 0, :], ABf[:, 1, :], ALU.add))
            w = WT[:, i, :]
            t = V.done(V.at().tensor_scalar(w, T16[:, :], T16[:, 0:1], None, ALU.subtract))
            t = S.done(S.at(t).activation(w, w, ACT.Exp, accum_out=sums[:, 0:1]))
            ready[u] = t_idx
            yield
            V.done(V.at(t).reciprocal(sums[:, 1:2], sums[:, 0:1]))
            V.done(V.at().tensor_scalar(w, w, sums[:, 1:2], None, ALU.mult))

        def gather(table, u, j):
            s, view, readers = GR.take()
            e = G.free(*readers, ready[u])
            t = GR.loaded(s, e.indirect_dma_start(view, None, table, bass.IndirectOffsetOnAxis(
                ap=IDX[:, u % 4, j:j + 1], axis=0)))
            return s, view, t

        def prepare_rest():
            if late is not None:
                for slab in wq:
                    release_w(slab, PE.last())
                yield from late
                wq[:] = [load_slab(A["p_w_q"][l], n * 512, 512) for n in range(2)]
            for b in order[1:]:
                yield from prepare(b)
            for slab in wq:
                release_w(slab, PE.last())
            t_qrow[:] = [PE.last(), V.last(), S.last()]

        def finish(b, po, acc, t, rows):
            sg, view, tgate = spread(rows[0])
            yield
            if acc is not None:
                for half in range(2):
                    t = V.done(V.at(t).tensor_tensor(po[1][:, half, :], po[1][:, half, :],
                                                     acc[1][:, half * 512:(half + 1) * 512], ALU.add))
                BC.release(acc[0], t)
            for half in range(2):
                _, tp = residual(b, half * 512, po[1][:, half, :], t, (view, tgate))
            BC.release(sg, tp)
            PO.release(po[0], tp)
            yield
            normalize(X[:, b, :], X[:, b, :], 0, 1024)
            yield
            for i in (1, 2):
                s, view, t = spread(rows[i])
                yield
                BC.release(s, V.done(V.at(t).tensor_tensor(X[:, b, :], X[:, b, :], view, (None, ALU.mult, ALU.add)[i])))
                yield
            settled.add(b)

        def others():
            for needs, work in more:
                while not needs <= settled:
                    yield
                yield from work

        for _ in prepare(order[0], load_bc, lambda row: row):
            pass
        t_qrow[:] = []
        t_k = [load_once(kbd[0:64, 0:128], A["keysT"][l, 0], PE.last(), by=S),
               load_once(kbd[64:128, 128:256], A["keysT"][l, 1], by=S)]
        for _ in route(0):
            pass
        G.free(*everyone())
        rest, extra, ends = prepare_rest(), others(), iter(())
        for u in range(len(units) + 1):
            while u + 1 < len(units) and units[u + 1][0] not in t_q:
                next(rest)
            nxt = route(u + 1) if u + 1 < len(units) else iter(())
            if u:
                b, h = units[u - 1]
                nv = by_vector[order.index(b)]
                if h == 0:
                    acc = None
                    po = PO.take()
                    PE.free(*po[2])
                if h == 7:
                    rows = [fetch(mod_row(l, 5, streams[b]), *mod_done[l, 5], ring=BR2),
                            fetch(A["ln_g"][l, 1], ring=BR2), fetch(A["ln_b"][l, 1], ring=BR2)]
                av = ACTV[:, (u - 1) % 4, :]
                t = S.done(S.at(V.last()).activation(av, av, ACT.Gelu_apprx_tanh))
                t_a = V.done(V.at(t).tensor_tensor(av, av, WT[:, (u - 1) % 4, :], ALU.mult))
            for j in range(16):
                if u < len(units):
                    s, view, t = gather(A["p_u"], u, j)
                    t = V.done(V.free(t).tensor_tensor_reduce(view, view, H[:, units[u][0], :], 1.0, 0.0, ALU.mult,
                                                              ALU.add, ACTV[:, u % 4, j:j + 1]))
                    GR.release(s, t)
                if u:
                    s, view, t = gather(A["p_v"], u - 1, j)
                    t_last = t
                    if (j * nv) // 16 != (j + 1) * nv // 16 and j < 15:
                        if acc is None:
                            acc = BC.take()
                            t = V.done(V.at(t, *acc[2]).tensor_scalar(acc[1], view, av[:, j:j + 1], None, ALU.mult))
                        else:
                            t = V.done(V.at(t).scalar_tensor_tensor(acc[1], view, av[:, j:j + 1], acc[1], ALU.mult,
                                                                    ALU.add))
                        GR.release(s, t)
                    else:
                        sdg, dg, dr = DG.take()
                        td = S.done(S.free(t_a, *dr).activation(dg[:, :], ident[:, :], ACT.Copy, scale=av[:, j:j + 1]))
                        for half in range(2):
                            mm = PE.free(t, td).matmul(po[1][:, half, :], dg[:, :],
                                                       view[:, half * 512:(half + 1) * 512],
                                                       start=(h == 0 and j == 0), stop=(h == 7 and j == 15))
                        t = PE.done(mm)
                        GR.release(s, t)
                        DG.release(sdg, t)
                next(nxt, None)
                if u == 0 and len(order) > 2:
                    next(rest, None)
                for back in (ends, rest):
                    if next(back, 0) != 0:
                        break
                else:
                    next(extra, None)
            for _ in nxt:
                pass
            if u:
                used[(u - 1) % 4] = (t_last,)
                if h == 7:
                    for _ in ends:
                        pass
                    ends = finish(b, po, acc, t, rows)
        for _ in ends:
            pass
        for _ in extra:
            pass
        barrier()

    gla_tri = [SC[:, 0:128], SC[:, 128:256]]

    def gla_tiles():
        tri = gla_tri
        G.done(G.at(*t_qrow).affine_select(
            out=tri[0], in_=ones[:, :], compare_op=ALU.is_ge, fill=0.0, base=0, pattern=[[1, 128]],
            channel_multiplier=-1))
        G.done(G.at().memset(SC[0:64, 64:128], 0.0))
        G.done(G.at().affine_select(out=tri[1], in_=ones[:, :], compare_op=ALU.is_ge, fill=0.0, base=0,
                                    pattern=[[-1, 128]], channel_multiplier=1))
        G.done(G.at().memset(SC[64:128, 128:192], 0.0))
        return G.done(G.at().memset(SC[32:33, 256:768], 1.0))

    glT = SC[0:33, 256:768]

    def gla_gates(blks, wslot, bT, raw, t_gl, *tokens, pace=1):
        prev = {}
        for b in blks:
            gt = raw(b)
            for j in range(2):
                s, ps, readers = PS.take()
                t = group(ps, [(glT[:, b * 128:(b + 1) * 128], wslot[1][:, j, :])], *t_gl, wslot[2], *tokens, *readers)
                gs = gt[:, j * 512:(j + 1) * 512]
                S.done(S.at(t, *prev.get(b % 2, ()), *tokens).activation(gs, ps, ACT.Abs))
                S.done(S.at().activation(gs, gs, ACT.Exp, scale=-1.0))
                t = S.done(S.at().activation(gs, gs, ACT.Ln, bias=1.0))
                t = V.done(V.at(t).scalar_tensor_tensor(gs, ps, 0.0, gs, ALU.min, ALU.subtract))
                PS.release(s, t)
                t_gg = t
                yield from steps(pace)
                s, ps, readers = PS.take()
                e = PE.free(t_gg, *readers)
                for h in range(4):
                    mm = e.matmul(ps[:, h * 128:(h + 1) * 128], gs[:, h * 128:(h + 1) * 128], gla_tri[j],
                                  start=True, stop=True)
                t = PE.done(mm)
                prev[b % 2] = (t,)
                t = S.done(S.at(t).activation(bT(j, b), ps.rearrange("p (h t) -> p h t", h=4), ACT.Copy,
                                              scale=1.0 / 16.0))
                PS.release(s, t)
                yield from steps(pace)
        WR.release(wslot[0], PE.last())

    def gla_ctx():
        w = A["b_w_in"][0]
        wv = w.rearrange("(k p) n -> p k n", p=128)
        hT = lambda k: HT[:, k, 256:512]
        t = yield from modulated_work(1, 0, 1, [2, 3])
        yield
        t_h = []
        for b in (2, 3):
            t_h += to_HT(H, [b], t)
            yield
        t_g = gla_tiles()
        slab = [load_w(wv[:, k:k + 4, 3072:3104]) for k in (0, 4)]
        yield from cols_work(slab, [(0, 0, 32)], hT, 256, lambda j, ps, t: S.done(
            S.free(t, t_g).activation(glT[0:32, 256:512], ps, ACT.Copy)), *t_h, pace=2)
        bT = H[:, 2:4, :].rearrange("p b n -> p (b n)").rearrange("p (u t) -> p u t", u=8)
        yield from gla_gates([2, 3], load_w(A["wgate"], 33),
                             lambda j, b: bT[:, 4 * j:4 * j + 4, (b - 2) * 128:(b - 1) * 128],
                             lambda b: X[:, b, :], (S.last(),), t_g, pace=3)
        kT = BIG[:, 14336:15360].rearrange("p (h t) -> p h t", h=4)
        KD, st = BIG[:, 15360:15616], [BIG[:, 15616 + 256 * i:15872 + 256 * i] for i in range(2)]
        KE = BIG[:, 16128:16384].rearrange("p (b t) -> p b t", b=2)
        dc = ctxdc[:, :]
        v_ = X[:, 2:4, :]
        t_old = V.last()
        yield from cols_work(load_slab(w, 512, 512), [(h, h * 128, 128) for h in range(4)], hT, 256,
                             lambda h, ps, t: S.done(S.free(t).activation(kT[:, h, :], ps, ACT.Copy)), pace=3)
        for n in range(2):
            yield from rows_work(load_slab(w, 1024 + n * 512, 512), lambda k, b: HT[:, k, b * 128:(b + 1) * 128],
                                 [2, 3], 512, lambda b, ps, t: S.done(S.free(t, t_old).activation(
                                     v_[:, b - 2, n * 512:n * 512 + 512], ps, ACT.Copy)), pace=5)
        t_p = S.last()
        t_kd = PE.last()
        for h in range(4):
            for j in range(2):
                b3 = bT[:, 4 * j + h, :].rearrange("p (c t) -> p c t", t=64)
                end = 63 if j == 0 else 0
                t = V.done(V.at(t_p, t_kd).tensor_tensor(
                    KD.rearrange("p (c t) -> p c t", t=64), b3[:, :, end:end + 1].to_broadcast([128, 4, 64]), b3,
                    ALU.subtract))
                t = S.done(S.at(t).activation(KD, KD, ACT.Exp))
                t_dc = S.done(S.at().activation(dc, b3[:, :, end], ACT.Exp))
                yield from steps(2)
                t = V.done(V.at(t).tensor_tensor(KD, KD, kT[:, h, :], ALU.mult))
                s, ps, readers = PS.take()
                e = PE.free(t, *readers)
                for b in range(2):
                    mm = e.transpose(ps[:, b * 128:(b + 1) * 128], KD[:, b * 128:(b + 1) * 128], ident[:, :])
                t = t_kd = PE.done(mm)
                t_ke = S.done(S.free(t).activation(KE, ps[:, 0:256].rearrange("p (b t) -> p b t", b=2), ACT.Copy))
                PS.release(s, t_ke)
                yield from steps(2)
                state = None
                for n in range(4):
                    c = n if j == 0 else 3 - n
                    b, a = c // 2, c % 2
                    rows = slice(64 * a, 64 * a + 64)
                    s, ps, readers = PS.take()
                    t = group(ps[:, 0:256], [(KE[rows, b, :], v_[rows, b, h * 256:(h + 1) * 256])], t_ke, *readers)
                    new = HT[:, 4 * j + h, 256:512] if n == 3 else st[n % 2]
                    if n == 0:
                        t = V.done(V.at(t).tensor_copy(new, ps[:, 0:256]))
                    else:
                        t = V.done(V.at(t, t_dc).scalar_tensor_tensor(new, state, dc[:, c:c + 1], ps[:, 0:256],
                                                                      ALU.mult, ALU.add))
                    PS.release(s, t)
                    state = new
                    yield

    ctxdc = sb("ctxdc", [128, 4])

    def gla():
        barrier()
        tri = gla_tri
        q_ = BIG[:, 0:1024].rearrange("p (h t) -> p h t", h=4)
        k_ = BIG[:, 1024:2048].rearrange("p (h t) -> p h t", h=4)
        v_ = BIG[:, 2048:4096].rearrange("p (b n) -> p b n", b=2)
        bT = BIG[:, 4096:6144].rearrange("p (u t) -> p u t", u=8)
        QI = BIG[:, 6144:7168].rearrange("p (u t) -> p u t", u=4)
        ATT = BIG[:, 7168:8192].rearrange("p (u b t) -> p u b t", u=4, b=2)
        KE = BIG[:, 8192:9216].rearrange("p (u b t) -> p u b t", u=4, b=2)
        SS = BIG[:, 9216:10752].rearrange("p (u n) -> p u n", u=6)
        EB, EN, KI, KD = (BIG[:, 10752 + 512 * i:11264 + 512 * i].rearrange("p (a t) -> p a t", a=2)
                          for i in range(4))
        dcs = BIG[:, 12800:12816].rearrange("p (u c) -> p u c", u=4)
        gst = BIG[:, 15360:15408].rearrange("p (i c) -> p i c", i=8)
        gmv = BIG[:, 15408:15424].rearrange("p (i c) -> p i c", i=8)
        gsd = BIG[:, 15424:15432]
        r_ = H[:, 0:2, :]
        Y = H[:, 2:4, :]
        G.done(G.at().memset(BIG[:, 7168:8192], 0.0))
        t_g = gla_tiles()
        t = modulated(1, 0, 1, range(2))
        t_h = to_HT(H, range(2), t)
        w = A["b_w_in"][0]
        hT = lambda k: HT[:, k, 0:256]
        wv = w.rearrange("(k p) n -> p k n", p=128)
        slab = [load_w(wv[:, k:k + 4, 3072:3104]) for k in (0, 4)]
        cols_proj(slab, [(0, 0, 32)], hT, 256,
                  lambda j, ps, t: S.done(S.free(t, t_g).activation(glT[0:32, 0:256], ps, ACT.Copy)), *t_h)
        gates = gla_gates([0, 1], load_w(A["wgate"], 33),
                          lambda j, b: bT[:, 4 * j:4 * j + 4, b * 128:(b + 1) * 128],
                          lambda b: Y[:, b, :], (S.last(),), t_g)
        next(gates)

        def to(dst):
            return lambda name, ps, t: copy_out(dst(name), ps, t)

        def projections():
            yield from cols_work(load_slab(w, 0, 512), [(h, h * 128, 128) for h in range(4)], hT, 256,
                                 to(lambda h: q_[:, h, :]), pace=1)
            yield from cols_work(load_slab(w, 512, 512), [(h, h * 128, 128) for h in range(4)], hT, 256,
                                 to(lambda h: k_[:, h, :]), pace=1)
            for n in range(2):
                yield from rows_work(load_slab(w, 1024 + n * 512, 512), lambda k, b: HT[:, k, b * 128:(b + 1) * 128],
                                     range(2), 512, lambda b, ps, t: copy_out(v_[:, b, n * 512:n * 512 + 512], ps, t),
                                     pace=1)

        in_turn(projections(), gates)
        t_all = everyone()
        PE.free(*t_all)
        V.free(*t_all)
        S.free(*t_all)

        def readout():
            for n in range(2):
                yield from rows_work(load_slab(w, 2048 + n * 512, 512), lambda k, b: HT[:, k, b * 128:(b + 1) * 128],
                                     range(2), 512, lambda b, ps, t: S.done(S.free(t).activation(
                                         r_[:, b, n * 512:n * 512 + 512], ps, ACT.Silu)), pace=3)

        tk = {}

        def prep(h):
            for j in range(2):
                i = (h % 2) * 2 + j
                bt = bT[:, 4 * j + h, :]
                b3 = bt.rearrange("p (c t) -> p c t", t=64)
                end = 63 if j == 0 else 0
                kd3 = KD[:, j, :].rearrange("p (c t) -> p c t", t=64)
                old = tk.get((h - 1, j), ())
                t1 = V.done(V.at(*old).tensor_tensor(kd3, b3[:, :, end:end + 1].to_broadcast([128, 4, 64]), b3,
                                                     ALU.subtract))
                t1 = S.done(S.at(t1).activation(KD[:, j, :], KD[:, j, :], ACT.Exp))
                t2 = S.done(S.at().activation(EB[:, j, :], bt, ACT.Exp))
                t3 = S.done(S.at().activation(EN[:, j, :], bt, ACT.Exp, scale=-1.0))
                t_dc = S.done(S.at().activation(dcs[:, i, :], b3[:, :, end], ACT.Exp))
                yield
                t_kd = V.done(V.at(t1).tensor_tensor(KD[:, j, :], KD[:, j, :], k_[:, h, :], ALU.mult))
                s, ps, readers = PS.take()
                e = PE.free(t_kd, *readers)
                for b in range(2):
                    mm = e.transpose(ps[:, b * 128:(b + 1) * 128], KD[:, j, b * 128:(b + 1) * 128], ident[:, :])
                t = PE.done(mm)
                t_ke = S.done(S.free(t).activation(KE[:, i, :, :], ps[:, 0:256].rearrange("p (b t) -> p b t", b=2),
                                                   ACT.Copy))
                PS.release(s, t_ke)
                yield
                V.done(V.at(t2).scalar_tensor_tensor(QI[:, i, :], q_[:, h, :], 128.0 ** -0.5, EB[:, j, :],
                                                     ALU.mult, ALU.mult))
                t = V.done(V.at(t3).tensor_tensor(KI[:, j, :], k_[:, h, :], EN[:, j, :], ALU.mult))
                yield
                s, ps, readers = PS.take()
                e = PE.free(t, *readers)
                for b in range(2):
                    mm = e.matmul(ps[:, b * 128:(b + 1) * 128], KI[:, j, b * 128:(b + 1) * 128],
                                  QI[:, i, b * 128:(b + 1) * 128], start=True, stop=True)
                t = PE.done(mm)
                tk[h, j] = (t,)
                for b in range(2):
                    t_at = V.done(V.at(t).copy_predicated(ATT[:, i, b, :], tri[j].bitcast(I32),
                                                          ps[:, b * 128:(b + 1) * 128]))
                PS.release(s, t_at)
                tk[h, j, "ready"] = (t_at, t_ke, t_dc)
                yield

        orders = [[(0, 0), (0, 1), (1, 0), (1, 1)], [(1, 1), (1, 0), (0, 1), (0, 0)]]

        def chain(h):
            so, po, readers = PO.take()
            PE.free(*readers)
            hv = slice(h * 256, (h + 1) * 256)
            for j in range(2):
                e = PE.free(*tk[h, j, "ready"])
                for b in range(2):
                    mm = e.matmul(po[:, b, 0:256], ATT[:, (h % 2) * 2 + j, b, :], v_[:, b, hv],
                                  start=(j == 0), stop=False, skip_group_check=True)
            t_read = PE.done(mm)
            yield
            state = [(HT[:, 4 * j + h, 256:512], t_read) for j in range(2)]
            reads = [{}, {}]
            for n in range(4):
                for j in range(2):
                    i = (h % 2) * 2 + j
                    b, a = orders[j][n]
                    rows = slice(64 * a, 64 * a + 64)
                    if n < 3:
                        s, ps, readers = PS.take()
                        t = group(ps[:, 0:256], [(KE[rows, i, b, :], v_[rows, b, hv])], *readers)
                    tc = slice(b * 128 + a * 64, b * 128 + a * 64 + 64)
                    mm = PE.free(state[j][1]).matmul(po[rows, b, 0:256], QI[:, i, tc], state[j][0], start=False,
                                                     stop=False, skip_group_check=True)
                    PE.done(mm)
                    if n < 3:
                        new = SS[:, 3 * j + n, :]
                        c = 2 * b + a
                        t_st = V.done(V.at(t, t_read).scalar_tensor_tensor(
                            new, state[j][0], dcs[:, i, c:c + 1], ps[:, 0:256], ALU.mult, ALU.add))
                        PS.release(s, t_st)
                        state[j] = (new, t_st)
                    yield
            t = S.done(S.at(PE.last()).activation(Y[:, :, hv], po[:, :, 0:256], ACT.Copy))
            PO.release(so, t)
            yield

        rd = readout()
        in_turn(prep(0), (next(rd, None) for _ in range(4)))
        for h in range(4):
            if h < 3:
                in_turn(chain(h), prep(h + 1), (next(rd, None) for _ in range(6)))
            else:
                for _ in rd:
                    pass
                in_turn(chain(h))
        t_y = S.last()
        for b in range(2):
            rows = [A["b_gn_g"][0]], [mod_row(1, 2, 0), *mod_done[1, 2]]
            if b:
                yield
                rows = [fetch(*row) for row in rows]
                yield from steps(5)
            four = slice(4 * b, 4 * b + 4)
            for h in range(4):
                V.done(V.at(t_y).bn_stats(gst[:, 4 * b + h, :], Y[:, b, h * 256:(h + 1) * 256]))
            for i in range(4 * b, 4 * b + 4):
                V.done(V.at().bn_aggr(gmv[:, i, :], gst[:, i, :]))
            t = V.done(V.at().tensor_scalar(gsd[:, four], gmv[:, four, 1], EPS, None, ALU.add))
            t = S.done(S.at(t).activation(gsd[:, four], gsd[:, four], ACT.Sqrt))
            if b:
                yield
            V.done(V.at(t).reciprocal(gsd[:, four], gsd[:, four]))
            for h in range(4):
                i = 4 * b + h
                y = Y[:, b, h * 256:(h + 1) * 256]
                V.done(V.at().tensor_scalar(y, y, gmv[:, i, 0:1], gsd[:, i:i + 1], ALU.subtract, ALU.mult))
            sgn, gnv, tgn = spread(rows[0]) if b else load_bc(*rows[0])
            V.done(V.at(tgn).tensor_tensor(Y[:, b, :], Y[:, b, :], gnv, ALU.mult))
            t = V.done(V.at().tensor_tensor(Y[:, b, :], Y[:, b, :], r_[:, b, :], ALU.mult))
            BC.release(sgn, t)
            if b:
                yield from steps(2)
            t_h = to_HT(Y, [b], t, t_y)
            gate = spread(rows[1]) if b else load_bc(*rows[1])
            yield from mixer_out(A["b_w_out"][0], {0: gate}, [b], t_h, 4 * b)

    def sb_ssm():
        barrier()
        t_h = to_HT(X, range(2))
        zz, ll, nn = (BIG[:, 2048 * i:2048 * i + 2048] for i in range(3))
        ZZ, LL, NN = (a.rearrange("p (h n) -> p h n", h=4) for a in (zz, ll, nn))
        q_ = BIG[:, 6144:7168].rearrange("p (h t) -> p h t", h=4)
        k_ = BIG[:, 7168:8192].rearrange("p (h t) -> p h t", h=4)
        XR = BIG[:, 8192:12288].rearrange("p (j t) -> p j t", j=16)
        XI = BIG[:, 12288:16384].rearrange("p (j t) -> p j t", j=16)
        XR4 = BIG[:, 8192:12288].rearrange("p (j c t) -> p j c t", j=16, c=16)
        XI4 = BIG[:, 12288:16384].rearrange("p (j c t) -> p j c t", j=16, c=16)
        AO = X[:, 2, :].rearrange("p (h t) -> p h t", h=4)
        TT = Ring([X[:, 3, 512 * i:512 * i + 512] for i in range(2)], [None] * 2)
        v_ = H[:, 0, :].rearrange("p (b n) -> p b n", b=2)
        uT = H[:, 1, :].rearrange("p (c t) -> p c t", c=4)
        yT = H[:, 2, :].rearrange("p (c t) -> p c t", c=4)
        zT = H[:, 3, :].rearrange("p (c t) -> p c t", c=4)
        strict = SC[:, 0:128]
        uu = [SC[:, a:a + 256].rearrange("p (j c) -> p j c", j=16) for a in (128, 384, 1152, 1408)]
        PW = SC[:, 640:1152].rearrange("p (i t j) -> p i t j", i=2, t=16)
        t_m = G.done(G.at().affine_select(out=strict, in_=ones[:, :], compare_op=ALU.is_gt, fill=0.0, base=0,
                                          pattern=[[-1, 128]], channel_multiplier=1))
        c_ = sb("s5c", [128, 13, 16])
        cl = [c_[:, i, :] for i in range(13)]
        dT = sb("s5d", [128, 4])
        bglu = sb("bglu", [128, 4])
        t_l = [load_once(cl[0], A["ldt"]), load_once(cl[1], A["lre"]), load_once(cl[2], A["lim"])]
        t_d = load_once(dT[:, :], A["s5dT"])
        t_bg = load_once(bglu[:, :], A["bgluT"])
        w = A["sb_ssm_w_in_2"][0]
        hT = lambda k: HT[:, k, 0:256]

        def evac(dst):
            return lambda i, ps, t: S.done(S.free(t).activation(dst(i), ps, ACT.Copy))

        quarters = [(i, i * 128, 128) for i in range(4)]
        cols_proj(load_slab(w, 1536, 512), quarters, hT, 256, evac(lambda i: uT[:, i, :]), *t_h)
        t_u = S.last()

        def vt(o, a, b, op):
            return V.done(V.at().tensor_tensor(o, a, b, op))

        def vs(o, a, s1, s2, o1, o2=None):
            if o2 is None:
                return V.done(V.at().tensor_scalar(o, a, s1, None, o1))
            return V.done(V.at().tensor_scalar(o, a, s1, s2, o1, o2))

        dt, lr, li, ar, ai, cr, ci, den, x0, x1, x2, x3 = cl[0:12]
        t = S.done(S.at(*t_l).activation(dt, dt, ACT.Exp))
        V.free(t, *t_l)
        t = vt(x0, lr, dt, ALU.mult)
        t = S.done(S.at(t).activation(x0, x0, ACT.Exp))
        V.free(t)
        vt(x1, li, dt, ALU.mult)
        vs(x2, x1, 1.0 / TWO_PI, 12582912.0, ALU.mult, ALU.add)
        vs(x2, x2, -12582912.0, None, ALU.add)
        for c in (6.28125, 0.0019350051879882812, 3.0199159819567e-07):
            V.done(V.at().scalar_tensor_tensor(x1, x2, -c, x1, ALU.mult, ALU.add))
        vs(x1, x1, PI - 1e-6, -(PI - 1e-6), ALU.min, ALU.max)
        t = V.last()
        t = S.done(S.at(t).activation(x2, x1, ACT.Abs))
        V.free(t)
        t = vs(x2, x2, -1.0, PI / 2, ALU.mult, ALU.add)
        S.done(S.at(t).activation(x2, x2, ACT.Sin))
        t = S.done(S.at().activation(x1, x1, ACT.Sin))
        V.free(t)
        vt(ar, x0, x2, ALU.mult)
        vt(ai, x0, x1, ALU.mult)
        vt(x0, lr, lr, ALU.mult)
        vt(x1, li, li, ALU.mult)
        vt(den, x0, x1, ALU.add)
        V.done(V.at().reciprocal(den, den))
        vs(x3, ar, -1.0, None, ALU.add)
        vt(x0, x3, lr, ALU.mult)
        vt(x1, ai, li, ALU.mult)
        vt(x0, x0, x1, ALU.add)
        vt(cr, x0, den, ALU.mult)
        vt(x0, ai, lr, ALU.mult)
        vt(x1, x3, li, ALU.mult)
        vt(x0, x0, x1, ALU.subtract)
        t_co = vt(ci, x0, den, ALU.mult)

        def vf(o, a, b, op, *tokens):
            return V.done(V.free(*tokens).tensor_tensor(o, a, b, op))

        def cmul(pr, pi, sr, si, a, prev, out=None):
            o = out or (a[0], a[2])
            vf(a[0], sr, pr, ALU.mult, prev[0])
            t2 = vf(a[1], si, pi, ALU.mult, prev[1])
            vf(a[2], sr, pi, ALU.mult)
            t4 = vf(a[3], si, pr, ALU.mult)
            return vf(o[0], a[0], a[1], ALU.subtract, t2), vf(o[1], a[2], a[3], ALU.add, t4)

        def cmadd(dr, di, pr, pi, sr, si, a, prev):
            t5, t6 = cmul(pr, pi, sr, si, a, prev)
            return vf(dr, dr, a[0], ALU.add, t5), vf(di, di, a[2], ALU.add, t6)

        def drive():
            wb = [load_w(A["s5_br"]), load_w(A["s5_bi"])]
            for j in range(16):
                s, ps, readers = PS.take()
                PE.free(t_u, *readers)
                for i in range(2):
                    t = group(ps[:, i * 256:(i + 1) * 256], [(wb[i][1][:, j, :], uT[:, j // 4, :])], wb[i][2])
                P, Q = ps[:, 0:256], ps[:, 256:512]
                st, tt, rr = TT.take()
                S.done(S.free(t, t_co, *rr).activation(tt[:, 0:256], Q, ACT.Copy, scale=ci[:, j:j + 1]))
                t = S.done(S.free().activation(tt[:, 256:512], P, ACT.Copy, scale=ci[:, j:j + 1]))
                V.done(V.at(t).scalar_tensor_tensor(XR[:, j, :], P, cr[:, j:j + 1], tt[:, 0:256],
                                                    ALU.mult, ALU.subtract))
                t = V.done(V.free().scalar_tensor_tensor(XI[:, j, :], Q, cr[:, j:j + 1], tt[:, 256:512],
                                                         ALU.mult, ALU.add))
                PS.release(s, t)
                TT.release(st, t)
            release_w(wb, PE.last())

        def state_space():
            V.done(V.at().tensor_copy(PW[:, 0, 0, :], ar))
            V.done(V.at().tensor_copy(PW[:, 1, 0, :], ai))
            prev = (V.last(), V.last())
            for n in range(1, 16):
                prev = cmul(ar, ai, PW[:, 0, n - 1, :], PW[:, 1, n - 1, :], (x0, x1, x2, x3), prev,
                            (PW[:, 0, n, :], PW[:, 1, n, :]))
                if n % 2:
                    yield
            bc = lambda ap, n: ap.unsqueeze(2).to_broadcast([128, 16, n])
            prev = (V.last(), V.last())
            for n in range(1, 16):
                prev = cmadd(XR4[:, :, :, n], XI4[:, :, :, n], bc(ar, 16), bc(ai, 16), XR4[:, :, :, n - 1],
                             XI4[:, :, :, n - 1], uu, prev)
                yield
            for c in range(1, 16):
                prev = cmadd(XR4[:, :, c, 15], XI4[:, :, c, 15], PW[:, 0, 15, :], PW[:, 1, 15, :],
                             XR4[:, :, c - 1, 15], XI4[:, :, c - 1, 15], (x0, x1, x2, x3), prev)
                if c % 2:
                    yield
            for n in range(15):
                prev = cmadd(XR4[:, :, 1:16, n], XI4[:, :, 1:16, n], bc(PW[:, 0, n, :], 15), bc(PW[:, 1, n, :], 15),
                             XR4[:, :, 0:15, 15], XI4[:, :, 0:15, 15], [u[:, :, 0:15] for u in uu], prev)
                yield

        def both(k, b):
            bl = slice(b * 128, (b + 1) * 128)
            return AO[:, k, bl] if k < 4 else yT[:, k - 4, bl]

        begun = []

        def attention():
            cols_proj(load_slab(w, 0, 512), quarters, hT, 256, evac(lambda i: q_[:, i, :]))
            yield from steps(3)
            cols_proj(load_slab(w, 512, 512), quarters, hT, 256, evac(lambda i: k_[:, i, :]))
            yield from steps(3)
            rows_proj(load_slab(w, 1024, 512), lambda k, b: HT[:, k, b * 128:(b + 1) * 128], range(2), 512,
                      evac(lambda b: v_[:, b, :]))
            t_p = S.last()
            yield from steps(5)
            keep = dict(compare_op=ALU.is_gt, fill=0.0, base=0, pattern=[[0, 4], [-128, 2], [1, 256]],
                        channel_multiplier=-1)
            t_old = ()
            for g in range(2):
                for i in range(4):
                    h = 4 * g + i
                    p = slice(64 * (h % 2), 64 * (h % 2) + 64)
                    s, ps, readers = PS.take()
                    e = PE.free(t_p, *readers)
                    for sk in range(2):
                        mm = e.matmul(ps[:, sk * 256:(sk + 1) * 256], k_[p, h // 2, sk * 128:(sk + 1) * 128],
                                      q_[p, h // 2, :], start=True, stop=True)
                    t = PE.done(mm)
                    t_z = S.done(S.free(t, *t_old).activation(ZZ[:, i, :], ps, ACT.Copy, scale=0.125))
                    PS.release(s, t_z)
                yield
                S.done(S.at(*t_old).activation(nn, zz, ACT.Abs))
                S.done(S.at().activation(nn, nn, ACT.Exp, scale=-1.0))
                t_n = S.done(S.at().activation(nn, nn, ACT.Ln, bias=1.0))
                yield from steps(9 if g == 0 else 5)
                V.done(V.at(t_n, *t_old).scalar_tensor_tensor(ll, zz, 0.0, nn, ALU.min, ALU.subtract))
                t = V.done(V.at().tensor_tensor(nn, ll, zz, ALU.subtract))
                n4 = nn.rearrange("p (h b q) -> p h b q", h=4, b=2)
                l4 = ll.rearrange("p (h b q) -> p h b q", h=4, b=2)
                t_n = G.done(G.at(t).affine_select(out=n4, in_=n4, **keep))
                yield
                yield
                for i in range(4):
                    s, ps, readers = PS.take()
                    PE.free(t_n, t_m, *readers)
                    nh = NN[:, i, :]
                    group(ps[:, 0:256], [(strict, nh[:, 0:256]), (ones[:, :], nh[:, 256:512])])
                    t = group(ps[:, 256:512], [(strict, nh[:, 256:512])])
                    t = V.done(V.free(t).tensor_tensor(LL[:, i, :], LL[:, i, :], ps, ALU.add))
                    PS.release(s, t)
                    yield
                t = S.done(S.at(t).activation(ll, ll, ACT.Exp))
                t_w = G.done(G.at(t).affine_select(out=l4, in_=l4, **keep))
                yield
                yield
                for i in range(4):
                    h = 4 * g + i
                    r = slice(64 * (h % 2), 64 * (h % 2) + 64)
                    s, ps, readers = PS.take()
                    PE.free(t_w, *readers)
                    t = group(ps[r, 0:256], [(v_[:, b, h * 64:(h + 1) * 64], LL[:, i, b * 256:(b + 1) * 256])
                                             for b in range(2)])
                    PS.release(s, S.done(S.free(t).activation(AO[r, h // 2, :], ps[r, 0:256], ACT.Copy)))
                t_old = (t, t_w, V.last())
                yield
            begun[:] = yield from begin_out(A["sb_ssm_w_out_2"][0], both, S.last())

        drive()
        in_turn(state_space(), attention())
        t_x = V.last()
        wc = [load_w(A["s5_cr"]), load_w(A["s5_ci"])]
        for c in range(4):
            s, ps, readers = PS.take()
            PE.free(t_x, *readers)
            for i, xx in enumerate((XR, XI)):
                t = group(ps[:, i * 256:(i + 1) * 256],
                          [(wc[i][1][:, 4 * c + m, :], xx[:, 4 * c + m, :]) for m in range(4)], wc[i][2])
            V.done(V.at(t, t_d).scalar_tensor_tensor(yT[:, c, :], uT[:, c, :], dT[:, c:c + 1], ps[:, 0:256],
                                                     ALU.mult, ALU.add))
            t = V.done(V.at().tensor_tensor(yT[:, c, :], yT[:, c, :], ps[:, 256:512], ALU.subtract))
            PS.release(s, t)
            t_y = S.done(S.free(t).activation(yT[:, c, :], yT[:, c, :], ACT.Gelu_apprx_tanh))
        release_w(wc, PE.last())
        slab = load_slab(A["ssm_w_glu_2"][0], 0, 512, kts=4)
        cols_proj(slab, quarters, lambda k: yT[:, k, :], 256,
                  lambda c, ps, t: S.done(S.free(t, t_bg).activation(zT[:, c, :], ps, ACT.Sigmoid,
                                                                     bias=bglu[:, c:c + 1])), t_y)
        t_z = V.done(V.at(S.last(), PE.last()).tensor_tensor(H[:, 2, :], H[:, 2, :], H[:, 3, :], ALU.mult))

        out_and_norm(A["sb_ssm_w_out_2"][0], both, (A["ln_mix_g_2"][0], A["ln_mix_b_2"][0]), t_z, begun=begun)

    def norm_rows(*rows):
        return [load_bc(row) for row in rows]

    def norm_block(b, norm):
        normalize(X[:, b, :], X[:, b, :], b, 1024)
        for (s, view, t), op in zip(norm, (ALU.mult, ALU.add)):
            V.done(V.at(t).tensor_tensor(X[:, b, :], X[:, b, :], view, op))

    def begin_out(w, lhs, *tokens):
        wv = w.rearrange("(k p) n -> p k n", p=128)
        slots = [load_w(wv[:, 0:4, n * 512:(n + 1) * 512]) for n in range(2)]
        begun = [PO.take() for b in range(2)]
        for b in range(2):
            PE.free(*begun[b][2], *tokens)
            for n in range(2):
                PE.free(slots[n][2])
                for k in range(4):
                    mm = PE.eng.matmul(begun[b][1][:, n, :], lhs(k, b), slots[n][1][:, k, :], start=(k == 0),
                                       stop=False)
                t = PE.done(mm)
                yield from steps(2)
        release_w(slots, t)
        return begun

    def out_and_norm(w, lhs, rows, *tokens, begun=None):
        wv = w.rearrange("(k p) n -> p k n", p=128)
        first = 4 if begun else 0
        slabs = [[load_w(wv[:, k:k + 4, n * 512:(n + 1) * 512]) for k in range(first, 8, 4)] for n in range(2)]
        norm = norm_rows(*rows)
        for b in range(2):
            for n in range(2):
                if begun:
                    s, ps, readers = begun[b][0], begun[b][1][:, n, :], ()
                else:
                    s, ps, readers = PS.take()
                PE.free(*readers, *tokens)
                for k in range(first, 8):
                    _, wt, t = slabs[n][(k - first) // 4]
                    mm = PE.free(t).matmul(ps, lhs(k, b), wt[:, k % 4, :], start=(k == 0), stop=(k == 7))
                t = PE.done(mm)
                t2 = residual(b, n * 512, ps, t)
                if not begun:
                    PS.release(s, t2)
            if begun:
                PO.release(s, t2)
            norm_block(b, norm)
        for slab in slabs:
            release_w(slab, t)
        for row in norm:
            BC.release(row[0], V.last())

    def mlp(l):
        barrier()
        t_h = to_HT(X, range(2))
        F = BIG[:, 0:8192].rearrange("p (f t) -> p f t", f=32)
        RL = Ring([BIG[:, 8192 + 256 * i:8448 + 256 * i] for i in range(4)], [None] * 4)
        for n in range(8):
            slab = load_slab(A["mlp_w1_2"][l], n * 512, 512)

            def evac(f, ps, t):
                sr, rl, rr = RL.take()
                t = S.done(S.free(t, *rr).activation(rl, ps, ACT.Relu))
                t2 = V.done(V.free(t).tensor_tensor(F[:, f, :], rl, rl, ALU.mult))
                RL.release(sr, t2)
                return t

            cols_proj(slab, [(4 * n + j, j * 128, 128) for j in range(4)], lambda k: HT[:, k, 0:256], 256, evac, *t_h)
        t_f = V.last()
        w2 = A["mlp_w2_2"][l].rearrange("(k p) n -> p k n", p=128)
        acc = []
        for b in range(2):
            so, po, readers = PO.take()
            PE.free(*readers)
            acc.append((so, po))

        def add(b, n, k, kk, wv):
            return PE.eng.matmul(acc[b][1][:, n, :], F[:, k + kk, b * 128:(b + 1) * 128],
                             wv[:, kk, n * 512:(n + 1) * 512], start=(k + kk == 0), stop=(k + kk == 31))

        for k in range(0, 24, 2):
            ws, wv, wt = load_w(w2[:, k:k + 2, :])
            PE.free(t_f, wt)
            for kk in range(2):
                for b in range(2):
                    for n in range(2):
                        mm = add(b, n, k, kk, wv)
            WR.release(ws, PE.done(mm))
        held = [(k, *load_w(w2[:, k:k + 2, :])) for k in range(24, 32, 2)]
        norm = norm_rows(A["ln_ffn_g_2"][l], A["ln_ffn_b_2"][l])
        for b in range(2):
            for n in range(2):
                for k, ws, wv, wt in held:
                    PE.free(wt)
                    for kk in range(2):
                        mm = add(b, n, k, kk, wv)
                t = PE.done(mm)
                t2 = residual(b, n * 512, acc[b][1][:, n, :], t)
            PO.release(acc[b][0], t2)
            norm_block(b, norm)
        for k, ws, wv, wt in held:
            WR.release(ws, t)
        for row in norm:
            BC.release(row[0], V.last())

    def dsa():
        barrier()
        t_h = to_HT(X, range(2))
        q_ = BIG[:, 0:2048].rearrange("p (h t) -> p h t", h=8)
        k_ = BIG[:, 2048:3072].rearrange("p (h t) -> p h t", h=4)
        qi = BIG[:, 3072:3584].rearrange("p (h t) -> p h t", h=2)
        ki = BIG[:, 3584:3840]
        v_ = BIG[:, 3840:4352].rearrange("p (b n) -> p b n", b=2)
        wi = BIG[:, 4352:4368].rearrange("p (b n) -> p b n", b=2)
        m8 = BIG[:, 4368:4376]
        nm = BIG[:, 4376:4440]
        score = BIG[:, 4480:4992]
        nd = BIG[:, 4992:5504]
        mn = BIG[:, 5504:6016]
        OT = BIG[:, 6016:8064].rearrange("p (h t) -> p h t", h=8)
        RL = Ring([BIG[:, 8192 + 256 * i:8448 + 256 * i] for i in range(4)], [None] * 4)
        LG = Ring([BIG[:, 9216 + 512 * i:9728 + 512 * i] for i in range(4)], [None] * 4)
        PT = Ring([BIG[:, 11264 + 512 * i:11776 + 512 * i] for i in range(4)], [None] * 4)
        t_nd = G.done(G.at().iota(nd.rearrange("p (b s) -> p b s", b=2), pattern=[[-128, 2], [1, 256]], base=0,
                                  channel_multiplier=-1, allow_small_or_imprecise_dtypes=True))
        w = A["dsa_w"]
        hT = lambda k: HT[:, k, 0:256]
        rows = lambda k, b: HT[:, k, b * 128:(b + 1) * 128]
        wv = w.rearrange("(k p) n -> p k n", p=128)
        slab = load_slab(w, 1536, 512)
        last_slab = [load_w(wv[:, k:k + 4, 2048:2184]) for k in (0, 4)]
        for g in range(3):
            s, ps, readers = PS.take()
            pairs = []
            for k in range(8):
                ws = slab if g < 2 else last_slab
                c0 = 256 + g * 128 if g < 2 else 0
                pairs.append((ws[k // 4][1][:, k % 4, c0:c0 + 128], hT(k), ws[k // 4][2]))
            t = group(ps[:, 0:256], pairs, *readers, *t_h)
            PS.release(s, copy_out(qi[:, g, :] if g < 2 else ki, ps[:, 0:256], t))
        for b in range(2):
            s, ps, readers = PS.take()
            t = group(ps[:, 0:8], [(rows(k, b), last_slab[k // 4][1][:, k % 4, 128:136]) for k in range(8)], *readers)
            PS.release(s, copy_out(wi[:, b, :], ps[:, 0:8], t))
            s, ps, readers = PS.take()
            t = group(ps[:, 0:256], [(rows(k, b), slab[k // 4][1][:, k % 4, 0:256]) for k in range(8)], *readers)
            PS.release(s, copy_out(v_[:, b, :], ps[:, 0:256], t))
        release_w(slab + last_slab, PE.last())
        t_i = (V.last(), S.last())

        def select():
            for h in range(8):
                for b in range(2):
                    sc = score[:, b * 256:(b + 1) * 256]
                    p = slice(32 * (h % 4), 32 * (h % 4) + 32)
                    s, ps, readers = PS.take()
                    t = group(ps[:, 0:256], [(qi[p, h // 4, b * 128:(b + 1) * 128], ki[p, :])], *t_i, *readers)
                    sr, rl, rr = RL.take()
                    t = S.done(S.free(t, *rr).activation(rl, ps[:, 0:256], ACT.Relu))
                    PS.release(s, t)
                    if h == 0:
                        t = V.done(V.at(t, *t_i).tensor_scalar(sc, rl, wi[:, b, h:h + 1], None, ALU.mult))
                    else:
                        t = V.done(V.at(t).scalar_tensor_tensor(sc, rl, wi[:, b, h:h + 1], sc, ALU.mult, ALU.add))
                    RL.release(sr, t)
                yield
            t = V.done(V.at().tensor_scalar(score, score, (32.0 ** -0.5) * (8.0 ** -0.5), None, ALU.mult))
            s3 = score.rearrange("p (b s) -> p b s", b=2)
            t = G.done(G.at(t).affine_select(out=s3, in_=s3, compare_op=ALU.is_ge, fill=-1.0e38, base=0,
                                             pattern=[[128, 2], [-1, 256]], channel_multiplier=1))
            V.free(t)
            yield
            for b in range(2):
                sc = score[:, b * 256:(b + 1) * 256]
                for r in range(8):
                    V.done(V.at().max(m8, sc))
                    V.done(V.at().match_replace(sc, m8, sc, NEG))
                    yield
            t = V.done(V.at().tensor_scalar(mn, score, -2.0e38, -1.0e30, ALU.is_gt, ALU.mult))
            m3 = mn.rearrange("p (b s) -> p b s", b=2)
            t = G.done(G.at(t).affine_select(out=m3, in_=m3, compare_op=ALU.is_ge, fill=-1.0e30, base=0,
                                             pattern=[[128, 2], [-1, 256]], channel_multiplier=1))
            V.free(t, t_nd)
            yield

        def evac(dst, ps, t):
            return S.done(S.free(t).activation(dst, ps, ACT.Copy))

        def projections():
            slab = load_slab(w, 1024, 512)
            for h in range(4):
                s, ps, readers = PS.take()
                t = group(ps[:, 0:256], [(slab[k // 4][1][:, k % 4, h * 128:(h + 1) * 128], hT(k), slab[k // 4][2])
                                         for k in range(8)], *readers)
                PS.release(s, evac(k_[:, h, :], ps[:, 0:256], t))
                yield
            release_w(slab, PE.last())
            for n in range(2):
                slab = load_slab(w, n * 512, 512)
                for i in range(4):
                    s, ps, readers = PS.take()
                    t = group(ps[:, 0:256], [(slab[k // 4][1][:, k % 4, i * 128:(i + 1) * 128], hT(k),
                                              slab[k // 4][2]) for k in range(8)], *readers)
                    PS.release(s, evac(q_[:, 4 * n + i, :], ps[:, 0:256], t))
                    yield
                release_w(slab, PE.last())

        in_turn(select(), projections())
        t_p = (V.last(), S.last())
        PQ = Ring([view[:, n, :] for view in PO.views for n in range(2)], [None] * 4)
        lgs, pts = {}, {}

        products = {}

        def multiply(h):
            p = slice(64 * (h % 2), 64 * (h % 2) + 64)
            s, ps, readers = PS.take()
            PE.free(*t_p, *readers)
            for b in range(2):
                t = group(ps[:, b * 256:(b + 1) * 256], [(q_[p, h // 2, b * 128:(b + 1) * 128], k_[p, h // 4, :])])
            products[h] = (s, ps, t)

        def scores(h):
            s, ps, t = products[h]
            sl, lg, lr_ = LG.take()
            V.done(V.at(*lr_).scalar_tensor_tensor(lg, nd, 2.0 ** (-8.0 * (h + 1) / 16), mn, ALU.mult, ALU.add))
            t = V.done(V.at(t).scalar_tensor_tensor(lg, ps, 0.125, lg, ALU.mult, ALU.add))
            PS.release(s, t)
            lg3 = lg.rearrange("p (b s) -> p b s", b=2)
            t = V.done(V.at().tensor_reduce(nm[:, 2 * h:2 * h + 2], lg3, AX, ALU.max, negate=True))
            for b in range(2):
                t = S.done(S.free(t).activation(lg3[:, b, :], lg3[:, b, :], ACT.Exp,
                                                bias=nm[:, 2 * h + b:2 * h + b + 1],
                                                accum_out=nm[:, 32 + 2 * h + b:33 + 2 * h + b]))
            lgs[h] = (sl, lg, lg3, t)

        def spread(h):
            sl, lg, lg3, t = lgs[h]
            z = nm[:, 32 + 2 * h:34 + 2 * h]
            V.done(V.at(t).reciprocal(z, z))
            for b in range(2):
                t = V.done(V.at().tensor_scalar(lg3[:, b, :], lg3[:, b, :], z[:, b:b + 1], None, ALU.mult))
            s, ps, readers = PQ.take()
            e = PE.free(t, *readers)
            for b in range(2):
                for sk in range(2):
                    mm = e.transpose(ps[:, sk * 256 + b * 128:sk * 256 + b * 128 + 128],
                                     lg[:, b * 256 + sk * 128:b * 256 + sk * 128 + 128], ident[:, :])
            t = PE.done(mm)
            LG.release(sl, t)
            sp_, pt, pr_ = PT.take()
            t = S.done(S.free(t, *pr_).activation(pt, ps, ACT.Copy))
            PQ.release(s, t)
            pts[h] = (sp_, pt, t)

        def outputs(h):
            sp_, pt, t = pts[h]
            kv = h // 4
            r = slice(64 * (h % 2), 64 * (h % 2) + 64)
            s, ps, readers = PQ.take()
            t = group(ps[r, 0:256], [(v_[:, sk, kv * 64:(kv + 1) * 64], pt[:, sk * 256:(sk + 1) * 256])
                                     for sk in range(2)], t, *readers)
            PT.release(sp_, t)
            PQ.release(s, S.done(S.free(t).activation(OT[r, h // 2, :], ps[r, 0:256], ACT.Copy)))

        multiply(0)
        for h in range(16 + 3):
            if h + 1 < 16:
                multiply(h + 1)
            if h < 16:
                scores(h)
            if 2 <= h < 18:
                spread(h - 2)
            if 3 <= h:
                outputs(h - 3)
        t_o = S.last()
        wo = A["dsa_w_out_2"][0]
        out_and_norm(wo, lambda k, b: OT[:, k, b * 128:(b + 1) * 128], (A["ln_mix_g_2"][1], A["ln_mix_b_2"][1]), t_o)

    V.free(*t_x)
    PE.free(*t_x)
    t_silu = ()
    if "mod0" in parts or "mod1" in parts:
        t = S.done(S.at(t_sc).activation(scS[:, :, :], scT[:, :, :], ACT.Sigmoid))
        t_silu = (V.done(V.at(t).tensor_tensor(scS[:, :, :], scS[:, :, :], scT[:, :, :], ALU.mult)),)
    if "mod0" in parts:
        for _ in modulation(0, 0, 4):
            pass
    if "mix0" in parts:
        of = lambda a: (lambda b: BIG[:, a + (b - 2) * 1024:a + (b - 1) * 1024])
        for _ in chunk_mlp([2], of(0), of(2048), 0):
            pass

        def late_mixing():
            yield from modulation(0, 10, 2)
            yield from chunk_mlp([3, 0, 1], lambda b: H[:, b, :],
                                 lambda b: BIG[:, 12288 + b * 1024:13312 + b * 1024], 3)

        late = late_mixing()
    if "peer0" in parts:
        more = []
        if "mod1" in parts:
            more += [(set(), modulation(1, 0, 4)), (set(), modulation(1, 4, 8))]
        if "mix1" in parts:
            more.append(({2, 3}, gla_ctx()))
        peer(0, [2, 3, 0, 1], more, late, (8, 8, 6, 0))
    elif "mod1" in parts:
        for g in (modulation(1, 0, 4), modulation(1, 4, 8), gla_ctx()):
            for _ in g:
                pass
    if "mix1" in parts:
        rest_of_gla = gla()
        next(rest_of_gla)
    if "peer1" in parts:
        peer(1, [0, 1], late=rest_of_gla, by_vector=(6, 0))
    if "sb" in parts:
        sb_ssm()
    if "mlp0" in parts:
        mlp(0)
    if "dsa" in parts:
        dsa()
    if "mlp1" in parts:
        mlp(1)
    s_out = sem("s_out")
    D.free(V.last()).dma_start(out[0].rearrange("(b p) d -> p b d", p=128), X[:, 0:2, :]).then_inc(s_out, 16)
    nc.sync.wait_ge(s_out, 16)
    for i in range(2):
        if ms_count[i]:
            nc.sync.wait_ge(s_ms[i], ms_count[i])
    ctx.close()


_OUTS = [((1, 256, 1024), 'float32')]


def layout(inputs):
    import numpy as np

    def c(a):
        return np.ascontiguousarray(a)

    a = {k: np.asarray(v) for k, v in inputs.items()}
    o = {}
    for k in ("x", "ctx", "w_mod", "b_mod", "ln_g", "ln_b", "a_w_in", "a_norm_g", "a_norm_b", "a_w_out", "b_w_in",
              "b_gn_g", "b_w_out", "p_w_q", "sb_ssm_w_in_2", "ssm_w_glu_2",
              "sb_ssm_w_out_2", "dsa_w_out_2", "ln_mix_g_2", "ln_mix_b_2", "ln_ffn_g_2", "ln_ffn_b_2",
              "mlp_w1_2", "mlp_w2_2"):
        o[k] = c(a[k])
    o["p_u"] = c(a["p_u"].reshape(32768, 1024))
    o["p_v"] = c(a["p_v"].reshape(32768, 1024))
    w = a["dsa_w_in_2"][0]
    k = np.repeat(w[:, 1024:1280].reshape(1024, 4, 1, 64), 2, axis=2).reshape(1024, 512)
    ki = np.repeat(w[:, 1792:1824].reshape(1024, 1, 32), 4, axis=1).reshape(1024, 128)
    o["dsa_w"] = c(np.concatenate([w[:, 0:1024], k, w[:, 1280:1792], ki, w[:, 1824:1832]], axis=1))
    w = np.zeros((33, 2, 512), np.float32)
    w[0:16, 0] = a["b_w_gate"][0, 0]
    w[16:32, 1] = a["b_w_gate"][0, 1]
    w[32] = a["b_gate_bias"][0]
    o["wgate"] = w
    cc = np.stack([a["c"][0], a["c_ctx"]])
    o["cT"] = c(cc.reshape(2, 8, 128).transpose(2, 1, 0))
    o["a_b_sT"] = c(a["a_b_s"][0].T)
    o["a_w_sT"] = c(a["a_w_s"][0].transpose(2, 0, 1))
    o["keysT"] = c(a["p_keys"].transpose(0, 1, 3, 2))
    o["ldt"] = c(np.repeat(a["ssm_log_dt_2"][0], 64).reshape(16, 128).T)
    o["lre"] = c(a["ssm_lam_re_2"][0].reshape(16, 128).T)
    o["lim"] = c(a["ssm_lam_im_2"][0].reshape(16, 128).T)
    o["s5dT"] = c(a["ssm_d_2"][0].reshape(4, 128).T)
    o["bgluT"] = c(a["ssm_b_glu_2"][0].reshape(4, 128).T)
    for name, key in (("s5_br", "ssm_b_re_2"), ("s5_bi", "ssm_b_im_2")):
        w = np.zeros((128, 16, 128), np.float32)
        for g in range(32):
            w[(g % 8) * 16:(g % 8) * 16 + 16, g // 2, (g % 2) * 64:(g % 2) * 64 + 64] = a[key][0, g].T
        o[name] = w
    for name, key in (("s5_cr", "ssm_c_re_2"), ("s5_ci", "ssm_c_im_2")):
        w = np.zeros((128, 16, 128), np.float32)
        for g in range(32):
            w[(g % 2) * 64:(g % 2) * 64 + 64, g // 2, (g % 8) * 16:(g % 8) * 16 + 16] = a[key][0, g].T
        o[name] = w
    return o


def kernel(**inputs):
    import numpy as _np
    import concourse.bacc as _bacc
    from concourse import mybir as _mybir
    from concourse.bass_utils import run_bass_kernel_spmd as _run

    nc = _bacc.Bacc("TRN2", target_bir_lowering=False, num_devices=1)
    arrays, args = {}, {}
    for name, a in layout(inputs).items():
        arrays[f"in_{name}_dram"] = a
        args[name] = nc.dram_tensor(f"in_{name}_dram", a.shape, _mybir.dt.from_np(a.dtype), kind="ExternalInput").ap()
    shape, dtype = _OUTS[0]
    out = nc.dram_tensor("out_0_dram", shape, _mybir.dt.from_np(_np.dtype(dtype)), kind="ExternalOutput").ap()
    program(nc, args, out)
    r = _run(nc, [arrays], core_ids=[0])
    return r.results[0]["out_0_dram"]
```
